# Optimizing a Trainium2 kernel written in Bass

```python
import math
import jax, jax.numpy as jnp
from jax import lax
import numpy as np

D_MODEL = 1024
BATCH = 1
SEQ = 512
DEPTH = 1

N_MEM = 256
HEAD_DIM = 64
A_HEADS = 8
A_WIDTH = A_HEADS * HEAD_DIM
IDX_HEADS = 4
IDX_DIM = 64
TOPK_MAX = 256
B_HEADS = 4
B_VDIM = 2 * HEAD_DIM
B_WIDTH = B_HEADS * B_VDIM
MIX_WIDTH = A_WIDTH + B_WIDTH
IN_SIZES = (A_WIDTH, HEAD_DIM, HEAD_DIM, IDX_HEADS * IDX_DIM, IDX_DIM, IDX_HEADS,
            2 * B_HEADS * HEAD_DIM, 2 * B_HEADS * HEAD_DIM, B_WIDTH)
IN_COLS = sum(IN_SIZES)
X_HEADS = 4
X_HEAD_DIM = D_MODEL // X_HEADS
D_FF = 2816
CONV_W = 3
ROPE_THETA = 10000.0
EPS = 1e-6
Q_BLOCK = 128


def rms_normalize(x):
    xf = x.astype(jnp.float32)
    y = xf * lax.rsqrt(jnp.mean(xf * xf, axis=-1, keepdims=True) + EPS)
    return y.astype(x.dtype)

def rmsnorm(x, g):
    xf = x.astype(jnp.float32)
    y = xf * lax.rsqrt(jnp.mean(xf * xf, axis=-1, keepdims=True) + EPS)
    return (y * g.astype(jnp.float32)).astype(x.dtype)

def rope_tables(positions, dim):
    inv_freq = 1.0 / (ROPE_THETA ** (jnp.arange(0, dim, 2, dtype=jnp.float32) / dim))
    ang = positions.astype(jnp.float32)[..., None] * inv_freq
    return jnp.cos(ang), jnp.sin(ang)

def rope(x, cos, sin):
    shape = cos.shape[:2] + (1,) * (x.ndim - 3) + cos.shape[-1:]
    c = cos.reshape(shape).astype(x.dtype)
    s = sin.reshape(shape).astype(x.dtype)
    x1, x2 = jnp.split(x, 2, axis=-1)
    return jnp.concatenate([x1 * c - x2 * s, x2 * c + x1 * s], axis=-1)

def to_blocks(t, n_blk):
    return t.reshape((t.shape[0], n_blk, Q_BLOCK) + t.shape[2:]).swapaxes(0, 1)

def from_blocks(t):
    t = t.swapaxes(0, 1)
    return t.reshape((t.shape[0], t.shape[1] * t.shape[2]) + t.shape[3:])

def dsa_attention(q, k, v, q_idx, k_idx, w_idx):
    B, S, H, D = q.shape
    n_blk = S // Q_BLOCK
    topk = min(TOPK_MAX, S // 4)
    key_pos = jnp.arange(S)

    def block(args):
        qb, qib, wib, start = args
        qpos = start + jnp.arange(Q_BLOCK)
        causal = key_pos[None, :] <= qpos[:, None]
        logits = jnp.einsum('bqhd,bsd->bqhs', qib, k_idx)
        score = jnp.einsum('bqh,bqhs->bqs', wib, jax.nn.relu(logits)).astype(jnp.float32)
        score = jnp.where(causal[None], score, -jnp.inf)
        _, idx = lax.top_k(score, topk)
        k_sel = jax.vmap(lambda kk, ii: kk[ii])(k, idx)
        v_sel = jax.vmap(lambda vv, ii: vv[ii])(v, idx)
        valid = idx <= qpos[None, :, None]
        s = jnp.einsum('bqhd,bqkd->bqhk', qb, k_sel).astype(jnp.float32) * (D ** -0.5)
        s = jnp.where(valid[:, :, None, :], s, -jnp.inf)
        p = jax.nn.softmax(s, axis=-1).astype(v.dtype)
        return jnp.einsum('bqhk,bqkd->bqhd', p, v_sel)

    starts = jnp.arange(n_blk) * Q_BLOCK
    out = lax.map(block, (to_blocks(q, n_blk), to_blocks(q_idx, n_blk), to_blocks(w_idx, n_blk), starts))
    return from_blocks(out)

def diff_attention(q, k, v, lam):
    B, S, H, _, D = q.shape
    n_blk = S // Q_BLOCK
    key_pos = jnp.arange(S)

    def block(args):
        qb, start = args
        qpos = start + jnp.arange(Q_BLOCK)
        causal = key_pos[None, :] <= qpos[:, None]
        s = jnp.einsum('bqhcd,bshcd->bhcqs', qb, k).astype(jnp.float32) * (D ** -0.5)
        s = jnp.where(causal, s, -jnp.inf)
        p = jax.nn.softmax(s, axis=-1)
        a = (p[:, :, 0] - lam * p[:, :, 1]).astype(v.dtype)
        return jnp.einsum('bhqs,bshe->bqhe', a, v)

    starts = jnp.arange(n_blk) * Q_BLOCK
    out = lax.map(block, (to_blocks(q, n_blk), starts))
    return from_blocks(out)

def token_mixer(hn, cos, sin, w_in, g_qa, g_ka, g_qb, g_kb,
                lam_q1, lam_k1, lam_q2, lam_k2, w_out, lambda_init):
    B, S, _ = hn.shape
    proj = hn @ w_in
    offsets = np.cumsum(IN_SIZES)[:-1].tolist()
    q_a, k_a, v_a, q_i, k_i, w_i, q_b, k_b, v_b = jnp.split(proj, offsets, axis=-1)

    q_a = rope(rmsnorm(q_a.reshape(B, S, A_HEADS, HEAD_DIM), g_qa), cos, sin)
    k_a = rope(rmsnorm(k_a, g_ka), cos, sin)
    q_i = rope(q_i.reshape(B, S, IDX_HEADS, IDX_DIM), cos, sin)
    k_i = rope(k_i, cos, sin)
    w_i = w_i * (IDX_HEADS ** -0.5 * IDX_DIM ** -0.5)
    out_a = dsa_attention(q_a, k_a, v_a, q_i, k_i, w_i).reshape(B, S, A_WIDTH)

    q_b = rope(rmsnorm(q_b.reshape(B, S, B_HEADS, 2, HEAD_DIM), g_qb), cos, sin)
    k_b = rope(rmsnorm(k_b.reshape(B, S, B_HEADS, 2, HEAD_DIM), g_kb), cos, sin)
    v_b = v_b.reshape(B, S, B_HEADS, B_VDIM)
    f32 = jnp.float32
    lam = (jnp.exp(jnp.sum(lam_q1.astype(f32) * lam_k1.astype(f32)))
           - jnp.exp(jnp.sum(lam_q2.astype(f32) * lam_k2.astype(f32))) + lambda_init)
    out_b = diff_attention(q_b, k_b, v_b, lam)
    out_b = (rms_normalize(out_b) * (1.0 - lambda_init)).reshape(B, S, B_WIDTH)

    return jnp.concatenate([out_a, out_b], axis=-1) @ w_out

def cross_attention(hn, memn, w_xq, w_xk, w_xv, w_xo, g_xq, g_xk):
    B, S, _ = hn.shape
    M = memn.shape[1]
    q = rmsnorm((hn @ w_xq).reshape(B, S, X_HEADS, X_HEAD_DIM), g_xq)
    k = rmsnorm((memn @ w_xk).reshape(B, M, X_HEADS, X_HEAD_DIM), g_xk)
    v = (memn @ w_xv).reshape(B, M, X_HEADS, X_HEAD_DIM)
    s = jnp.einsum('bshd,bmhd->bhsm', q, k).astype(jnp.float32) * (X_HEAD_DIM ** -0.5)
    p = jax.nn.softmax(s, axis=-1).astype(v.dtype)
    o = jnp.einsum('bhsm,bmhd->bshd', p, v).reshape(B, S, D_MODEL)
    return o @ w_xo

def conv_glu(hn, w_ffn_in, conv_w, conv_b, w_ffn_out):
    S = hn.shape[1]
    a, gate = jnp.split(hn @ w_ffn_in, 2, axis=-1)
    a_pad = jnp.pad(a, ((0, 0), (CONV_W - 1, 0), (0, 0)))
    conv = conv_b + sum(a_pad[:, j:j + S] * conv_w[j] for j in range(CONV_W))
    return (jax.nn.gelu(conv) * gate) @ w_ffn_out

def first_inputs(seed: int = 0) -> dict:
    key = jax.random.key(seed)
    ks = iter(jax.random.split(key, 48))
    f32 = jnp.float32

    def nrm(shape, fan_in):
        return jax.random.normal(next(ks), shape, f32) * (fan_in ** -0.5)

    def gain(shape):
        return 1.0 + 0.02 * jax.random.normal(next(ks), shape, f32)

    x = jax.random.normal(next(ks), (BATCH, SEQ, D_MODEL), f32)
    mem = jax.random.normal(next(ks), (BATCH, N_MEM, D_MODEL), f32)
    offs = jax.random.randint(next(ks), (BATCH, 1), 0, 1024)
    positions = (offs + jnp.arange(SEQ, dtype=jnp.int32)[None, :]).astype(jnp.int32)
    L = DEPTH
    return {
        "x": x,
        "mem": mem,
        "positions": positions,
        "g_mix": gain((L, D_MODEL)),
        "w_in": nrm((L, D_MODEL, IN_COLS), D_MODEL),
        "g_qa": gain((L, HEAD_DIM)),
        "g_ka": gain((L, HEAD_DIM)),
        "g_qb": gain((L, HEAD_DIM)),
        "g_kb": gain((L, HEAD_DIM)),
        "lam_q1": 0.1 * jax.random.normal(next(ks), (L, HEAD_DIM), f32),
        "lam_k1": 0.1 * jax.random.normal(next(ks), (L, HEAD_DIM), f32),
        "lam_q2": 0.1 * jax.random.normal(next(ks), (L, HEAD_DIM), f32),
        "lam_k2": 0.1 * jax.random.normal(next(ks), (L, HEAD_DIM), f32),
        "w_out": nrm((L, MIX_WIDTH, D_MODEL), MIX_WIDTH),
        "g_xattn": gain((L, D_MODEL)),
        "g_mem": gain((L, D_MODEL)),
        "w_xq": nrm((L, D_MODEL, D_MODEL), D_MODEL),
        "w_xk": nrm((L, D_MODEL, D_MODEL), D_MODEL),
        "w_xv": nrm((L, D_MODEL, D_MODEL), D_MODEL),
        "w_xo": nrm((L, D_MODEL, D_MODEL), D_MODEL),
        "g_xq": gain((L, X_HEAD_DIM)),
        "g_xk": gain((L, X_HEAD_DIM)),
        "g_ffn": gain((L, D_MODEL)),
        "w_ffn_in": nrm((L, D_MODEL, 2 * D_FF), D_MODEL),
        "conv_w": nrm((L, CONV_W, D_FF), CONV_W),
        "conv_b": 0.02 * jax.random.normal(next(ks), (L, D_FF), f32),
        "w_ffn_out": nrm((L, D_FF, D_MODEL), D_FF),
    }

def first_block(x, mem, positions, g_mix, w_in, g_qa, g_ka, g_qb, g_kb,
              lam_q1, lam_k1, lam_q2, lam_k2, w_out, g_xattn, g_mem,
              w_xq, w_xk, w_xv, w_xo, g_xq, g_xk, g_ffn, w_ffn_in,
              conv_w, conv_b, w_ffn_out):
    cos, sin = rope_tables(positions, HEAD_DIM)
    h = x
    for l in range(DEPTH):
        lambda_init = 0.8 - 0.6 * math.exp(-0.3 * l)
        h = h + token_mixer(rmsnorm(h, g_mix[l]), cos, sin, w_in[l], g_qa[l], g_ka[l],
                            g_qb[l], g_kb[l], lam_q1[l], lam_k1[l], lam_q2[l], lam_k2[l],
                            w_out[l], lambda_init)
        h = h + cross_attention(rmsnorm(h, g_xattn[l]), rmsnorm(mem, g_mem[l]),
                                w_xq[l], w_xk[l], w_xv[l], w_xo[l], g_xq[l], g_xk[l])
        h = h + conv_glu(rmsnorm(h, g_ffn[l]), w_ffn_in[l], conv_w[l], conv_b[l], w_ffn_out[l])
    return h


HG_HEADS = 8
HG_DIM = 128
HG_WIDTH = HG_HEADS * HG_DIM
HG_CHUNK = 32
MLA_HEADS = 8
QK_NOPE = 128
QK_ROPE = 64
QK_DIM = QK_NOPE + QK_ROPE
V_DIM = 128
Q_LORA = 3 * D_MODEL // 8
KV_LORA = D_MODEL // 4
MLA_WIDTH = MLA_HEADS * V_DIM
N_BRANCH = 2
IN_SPLITS = (HG_WIDTH, HG_WIDTH, HG_WIDTH, HG_WIDTH,
             Q_LORA, KV_LORA, QK_ROPE, MLA_WIDTH,
             N_BRANCH * D_MODEL)
IN_COLS_2 = sum(IN_SPLITS)


def _split_points():
    pts, acc = [], 0
    for w in IN_SPLITS[:-1]:
        acc += w
        pts.append(acc)
    return pts

def rms_norm(x, g):
    xf = x.astype(jnp.float32)
    y = xf * lax.rsqrt(jnp.mean(xf * xf, axis=-1, keepdims=True) + EPS)
    return (y * g.astype(jnp.float32)).astype(x.dtype)

def forget_lower_bounds(lb_logits):
    return jnp.cumsum(jax.nn.softmax(lb_logits.astype(jnp.float32), axis=0), axis=0)[:DEPTH]

def rope_tables_2(seq):
    inv = ROPE_THETA ** (-jnp.arange(0, QK_ROPE, 2, dtype=jnp.float32) / QK_ROPE)
    ang = jnp.arange(seq, dtype=jnp.float32)[:, None] * inv[None, :]
    return jnp.cos(ang), jnp.sin(ang)

def apply_rope(x, cos, sin):
    xf = x.astype(jnp.float32)
    x1, x2 = xf[..., : QK_ROPE // 2], xf[..., QK_ROPE // 2:]
    out = jnp.concatenate([x1 * cos - x2 * sin, x2 * cos + x1 * sin], axis=-1)
    return out.astype(x.dtype)

def hgrn2_recurrence(q, k, v, log_f):
    B, S, H, dk = q.shape
    dv = v.shape[-1]
    C = HG_CHUNK
    N = S // C

    def to_chunks(t):
        return t.reshape(B, N, C, H, t.shape[-1]).transpose(1, 0, 3, 2, 4)

    q, k, v, log_f = to_chunks(q), to_chunks(k), to_chunks(v), to_chunks(log_f)
    b = jnp.cumsum(log_f, axis=3)
    b_last = b[:, :, :, -1:, :]
    q_in = q * jnp.exp(b)
    k_in = k * jnp.exp(-b)
    k_out = k * jnp.exp(b_last - b)
    chunk_decay = jnp.exp(b_last[:, :, :, 0, :])

    causal = jnp.tril(jnp.ones((C, C), dtype=bool))
    scores = jnp.einsum('nbhtk,nbhsk->nbhts', q_in, k_in)
    scores = jnp.where(causal, scores, 0.0)
    o_intra = jnp.einsum('nbhts,nbhsv->nbhtv', scores, v)

    def step(state, inp):
        q_n, k_n, v_n, dec_n = inp
        o_inter = jnp.einsum('bhtk,bhkv->bhtv', q_n, state)
        state = state * dec_n[..., None] + jnp.einsum('bhsk,bhsv->bhkv', k_n, v_n)
        return state, o_inter

    state0 = jnp.zeros((B, H, dk, dv), jnp.float32)
    _, o_inter = lax.scan(step, state0, (q_in, k_out, v, chunk_decay))
    o = o_intra + o_inter
    return o.transpose(1, 0, 3, 2, 4).reshape(B, S, H, dv)

def hgrn2_branch(hq, hf, hi, hz, lb, hg_norm_g):
    B, S, _ = hq.shape
    dt = hq.dtype
    f = lb + (1.0 - lb) * jax.nn.sigmoid(hf.astype(jnp.float32))
    q = jax.nn.silu(hq.astype(jnp.float32)).reshape(B, S, HG_HEADS, HG_DIM)
    k = (1.0 - f).reshape(B, S, HG_HEADS, HG_DIM)
    v = hi.astype(jnp.float32).reshape(B, S, HG_HEADS, HG_DIM)
    log_f = jnp.log(f).reshape(B, S, HG_HEADS, HG_DIM)
    o = hgrn2_recurrence(q, k, v, log_f).astype(dt)
    o = rms_norm(o, hg_norm_g)
    o = o * jax.nn.silu(hz).reshape(B, S, HG_HEADS, HG_DIM)
    return o.reshape(B, S, HG_WIDTH)

def mla_branch(cq, ckv, kr, mz, q_a_g, w_uq, kv_a_g, w_ukv):
    B, S, _ = cq.shape
    cos, sin = rope_tables_2(S)
    q = (rms_norm(cq, q_a_g) @ w_uq).reshape(B, S, MLA_HEADS, QK_DIM)
    q_nope = q[..., :QK_NOPE]
    q_pe = apply_rope(q[..., QK_NOPE:], cos[:, None, :], sin[:, None, :])
    kv = (rms_norm(ckv, kv_a_g) @ w_ukv).reshape(B, S, MLA_HEADS, QK_NOPE + V_DIM)
    k_nope, v = kv[..., :QK_NOPE], kv[..., QK_NOPE:]
    k_pe = apply_rope(kr, cos, sin)
    scale = QK_DIM ** -0.5
    key_pos = jnp.arange(S)

    def attend_block(blk):
        start = blk * Q_BLOCK
        qn = lax.dynamic_slice_in_dim(q_nope, start, Q_BLOCK, axis=1)
        qp = lax.dynamic_slice_in_dim(q_pe, start, Q_BLOCK, axis=1)
        s = (jnp.einsum('bqhd,bkhd->bhqk', qn, k_nope)
             + jnp.einsum('bqhr,bkr->bhqk', qp, k_pe)).astype(jnp.float32) * scale
        q_pos = start + jnp.arange(Q_BLOCK)
        s = jnp.where(q_pos[:, None] >= key_pos[None, :], s, -jnp.inf)
        p = jax.nn.softmax(s, axis=-1).astype(v.dtype)
        return jnp.einsum('bhqk,bkhd->bqhd', p, v)

    out = lax.map(attend_block, jnp.arange(S // Q_BLOCK))
    out = out.transpose(1, 0, 2, 3, 4).reshape(B, S, MLA_WIDTH)
    return out * jax.nn.silu(mz)

def second_inputs(seed: int = 0) -> dict:
    key = jax.random.key(seed)
    ks = jax.random.split(key, 16)
    f32 = jnp.float32

    def w(k, shape, fan_in):
        return jax.random.normal(k, shape, f32) * fan_in ** -0.5

    def gain(k, shape):
        return 1.0 + 0.02 * jax.random.normal(k, shape, f32)

    return {
        "x": jax.random.normal(ks[0], (BATCH, SEQ, D_MODEL), f32),
        "norm_g": gain(ks[1], (DEPTH, D_MODEL)),
        "w_in": w(ks[2], (DEPTH, D_MODEL, IN_COLS_2), D_MODEL),
        "b_gate": 0.02 * jax.random.normal(ks[3], (DEPTH, N_BRANCH * D_MODEL), f32),
        "lb_logits": 0.1 * jax.random.normal(ks[4], (DEPTH + 1, HG_WIDTH), f32),
        "hg_norm_g": gain(ks[5], (DEPTH, HG_DIM)),
        "q_a_g": gain(ks[6], (DEPTH, Q_LORA)),
        "w_uq": w(ks[7], (DEPTH, Q_LORA, MLA_HEADS * QK_DIM), Q_LORA),
        "kv_a_g": gain(ks[8], (DEPTH, KV_LORA)),
        "w_ukv": w(ks[9], (DEPTH, KV_LORA, MLA_HEADS * (QK_NOPE + V_DIM)), KV_LORA),
        "w_proj_a": w(ks[10], (DEPTH, HG_WIDTH, D_MODEL), HG_WIDTH),
        "w_proj_b": w(ks[11], (DEPTH, MLA_WIDTH, D_MODEL), MLA_WIDTH),
        "w_out": w(ks[12], (DEPTH, D_MODEL, D_MODEL), D_MODEL),
        "final_norm_g": gain(ks[13], (D_MODEL,)),
    }

def second_block(x, norm_g, w_in, b_gate, lb_logits, hg_norm_g, q_a_g, w_uq, kv_a_g, w_ukv,
              w_proj_a, w_proj_b, w_out, final_norm_g):
    B, S, _ = x.shape
    lower_bounds = forget_lower_bounds(lb_logits)
    pts = _split_points()
    for l in range(DEPTH):
        h = rms_norm(x, norm_g[l])
        proj = h @ w_in[l]
        hq, hf, hi, hz, cq, ckv, kr, mz, glog = jnp.split(proj, pts, axis=-1)
        y_a = hgrn2_branch(hq, hf, hi, hz, lower_bounds[l], hg_norm_g[l])
        y_b = mla_branch(cq, ckv, kr, mz, q_a_g[l], w_uq[l], kv_a_g[l], w_ukv[l])
        gates = jax.nn.sigmoid((glog + b_gate[l]).astype(jnp.float32)).astype(x.dtype)
        gates = gates.reshape(B, S, N_BRANCH, D_MODEL)
        merged = gates[:, :, 0] * (y_a @ w_proj_a[l]) + gates[:, :, 1] * (y_b @ w_proj_b[l])
        x = x + merged @ w_out[l]
    return rms_norm(x, final_norm_g)


def setup_inputs(seed=0):
    out = dict(first_inputs(seed))
    for name, value in second_inputs(seed + 1).items():
        if name != "x":
            out[name + "_2"] = value
    return out


def reference(
    x, mem, positions, g_mix, w_in, g_qa, g_ka, g_qb, g_kb, lam_q1, lam_k1, lam_q2, lam_k2,
    w_out, g_xattn, g_mem, w_xq, w_xk, w_xv, w_xo, g_xq, g_xk, g_ffn, w_ffn_in, conv_w, conv_b,
    w_ffn_out, norm_g_2, w_in_2, b_gate_2, lb_logits_2, hg_norm_g_2, q_a_g_2, w_uq_2, kv_a_g_2,
    w_ukv_2, w_proj_a_2, w_proj_b_2, w_out_2, final_norm_g_2,
):
    x = first_block(
        x, mem, positions, g_mix, w_in, g_qa, g_ka, g_qb, g_kb, lam_q1, lam_k1, lam_q2, lam_k2,
        w_out, g_xattn, g_mem, w_xq, w_xk, w_xv, w_xo, g_xq, g_xk, g_ffn, w_ffn_in, conv_w,
        conv_b, w_ffn_out,
    )
    return second_block(
        x, norm_g_2, w_in_2, b_gate_2, lb_logits_2, hg_norm_g_2, q_a_g_2, w_uq_2, kv_a_g_2,
        w_ukv_2, w_proj_a_2, w_proj_b_2, w_out_2, final_norm_g_2,
    )


_drawn_inputs = setup_inputs


def setup_inputs(seed=0):
    import zlib

    import numpy as np

    out = dict(_drawn_inputs(seed))
    spreads = {}
    factors = {'g_qa': 8.0,
     'g_ka': 8.0,
     'g_qb': 4.534,
     'g_kb': 4.815,
     'lam_q1': 6.18,
     'lam_k1': 8.0,
     'g_xattn': 8.0,
     'g_mem': 8.0,
     'g_xq': 8.0,
     'g_xk': 8.0,
     'g_ffn': 3.823,
     'conv_b': 5.629,
     'norm_g_2': 7.658,
     'b_gate_2': 8.0,
     'lb_logits_2': 8.0,
     'hg_norm_g_2': 29.887,
     'q_a_g_2': 8.0,
     'kv_a_g_2': 8.0,
     'final_norm_g_2': 7.716,
     'lam_k2': 2.925}
    for name, (base, spread) in spreads.items():
        noise = np.random.default_rng([zlib.crc32(name.encode()), seed]).standard_normal(out[name].shape)
        drawn = base * np.exp(spread * noise) if base else spread * noise
        out[name] = __import__('jax').numpy.asarray(drawn.astype(out[name].dtype))
    for name, factor in factors.items():
        out[name] = (out[name] * factor).astype(out[name].dtype)
    return out
```

```python
import math
from contextlib import ExitStack

import concourse.bass as bass
from concourse import mybir

F32 = mybir.dt.float32
F32R = mybir.dt.float32r
I32 = mybir.dt.int32
ALU = mybir.AluOpType
ACT = mybir.ActivationFunctionType
AX = mybir.AxisListType

P = 128
D = 1024
DC = D // P
SEQ = 512
TB = SEQ // P
N_MEM = 256
MB = N_MEM // P
BANKS = 8
BANK = 512
EPS = 1e-6
HEAD = 64
HALF = HEAD // 2
A_HEADS, IDX_HEADS, B_HEADS = 8, 4, 4
TOPK = min(256, SEQ // 4)
X_HEADS, X_HEAD = 4, 256
D_FF = 2816
FC = D_FF // P
CONV_W = 3
LAMBDA_INIT = 0.8 - 0.6 * math.exp(-0.3 * 0)
HG_HEADS, HG_CHUNK = 8, 32
MLA_HEADS, NOPE, PE_DIM, V_DIM = 8, 128, 64, 128
Q_LORA, KV_LORA = 384, 256
NEG = -1.0e30
TAKEN = -3.0e38

IN_TILES = ((0, 512), (512, 452), (964, 512), (1476, 512), (1988, 512))
HQ, HF, HI, HZ, CQ, CKV, KR, MZ, GLOG = 0, 1024, 2048, 3072, 4096, 4480, 4736, 4800, 5824
HALVES = ((0, 512), (512, 512))


class Weights:
    RAW, SPLIT, SIZE = 2, 3, 2048

    def __init__(self, nc, ctx):
        sb = lambda name, n, dt: ctx.enter_context(nc.sbuf_tensor(name, [P, n, self.SIZE], dt))
        self.raw = sb("weights_raw", self.RAW, F32)
        self.hi = sb("weights_rounded", self.SPLIT, F32R)
        self.lo = sb("weights_remainder", self.SPLIT, F32R)
        sem = lambda name: ctx.enter_context(nc.semaphore(name))
        self.loaded = [sem(f"weight_loaded_{i}") for i in range(self.RAW)]
        self.rounded = sem("weight_rounded")
        self.split = sem("weight_split")
        self.used = sem("weight_used")
        self.tiles = []
        self.used_at = []
        self.need = []
        self.n_loaded = self.n_rounded = self.n_split = self.n_taken = 0
        self.n_used = 0

    def plan(self, chunks, cols, pieces):
        slot = len(self.tiles) % self.RAW
        before = self.need[-self.RAW] if len(self.tiles) >= self.RAW else 0
        self.tiles.append((chunks, cols, pieces))
        self.need.append(before + 16 * len(pieces))

    def plan_rows(self, w, k_chunks, col_tiles, per=4):
        for c0, n in col_tiles:
            for k0 in range(0, k_chunks, per):
                kn = min(per, k_chunks - k0)
                src = w[k0 * P:(k0 + kn) * P, c0:c0 + n].rearrange("(k p) n -> p k n", p=P)
                self.plan(kn, n, [(None, 0, n, src)])

    def last(self):
        return len(self.tiles) - 1

    def view(self, ring, i, slots):
        kn, n, _ = self.tiles[i]
        return ring[:, i % slots, 0:kn * n].rearrange("p (k n) -> p k n", k=kn)

    def load_upto(self, sp, last):
        while self.n_loaded <= min(last, self.last()):
            i = self.n_loaded
            if i >= self.RAW:
                sp.wait_ge(self.split, i - self.RAW + 1)
            raw = self.view(self.raw, i, self.RAW)
            for k, c0, n, src in self.tiles[i][2]:
                dst = raw[:, :, :] if k is None else raw[:, k, c0:c0 + n]
                if k is not None and len(src.shape) == 3:
                    dst = dst.rearrange("p (h c) -> p h c", h=src.shape[1])
                sp.dma_start(dst, src).then_inc(self.loaded[i % self.RAW], 16)
            self.n_loaded += 1

    def round_upto(self, act, last):
        while self.n_rounded <= min(last, self.last()):
            i = self.n_rounded
            act.wait_ge(self.loaded[i % self.RAW], self.need[i])
            if i >= self.SPLIT:
                act.wait_ge(*self.used_at[i - self.SPLIT])
            act.activation(self.view(self.hi, i, self.SPLIT), self.view(self.raw, i, self.RAW),
                           ACT.Copy).then_inc(self.rounded, 1)
            self.n_rounded += 1

    def split_upto(self, pool, last):
        while self.n_split <= min(last, self.last()):
            i = self.n_split
            pool.wait_ge(self.rounded, i + 1)
            pool.tensor_tensor(self.view(self.lo, i, self.SPLIT), self.view(self.raw, i, self.RAW),
                               self.view(self.hi, i, self.SPLIT).bitcast(F32),
                               ALU.subtract).then_inc(self.split, 1)
            self.n_split += 1

    def take(self, pe, chunks, cols):
        i = self.n_taken
        assert self.tiles[i][:2] == (chunks, cols), (i, self.tiles[i][:2], chunks, cols)
        pe.wait_ge(self.split, i + 1)
        self.n_taken += 1
        return self.view(self.hi, i, self.SPLIT), self.view(self.lo, i, self.SPLIT)

    def release(self, ins, sem=None, value=None):
        if sem is None:
            self.n_used += 1
            ins.then_inc(self.used, 1)
            sem, value = self.used, self.n_used
        self.used_at.append((sem, value))


class Core:

    def __init__(self, nc, ctx):
        self.nc = nc
        self.w = Weights(nc, ctx)
        self.bank = [ctx.enter_context(nc.psum_tensor(f"bank{i}", [P, BANK], F32))
                     for i in range(BANKS)]
        sem = lambda name: ctx.enter_context(nc.semaphore(name))
        self.ready = sem("product_ready")
        self.freed = sem("product_read")
        self.groups = 0
        self.xh = ctx.enter_context(nc.sbuf_tensor("columns_rounded", [P, DC, SEQ], F32R))
        self.xl = ctx.enter_context(nc.sbuf_tensor("columns_remainder", [P, DC, SEQ], F32R))
        self.sems = []
        self.n_phase = 0

    def sem(self, name):
        s = self.nc.alloc_semaphore(name=f"{name}_{self.n_phase}")
        self.sems.append(s)
        return s

    def recycle(self):
        self.nc.clear_and_free_semaphores(self.sems)
        self.sems = []
        self.nc.all_engine_barrier()

    def wait_bank(self, pe, g):
        if g >= BANKS:
            pe.wait_ge(self.freed, self.groups_at_start + g - BANKS + 1)

    def products_by_rows(self, pe, g, k_chunks, col_tiles, rows=TB, per=4, x0=0):
        for c0, n in col_tiles:
            for k0 in range(0, k_chunks, per):
                kn = min(per, k_chunks - k0)
                hi, lo = self.w.take(pe, kn, n)
                final = k0 + kn == k_chunks
                for tb in range(rows):
                    if k0 == 0:
                        self.wait_bank(pe, g + tb)
                    for k in range(kn):
                        xs = (slice(None), x0 + k0 + k, slice(tb * P, (tb + 1) * P))
                        for a, b in ((self.xh, hi), (self.xh, lo), (self.xl, hi)):
                            last = k == kn - 1 and b is hi and a is self.xl
                            ins = pe.matmul(self.bank[(g + tb) % BANKS][:, 0:n], a[xs], b[:, k, :],
                                            start=(k0 + k == 0 and b is hi and a is self.xh),
                                            stop=(final and last))
                    if final:
                        ins.then_inc(self.ready, 1)
                        self.groups += 1
                if final:
                    self.w.release(ins, self.ready, self.groups)
                else:
                    self.w.release(ins)
            g += rows
        return g

    def products_by_columns(self, pe, g, k_chunks, cols, x0=0):
        hi, lo = self.w.take(pe, k_chunks, cols)
        for c in range(cols // P):
            self.wait_bank(pe, g)
            for k in range(k_chunks):
                ws = (slice(None), k, slice(c * P, (c + 1) * P))
                for n, (a, b) in enumerate(((hi, self.xh), (lo, self.xh), (hi, self.xl))):
                    ins = pe.matmul(self.bank[g % BANKS][:, :], a[ws], b[:, x0 + k, :],
                                    start=(k == 0 and n == 0), stop=(k == k_chunks - 1 and n == 2))
            ins.then_inc(self.ready, 1)
            self.groups += 1
            g += 1
        self.w.release(ins, self.ready, self.groups)
        return g

    def stage(self, ctx):
        self.n_phase += 1
        self.groups_at_start = self.groups
        self.tile0 = self.w.n_taken
        return ctx.enter_context(self.nc.Block())

    def ahead(self, n_tiles):
        return self.tile0 + n_tiles - 1 + self.w.SPLIT

    def stream(self, block, n_tiles):
        last = self.ahead(n_tiles)

        @block.sync
        def _(sp):
            self.w.load_upto(sp, last + self.w.RAW)

        @block.gpsimd
        def _(pool):
            self.w.split_upto(pool, last)

    def wait_group(self, eng, g):
        eng.wait_ge(self.ready, self.groups_at_start + g + 1)


class Turn:

    def __init__(self, eng, sem):
        self.eng, self.sem, self.n = eng, sem, 0

    def __call__(self, ins):
        ins.then_inc(self.sem, 1)
        self.n += 1
        return ins

    def wait(self):
        if self.n:
            self.eng.wait_ge(self.sem, self.n)


def to_columns(core, src, gain=None, rows=TB, norm=None, width=D, x0=0):
    nc, chunks = core.nc, width // P
    with ExitStack() as ctx:
        squared, mean, rooted, scaled = (core.sem(n) for n in ("squared", "mean", "rooted", "scaled"))
        turned, rounded, remainder = (core.sem(n) for n in ("turned", "rounded", "remainder"))
        block = core.stage(ctx)
        if norm is not None:
            scratch, small = norm
            ss, rms, rstd = small[:, 0:rows], small[:, 4:4 + rows], small[:, 8:8 + rows]
            y = scratch
        else:
            y = src

        @block.tensor
        def _(pe):
            for c in range(chunks):
                for tb in range(rows):
                    if norm is not None and c == 0:
                        pe.wait_ge(scaled, tb + 1)
                    ins = pe.transpose(core.bank[c][:, tb * P:(tb + 1) * P],
                                       y[:, tb, c * P:(c + 1) * P], core.ident[:, :])
                ins.then_inc(turned, 1)

        @block.scalar
        def _(act):
            if norm is not None:
                for tb in range(rows):
                    act.activation(scratch[:, tb, 0:width], src[:, tb, :], ACT.Square,
                                   accum_out=ss[:, tb:tb + 1]).then_inc(squared, 1)
                act.wait_ge(mean, 1)
                act.activation(rms, ss, ACT.Sqrt).then_inc(rooted, 1)
            for c in range(chunks):
                act.wait_ge(turned, c + 1)
                act.activation(core.xh[:, x0 + c, 0:rows * P], core.bank[c][:, 0:rows * P], ACT.Copy,
                               scale=1.0 if gain is None else gain[:, c:c + 1]).then_inc(rounded, 1)

        @block.vector
        def _(dve):
            if norm is not None:
                dve.wait_ge(squared, rows)
                dve.tensor_scalar(ss, ss, 1.0 / width, EPS, ALU.mult, ALU.add).then_inc(mean, 1)
                dve.wait_ge(rooted, 1)
                dve.reciprocal(rstd, rms).then_inc(mean, 1)
                dve.wait_ge(mean, 2)
                for tb in range(rows):
                    dve.tensor_scalar(y[:, tb, 0:width], src[:, tb, :], rstd[:, tb:tb + 1], None,
                                      ALU.mult).then_inc(scaled, 1)
            for c in range(chunks):
                dve.wait_ge(rounded, c + 1)
                hi = core.xh[:, x0 + c, 0:rows * P].bitcast(F32)
                lo = core.xl[:, x0 + c, 0:rows * P]
                if gain is None:
                    dve.tensor_tensor(lo, core.bank[c][:, 0:rows * P], hi,
                                      ALU.subtract).then_inc(remainder, 1)
                else:
                    dve.scalar_tensor_tensor(lo, core.bank[c][:, 0:rows * P], gain[:, c:c + 1], hi,
                                             ALU.mult, ALU.subtract).then_inc(remainder, 1)


def turn_heads(core, moves):
    with ExitStack() as ctx:
        turned, by_act, by_dve = (core.sem(n) for n in ("turned", "copied_act", "copied_dve"))
        block = core.stage(ctx)

        @block.tensor
        def _(pe):
            for g, (src, blocks, _) in enumerate(moves):
                if g >= BANKS:
                    pe.wait_ge((by_act, by_dve)[g % 2], (g - BANKS) // 2 + 1)
                for tb in range(blocks):
                    ins = pe.transpose(core.bank[g % BANKS][:, tb * P:(tb + 1) * P], src(tb),
                                       core.ident[:, :])
                ins.then_inc(turned, 1)

        @block.scalar
        def _(act):
            for g in range(0, len(moves), 2):
                act.wait_ge(turned, g + 1)
                act.activation(moves[g][2], core.bank[g % BANKS][:, 0:moves[g][1] * P],
                               ACT.Copy).then_inc(by_act, 1)

        @block.vector
        def _(dve):
            for g in range(1, len(moves), 2):
                dve.wait_ge(turned, g + 1)
                dve.tensor_copy(moves[g][2], core.bank[g % BANKS][:, 0:moves[g][1] * P])\
                   .then_inc(by_dve, 1)


def attention(core, units, scale, buf, before_dve=None, before_act=None, before_pe=None):
    S_RING, T_RING = 3, 2
    n = len(units)
    probs, turned_sb, small = buf
    S = core.bank[0:S_RING]
    T = core.bank[S_RING:S_RING + T_RING]
    O = core.bank[S_RING + T_RING:S_RING + 2 * T_RING]
    peak, sums = small[:, 0:n], small[:, n:2 * n]
    with ExitStack() as ctx:
        names = ("scores_ready", "biased", "peak_ready", "weights_ready", "turned_ready",
                 "turned_copied", "values_ready", "finished", "finish_step")
        (scores_ready, biased, peak_ready, weights_ready, turned_ready,
         turned_copied, values_ready, finished, finish_step) = (core.sem(x) for x in names)
        block = core.stage(ctx)

        @block.tensor
        def _(pe):
            for i in range(n + 3):
                if i < n:
                    pairs, keys = units[i][:2]
                    if i >= S_RING:
                        pe.wait_ge(biased, i - S_RING + 1)
                    for m, (q, k) in enumerate(pairs):
                        ins = pe.matmul(S[i % S_RING][:, 0:keys], q, k, start=(m == 0),
                                        stop=(m == len(pairs) - 1))
                    ins.then_inc(scores_ready, 1)
                j = i - 2
                if 0 <= j < n:
                    pe.wait_ge(weights_ready, j + 1)
                    if j >= T_RING:
                        pe.wait_ge(turned_copied, j - T_RING + 1)
                    for c in range(units[j][1] // P):
                        ins = pe.transpose(T[j % T_RING][:, c * P:(c + 1) * P],
                                           probs[:, j % S_RING, c * P:(c + 1) * P], core.ident[:, :])
                    ins.then_inc(turned_ready, 1)
                j = i - 3
                if 0 <= j < n:
                    _, keys, _, values, width, _ = units[j]
                    pe.wait_ge(turned_copied, j + 1)
                    if j >= T_RING:
                        pe.wait_ge(finished, j - T_RING + 1)
                    for c in range(keys // P):
                        ins = pe.matmul(O[j % T_RING][:, 0:width],
                                        turned_sb[:, j % T_RING, c * P:(c + 1) * P], values(c),
                                        start=(c == 0), stop=(c == keys // P - 1))
                    ins.then_inc(values_ready, 1)

        @block.vector
        def _(dve):
            turn = Turn(dve, finish_step)
            for i in range(n + 3):
                if i < n:
                    keys, bias = units[i][1:3]
                    dve.wait_ge(scores_ready, i + 1)
                    if i >= S_RING:
                        dve.wait_ge(turned_ready, i - S_RING + 1)
                    dve.tensor_tensor_reduce(
                        out=probs[:, i % S_RING, 0:keys], in0=S[i % S_RING][:, 0:keys], in1=bias,
                        scale=scale, scalar=-3.0e38, op0=ALU.add, op1=ALU.max,
                        accum_out=peak[:, i:i + 1]).then_inc(biased, 1)
                    dve.wait_ge(biased, i + 1)
                    dve.tensor_scalar(peak[:, i:i + 1], peak[:, i:i + 1], -1.0, None,
                                      ALU.mult).then_inc(peak_ready, 1)
                j = i - 3
                if 0 <= j < n:
                    dve.wait_ge(values_ready, j + 1)
                    ins = units[j][5](dve, turn, j, sums[:, j:j + 1],
                                      O[j % T_RING][:, 0:units[j][4]])
                    ins.then_inc(finished, 1)

        @block.scalar
        def _(act):
            for i in range(n + 2):
                if i < n:
                    keys = units[i][1]
                    act.wait_ge(peak_ready, i + 1)
                    p = probs[:, i % S_RING, 0:keys]
                    act.activation(p, p, ACT.Exp, bias=peak[:, i:i + 1],
                                   accum_out=sums[:, i:i + 1]).then_inc(weights_ready, 1)
                j = i - 2
                if 0 <= j < n:
                    keys = units[j][1]
                    act.wait_ge(turned_ready, j + 1)
                    if j >= T_RING:
                        act.wait_ge(values_ready, j - T_RING + 1)
                    act.activation(turned_sb[:, j % T_RING, 0:keys], T[j % T_RING][:, 0:keys],
                                   ACT.Copy).then_inc(turned_copied, 1)


def add_product(core, n_tiles, k_chunks, target, col_tiles=HALVES):
    with ExitStack() as ctx:
        block = core.stage(ctx)

        @block.tensor
        def _(pe):
            core.products_by_rows(pe, 0, k_chunks, col_tiles)

        core.stream(block, n_tiles)

        @block.scalar
        def _(act):
            core.w.round_upto(act, core.ahead(n_tiles))

        @block.vector
        def _(dve):
            g = 0
            for c0, n in col_tiles:
                for tb in range(TB):
                    core.wait_group(dve, g)
                    t = target[:, tb, c0:c0 + n]
                    dve.tensor_tensor(t, core.bank[g % BANKS][:, 0:n], t,
                                      ALU.add).then_inc(core.freed, 1)
                    g += 1


def head_norm(core, x, heads, squares, small, factor=1.0, gain=None, rows=TB):
    width = x.shape[2] // heads
    n = rows * heads
    mean, rms, rstd = small[:, 0:n], small[:, 32:32 + n], small[:, 64:64 + n]
    by_head = lambda a: a.rearrange("p t (h d) -> p t h d", h=heads)
    with ExitStack() as ctx:
        squared, meaned, rooted, normed = (core.sem(s) for s in ("squared", "mean", "rooted", "normed"))
        block = core.stage(ctx)

        @block.scalar
        def _(act):
            for tb in range(rows):
                act.activation(squares[:, tb, :], x[:, tb, :], ACT.Square).then_inc(squared, 1)
            act.wait_ge(meaned, rows + 1)
            act.activation(rms, mean, ACT.Sqrt).then_inc(rooted, 1)

        @block.vector
        def _(dve):
            for tb in range(rows):
                dve.wait_ge(squared, tb + 1)
                dve.tensor_reduce(mean[:, tb * heads:(tb + 1) * heads],
                                  squares[:, tb, :].rearrange("p (h d) -> p h d", h=heads),
                                  AX.X, ALU.add).then_inc(meaned, 1)
            dve.wait_ge(meaned, rows)
            dve.tensor_scalar(mean, mean, 1.0 / width, EPS, ALU.mult, ALU.add).then_inc(meaned, 1)
            dve.wait_ge(rooted, 1)
            dve.reciprocal(rstd, rms).then_inc(normed, 1)
            dve.wait_ge(normed, 1)
            done = 1
            for tb in range(rows):
                xt = x[:, tb, :].rearrange("p (h d) -> p h d", h=heads)
                r = rstd[:, tb * heads:(tb + 1) * heads].unsqueeze(2).to_broadcast([P, heads, width])
                dve.tensor_tensor(xt, xt, r, ALU.mult).then_inc(normed, 1)
                done += 1
                dve.wait_ge(normed, done)
                if gain is not None:
                    g = gain.unsqueeze(1).to_broadcast([P, heads, width])
                    dve.tensor_tensor(xt, xt, g, ALU.mult).then_inc(normed, 1)
                    done += 1
                if factor != 1.0:
                    dve.tensor_scalar(xt, xt, factor, None, ALU.mult).then_inc(normed, 1)
                    done += 1


def rope(dve, turn, x, heads, tables, t1, t2, rows=TB):
    ca, cb, sa, sb = tables
    v = x.rearrange("p t (h d) -> p t h d", h=heads)
    x1, x2 = v[:, :, :, 0:HALF], v[:, :, :, HALF:HEAD]
    wide = lambda a: a.unsqueeze(2).to_broadcast([P, rows, heads, HALF])
    t1 = t1[:, 0:rows * heads * HALF].rearrange("p (t h d) -> p t h d", t=rows, h=heads)
    t2 = t2[:, 0:rows * heads * HALF].rearrange("p (t h d) -> p t h d", t=rows, h=heads)
    turn.wait()
    turn(dve.tensor_tensor(t1, x2, wide(sb), ALU.mult))
    turn(dve.tensor_tensor(t2, x1, wide(sa), ALU.mult))
    turn(dve.tensor_tensor(x1, x1, wide(ca), ALU.mult))
    turn(dve.tensor_tensor(x2, x2, wide(cb), ALU.mult))
    turn.wait()
    turn(dve.tensor_tensor(x1, x1, t1, ALU.subtract))
    turn(dve.tensor_tensor(x2, x2, t2, ALU.add))
    turn.wait()


def plan_weights(w, t):
    w.plan_rows(t["w_in"], DC, IN_TILES)
    w.plan_rows(t["w_out"], DC, HALVES)
    for name in ("w_xk", "w_xv", "w_xq", "w_xo"):
        w.plan_rows(t[name], DC, HALVES)
    for c in range(FC // 2):
        for c0 in (c * 2 * P, D_FF + c * 2 * P):
            w.plan_rows(t["w_ffn_in"], DC, ((c0, 2 * P),), per=DC)
    for k0 in range(0, FC, 4):
        w.plan_rows(t["w_ffn_out"][k0 * P:min(FC, k0 + 4) * P, :], min(4, FC - k0), HALVES)
    w.plan_rows(t["w_in_2"], DC, [(c, 2 * P) for c in range(HQ, HI, 2 * P)], per=DC)
    w.plan_rows(t["w_in_2"], DC, ((HI, 512), (HI + 512, 512)))
    w.plan_rows(t["w_in_2"], DC, ((HZ, 512), (HZ + 512, 512)))
    w.plan_rows(t["w_in_2"], DC, ((CQ, 384), (CKV, 320)))
    uq = t["w_uq_2"].rearrange("(k p) (h c) -> p k h c", p=P, c=NOPE + PE_DIM)
    for h0 in (0, 4):
        w.plan(3, 4 * NOPE, [(k, 0, 4 * NOPE, uq[:, k, h0:h0 + 4, 0:NOPE]) for k in range(3)])
    w.plan(3, 8 * PE_DIM, [(k, 0, 8 * PE_DIM, uq[:, k, :, NOPE:NOPE + PE_DIM]) for k in range(3)])
    ukv = t["w_ukv_2"].rearrange("(k p) (h c) -> p k h c", p=P, c=NOPE + V_DIM)
    w.plan(2, 8 * NOPE, [(k, 0, 8 * NOPE, ukv[:, k, :, 0:NOPE]) for k in range(2)])
    for h0 in (0, 4):
        w.plan(2, 4 * V_DIM, [(k, 0, 4 * V_DIM, ukv[:, k, h0:h0 + 4, NOPE:NOPE + V_DIM])
                              for k in range(2)])
    w.plan_rows(t["w_in_2"], DC, ((MZ, 512), (MZ + 512, 512)))
    w.plan_rows(t["w_in_2"], DC, [(GLOG + 512 * c, 512) for c in range(4)])
    for name in ("w_proj_a_2", "w_proj_b_2", "w_out_2"):
        w.plan_rows(t[name], DC, HALVES)


def two_blocks(nc, t, out, x_saved, y_saved, stop=None):
    ctx = ExitStack()
    with ctx:
        sb = lambda name, shape, dt=F32: ctx.enter_context(nc.sbuf_tensor(name, shape, dt))
        core = Core(nc, ctx)
        plan_weights(core.w, t)
        ident = core.ident = sb("identity", [P, P])
        causal = sb("causal", [P, BANK])
        mask32 = sb("chunk_mask", [P, P])
        columns = sb("column_vectors", [P, 160])
        trig = sb("trig", [P, 2, 2 * TB * HALF])
        small = sb("small", [P, 160])
        lower = sb("lower_bound", [P, 2 * HG_HEADS])
        neg_lambda = sb("neg_lambda", [P, 4])
        hg_gain = sb("hg_gain", [P, P])
        decay = sb("decay", [P, HG_HEADS, SEQ // HG_CHUNK])
        arena = sb("arena", [P, 24704])
        out_stored = ctx.enter_context(nc.semaphore("out_stored"))

        def view(at, *dims):
            n = 1
            for d in dims:
                n *= d
            a = arena[:, at:at + n]
            if len(dims) == 2:
                return a.rearrange("p (a b) -> p a b", a=dims[0])
            return a

        g_mix, g_xattn, g_mem, g_ffn, g_second = (columns[:, 8 * i:8 * i + 8] for i in range(5))
        conv_w, conv_b = columns[:, 40:106], columns[:, 106:128]
        q_a_gain, kv_a_gain, lb_logits = columns[:, 128:131], columns[:, 131:133], columns[:, 133:149]

        def by_chunk(name):
            return t[name].rearrange("l (c p) -> (l c) p", p=P)

        def over_partitions(v):
            return v[0, :].partition_broadcast(P)

        def load(stage_name, dst, src):
            with ExitStack() as c:
                done = core.sem(stage_name)
                block = core.stage(c)

                @block.sync
                def _(sp):
                    sp.dma_start(dst, src).then_inc(done, 16)
                    sp.wait_ge(done, 16)

        x = view(0, TB, D)
        spare = view(4096, TB, D)
        rows_v = view(8192, 2, P)
        position = arena[:, 8448:8456]
        positions_i = arena[:, 8456:8464].bitcast(I32)
        inv_freq = arena[:, 8464:8496]
        angle = view(8704, 2, 2 * TB * HALF)
        turns = view(9216, 2, 2 * TB * HALF)
        gains = view(10240, 4, HEAD)
        lams = view(10496, 4, HEAD)
        tables = arena[:, 14336:16384].rearrange("p (g k n) -> p g k n", g=4, k=4)
        with ExitStack() as c:
            loaded, made, step, ready_ang = (core.sem(s) for s in ("loaded", "made", "step", "angles"))
            x_in, turned, copied, sined = (core.sem(s) for s in ("x_in", "turned", "copied", "sined"))
            lam_exp, freq_set = core.sem("lam_exp"), core.sem("freq_set")
            block = core.stage(c)
            N_LOADS = 21

            @block.sync
            def _(sp):
                core.w.load_upto(sp, 1)
                sp.wait_ge(made, 1)
                at = 0
                for name, src in (("g_mix", by_chunk("g_mix")), ("g_xattn", by_chunk("g_xattn")),
                                  ("g_mem", by_chunk("g_mem")), ("g_ffn", by_chunk("g_ffn")),
                                  ("norm_g_2", by_chunk("norm_g_2")),
                                  ("conv_w", t["conv_w"].rearrange("l j (c p) -> (l j c) p", p=P)),
                                  ("conv_b", by_chunk("conv_b"))):
                    n = src.shape[0]
                    sp.dma_start(rows_v[at:at + n, 0, :], src).then_inc(loaded, 16)
                    at += n
                at = 0
                for name in ("q_a_g_2", "kv_a_g_2", "lb_logits_2"):
                    src = by_chunk(name)
                    sp.dma_start(rows_v[at:at + src.shape[0], 1, :], src).then_inc(loaded, 16)
                    at += src.shape[0]
                core.w.load_upto(sp, core.w.SPLIT - 1 + core.w.RAW)

            @block.gpsimd
            def _(pool):
                pool.memset(rows_v, 0.0).then_inc(made, 1)
                pool.memset(ident[:, :], 0.0).then_inc(made, 1)
                pool.memset(causal[:, :], 0.0).then_inc(made, 1)
                pool.memset(mask32[:, :], 1.0).then_inc(made, 1)
                pool.wait_ge(made, 4)
                pool.affine_select(out=ident[:, :], in_=ident[:, :], compare_op=ALU.not_equal, fill=1.0,
                                   base=0, pattern=[[-1, P]], channel_multiplier=1).then_inc(made, 1)
                diagonal = causal[:, 3 * P:4 * P]
                pool.affine_select(out=diagonal, in_=diagonal, compare_op=ALU.is_ge, fill=NEG,
                                   base=0, pattern=[[-1, P]], channel_multiplier=1).then_inc(made, 1)
                pool.affine_select(out=mask32[:, :], in_=mask32[:, :], compare_op=ALU.is_ge, fill=0.0,
                                   base=0, pattern=[[1, P]], channel_multiplier=-1).then_inc(made, 1)
                pool.wait_ge(made, 7)
                m4 = mask32[:, :].rearrange("p (c s) -> p c s", s=HG_CHUNK)
                pool.affine_select(out=m4, in_=m4, compare_op=ALU.is_ge, fill=0.0, base=0,
                                   pattern=[[-HG_CHUNK, P // HG_CHUNK], [0, HG_CHUNK]],
                                   channel_multiplier=1).then_inc(made, 1)
                pool.iota(positions_i[:, 4:8], [[P, TB]], base=0, channel_multiplier=1)\
                    .then_inc(made, 1)
                for i in range(HALF):
                    pool.memset(inv_freq[:, i:i + 1], 10000.0 ** (-2.0 * i / HEAD)).then_inc(freq_set, 1)
                core.w.split_upto(pool, core.w.SPLIT - 1)

            @block.scalar
            def _(act):
                act.dma_start(x, t["x"].rearrange("l (t p) d -> p (l t) d", p=P)).then_inc(x_in, 16)
                act.dma_start(positions_i[:, 0:4], t["positions"].rearrange("l (t p) -> p (l t)", p=P),
                              allow_slow_non_contiguous=True)\
                   .then_inc(loaded, 16)
                for i, name in enumerate(("g_qa", "g_ka", "g_qb", "g_kb")):
                    act.dma_start(gains[:, i, :], over_partitions(t[name])).then_inc(loaded, 16)
                for i, name in enumerate(("lam_q1", "lam_k1", "lam_q2", "lam_k2")):
                    act.dma_start(lams[:, i, :], over_partitions(t[name])).then_inc(loaded, 16)
                act.dma_start(hg_gain[:, :], over_partitions(t["hg_norm_g_2"])).then_inc(loaded, 16)
                core.w.round_upto(act, core.w.SPLIT - 1)
                act.wait_ge(ready_ang, 1)
                act.activation(trig[:, :, :], angle, ACT.Sin).then_inc(sined, 1)
                act.wait_ge(lam_exp, 1)
                act.activation(neg_lambda[:, 0:2], neg_lambda[:, 0:2], ACT.Exp).then_inc(sined, 1)
                act.activation(lb_logits, lb_logits, ACT.Exp).then_inc(sined, 1)
                act.wait_ge(x_in, 16)

            @block.tensor
            def _(pe):
                pe.wait_ge(made, 5)
                pe.wait_ge(loaded, 16 * (N_LOADS - 1))
                pe.transpose(core.bank[0][:, 0:P], rows_v[:, 0, :], ident[:, :])
                pe.transpose(core.bank[0][:, P:2 * P], rows_v[:, 1, :], ident[:, :]).then_inc(turned, 1)

            @block.vector
            def _(dve):
                turn = Turn(dve, step)
                dve.wait_ge(loaded, 16 * (N_LOADS - 1))
                dve.wait_ge(made, 9)
                dve.wait_ge(freq_set, HALF)
                turn(dve.tensor_copy(position, positions_i))
                turn.wait()
                ang = angle[:, 0, :].rearrange("p (t f) -> p t f", f=HALF)
                turn(dve.tensor_tensor(ang, position.unsqueeze(2).to_broadcast([P, 2 * TB, HALF]),
                                       inv_freq.unsqueeze(1).to_broadcast([P, 2 * TB, HALF]), ALU.mult))
                turn.wait()
                magic = 1.5 * 2.0 ** 23
                turn(dve.tensor_scalar(turns[:, 0, :], angle[:, 0, :], 0.5 / math.pi, None, ALU.mult))
                turn(dve.tensor_scalar(turns[:, 1, :], angle[:, 0, :], 0.5 / math.pi, 0.25,
                                       ALU.mult, ALU.add))
                turn(dve.tensor_copy(angle[:, 1, :], angle[:, 0, :]))
                turn.wait()
                turn(dve.tensor_scalar(turns, turns, magic, None, ALU.add))
                turn.wait()
                turn(dve.tensor_scalar(turns, turns, -magic, None, ALU.add))
                turn.wait()
                part1 = 6.28125
                part2 = 0.0019350051879882812
                part3 = 2.0 * math.pi - part1 - part2
                for part in (part1, part2, part3):
                    turn(dve.scalar_tensor_tensor(angle, turns, -part, angle, ALU.mult, ALU.add))
                    turn.wait()
                turn(dve.tensor_scalar(angle[:, 1, :], angle[:, 1, :], math.pi / 2, None, ALU.add))
                turn.wait()
                dve.tensor_scalar(angle, angle, 3.1415925, -3.1415925, ALU.min, ALU.max)\
                   .then_inc(ready_ang, 1)
                for i in range(2):
                    turn(dve.tensor_tensor(lams[:, 2 * i, :], lams[:, 2 * i, :], lams[:, 2 * i + 1, :],
                                           ALU.mult))
                    turn.wait()
                    turn(dve.tensor_reduce(neg_lambda[:, i:i + 1], lams[:, 2 * i, :], AX.X, ALU.add))
                dve.wait_ge(turned, 1)
                turn(dve.tensor_copy(columns[:, 0:149], core.bank[0][:, 0:149]))
                turn.wait()
                l0, l1 = lb_logits[:, 0:8], lb_logits[:, 8:16]
                top, total = small[:, 0:8], small[:, 8:16]
                turn(dve.tensor_tensor(top, l0, l1, ALU.max))
                turn.wait()
                turn(dve.tensor_tensor(l0, l0, top, ALU.subtract))
                dve.tensor_tensor(l1, l1, top, ALU.subtract).then_inc(lam_exp, 1)
                dve.wait_ge(sined, 3)
                turn(dve.tensor_tensor(neg_lambda[:, 2:3], neg_lambda[:, 1:2], neg_lambda[:, 0:1],
                                       ALU.subtract))
                turn(dve.tensor_tensor(total, l0, l1, ALU.add))
                turn.wait()
                turn(dve.tensor_scalar(neg_lambda[:, 2:3], neg_lambda[:, 2:3], -LAMBDA_INIT, None, ALU.add))
                turn(dve.reciprocal(total, total))
                turn.wait()
                turn(dve.tensor_tensor(lower[:, 0:8], l0, total, ALU.mult))
                turn(dve.tensor_tensor(lower[:, 8:16], l1, total, ALU.mult))
                sin1 = trig[:, 0, 0:TB * HALF].rearrange("p (t f) -> p t f", f=HALF)
                cos1 = trig[:, 1, 0:TB * HALF].rearrange("p (t f) -> p t f", f=HALF)
                for i in range(4):
                    for k, (tab, half) in enumerate(((cos1, 0), (cos1, 1), (sin1, 0), (sin1, 1))):
                        g = gains[:, i, half * HALF:(half + 1) * HALF].unsqueeze(1)\
                            .to_broadcast([P, TB, HALF])
                        turn(dve.tensor_tensor(tables[:, i, k, :].rearrange("p (t f) -> p t f", f=HALF),
                                               tab, g, ALU.mult))

        def table_views(i):
            return [tables[:, i, k, :].rearrange("p (t f) -> p t f", f=HALF) for k in range(4)]

        def plain_tables(which):
            s, c_ = (trig[:, k, which * TB * HALF:(which + 1) * TB * HALF]
                     .rearrange("p (t f) -> p t f", f=HALF) for k in (0, 1))
            return (c_, c_, s, s)

        to_columns(core, x, g_mix, norm=(spare, small))
        qa, mixed, qb, kb, vb = (view(at, TB, n) for at, n in
                                 ((0, 512), (2048, 452), (4096, 512), (6144, 512), (8192, 512)))
        squares = view(10240, TB, 512)
        t1, t2 = view(12288, 1024), view(13312, 1024)
        targets = (qa, mixed, qb, kb, vb)
        normed_heads = {0: (qa, 8), 1: (mixed[:, :, 0:HEAD], 1), 2: (qb, 8), 3: (kb, 8)}
        with ExitStack() as c:
            squared, meaned, rooted, step = (core.sem(s) for s in ("squared", "mean", "rooted", "step"))
            block = core.stage(c)

            @block.tensor
            def _(pe):
                core.products_by_rows(pe, 0, DC, IN_TILES)

            core.stream(block, 10)

            @block.scalar
            def _(act):
                for j, target in enumerate(targets):
                    core.w.round_upto(act, core.tile0 + 2 * j + 3)
                    for tb in range(TB):
                        core.wait_group(act, TB * j + tb)
                        act.activation(target[:, tb, :], core.bank[(TB * j + tb) % BANKS]
                                       [:, 0:IN_TILES[j][1]], ACT.Copy).then_inc(core.freed, 1)
                    if j in normed_heads:
                        src, heads = normed_heads[j]
                        act.wait_ge(core.freed, core.groups_at_start + TB * (j + 1))
                        if j:
                            act.wait_ge(meaned, 2 * j)
                        act.activation(squares[:, :, 0:heads * HEAD], src, ACT.Square)\
                           .then_inc(squared, 1)
                    if j - 1 in normed_heads:
                        n, at = TB * normed_heads[j - 1][1], (j - 1) % 2 * 32
                        act.wait_ge(meaned, 2 * j)
                        act.activation(small[:, 64 + at:64 + at + n], small[:, at:at + n], ACT.Sqrt)\
                           .then_inc(rooted, 1)
                core.w.round_upto(act, core.ahead(10))

            @block.vector
            def _(dve):
                turn = Turn(dve, step)

                def finish(j):
                    src, heads = normed_heads[j]
                    n, at = TB * heads, j % 2 * 32
                    dve.wait_ge(rooted, j + 1)
                    turn(dve.reciprocal(small[:, 128:128 + n], small[:, 64 + at:64 + at + n]))
                    turn.wait()
                    r = small[:, 128:128 + n].rearrange("p (t h) -> p t h", t=TB)
                    v = src.rearrange("p t (h d) -> p t h d", h=heads)
                    turn(dve.tensor_tensor(v, v, r.unsqueeze(3).to_broadcast([P, TB, heads, HEAD]),
                                           ALU.mult))
                    rope(dve, turn, src, heads, table_views(j), t1, t2)
                    if j == 1:
                        rope(dve, turn, mixed[:, :, 2 * HEAD:7 * HEAD], 5, plain_tables(0), t1, t2)

                for j in range(4):
                    src, heads = normed_heads[j]
                    mean = small[:, j % 2 * 32:j % 2 * 32 + TB * heads]
                    dve.wait_ge(squared, j + 1)
                    dve.tensor_reduce(mean, squares[:, :, 0:heads * HEAD]
                                      .rearrange("p t (h d) -> p t h d", h=heads), AX.X, ALU.add)\
                       .then_inc(meaned, 1)
                    dve.wait_ge(meaned, 2 * j + 1)
                    dve.tensor_scalar(mean, mean, 1.0 / HEAD, EPS, ALU.mult, ALU.add)\
                       .then_inc(meaned, 1)
                    if j == 0:
                        continue
                    finish(j - 1)
                finish(3)
                for src, dst in ((0, 0), (6, 1)):
                    for half in range(2):
                        turn(dve.tensor_copy(view(10240 + 512 * dst, TB, P)[:, :, half * HEAD:(half + 1) * HEAD],
                                             mixed[:, :, src * HEAD:(src + 1) * HEAD]))
        qaT, qbT, kbT = view(16384, 4, SEQ), view(18432, 4, SEQ), view(20480, 4, SEQ)
        kaT, kiT, qiT = view(22528, SEQ), view(23040, SEQ), view(23552, 2, SEQ)
        keys_twice = [view(10240 + 512 * i, TB, P) for i in range(2)]
        moves = [(lambda tb, s=src, q=q: s[:, tb, q * P:(q + 1) * P], TB, dst[:, q, :])
                 for src, dst in ((qa, qaT), (qb, qbT), (kb, kbT)) for q in range(4)]
        moves += [(lambda tb, s=keys_twice[0]: s[:, tb, :], TB, kaT),
                  (lambda tb, s=keys_twice[1]: s[:, tb, :], TB, kiT)]
        moves += [(lambda tb, q=q: mixed[:, tb, (2 + 2 * q) * HEAD:(4 + 2 * q) * HEAD], TB, qiT[:, q, :])
                  for q in range(2)]
        turn_heads(core, moves)

        relu, score, select = view(12288, 4, BANK), view(10240, 1, BANK)[:, 0, :], view(14336, 4, BANK)
        top8 = small[:, 96:104]
        with ExitStack() as c:
            scored, rectified, step, summed = (core.sem(s) for s in ("scored", "rectified", "step", "summed"))
            block = core.stage(c)

            @block.tensor
            def _(pe):
                for b in range(1, TB):
                    keys = (b + 1) * P
                    for h in range(IDX_HEADS):
                        half = slice((h % 2) * HEAD, (h % 2 + 1) * HEAD)
                        if b == 3:
                            pe.wait_ge(rectified, h + 1)
                        pe.matmul(core.bank[(b - 1) % 2 * 4 + h][:, 0:keys],
                                  qiT[half, h // 2, b * P:(b + 1) * P], kiT[half, 0:keys],
                                  start=True, stop=True).then_inc(scored, 1)

            @block.scalar
            def _(act):
                for b in range(1, TB):
                    keys = (b + 1) * P
                    if b > 1:
                        act.wait_ge(summed, b - 1)
                    for h in range(IDX_HEADS):
                        act.wait_ge(scored, (b - 1) * 4 + h + 1)
                        act.activation(relu[:, h, 0:keys], core.bank[(b - 1) % 2 * 4 + h][:, 0:keys],
                                       ACT.Relu).then_inc(rectified, 1)

            @block.vector
            def _(dve):
                turn = Turn(dve, step)
                w_idx = mixed[:, :, 7 * HEAD:7 * HEAD + IDX_HEADS]
                turn(dve.tensor_scalar(w_idx, w_idx, IDX_HEADS ** -0.5 * HEAD ** -0.5, None, ALU.mult))
                turn.wait()
                for b in range(1, TB):
                    keys = (b + 1) * P
                    s = score[:, 0:keys]
                    dve.wait_ge(rectified, 4 * b)
                    turn(dve.tensor_scalar(s, relu[:, 0, 0:keys], w_idx[:, b, 0:1], None, ALU.mult))
                    for h in range(1, IDX_HEADS):
                        turn.wait()
                        ins = dve.scalar_tensor_tensor(s, relu[:, h, 0:keys], w_idx[:, b, h:h + 1], s,
                                                       ALU.mult, ALU.add)
                        if h < IDX_HEADS - 1:
                            turn(ins)
                    ins.then_inc(summed, 1)
                    dve.wait_ge(summed, b)
                    turn(dve.tensor_tensor(s, s, causal[:, BANK - keys:BANK], ALU.add))
                    for _i in range(TOPK // 8):
                        turn.wait()
                        turn(dve.max(top8, s))
                        turn.wait()
                        turn(dve.match_replace(s, top8, s, TAKEN))
                    turn.wait()
                    turn(dve.tensor_scalar(select[:, b, 0:keys], s, TAKEN, None, ALU.is_equal))
                    turn.wait()
                    turn(dve.tensor_scalar(select[:, b, 0:keys], select[:, b, 0:keys], -1.0, -NEG,
                                           ALU.add, ALU.mult))

        mix = view(4096, TB, D)
        buffers = (view(0, 3, BANK), view(10240, 2, BANK), small)

        def weighted(target):
            def finish(dve, turn, j, sums, values):
                turn(dve.reciprocal(sums, sums))
                turn.wait()
                return dve.tensor_scalar(target, values, sums, None, ALU.mult)
            return finish

        def less_weighted(target, first):
            def finish(dve, turn, j, sums, values):
                turn(dve.reciprocal(sums, sums))
                turn.wait()
                turn(dve.tensor_scalar(sums, sums, neg_lambda[:, 2:3], None, ALU.mult))
                turn.wait()
                return dve.scalar_tensor_tensor(target, values, sums, first, ALU.mult, ALU.add)
            return finish

        units = []
        for b in range(TB):
            keys = (b + 1) * P
            for h in range(A_HEADS):
                half = slice((h % 2) * HEAD, (h % 2 + 1) * HEAD)
                bias = select[:, b, 0:keys] if b else causal[:, 3 * P:4 * P]
                units.append(([(qaT[half, h // 2, b * P:(b + 1) * P], kaT[half, 0:keys])], keys, bias,
                              lambda k: mixed[:, k, HEAD:2 * HEAD], HEAD,
                              weighted(mix[:, b, h * HEAD:(h + 1) * HEAD])))
        attention(core, units, HEAD ** -0.5, buffers)
        units = []
        for b in range(TB):
            keys = (b + 1) * P
            for h in range(B_HEADS):
                first = view(12288, 2, P)[:, h % 2, :]
                target = mix[:, b, 512 + h * P:512 + (h + 1) * P]
                for k in range(2):
                    half = slice(k * HEAD, (k + 1) * HEAD)
                    units.append(([(qbT[half, h, b * P:(b + 1) * P], kbT[half, h, 0:keys])], keys,
                                  causal[:, BANK - keys:BANK],
                                  lambda c_, h=h: vb[:, c_, h * P:(h + 1) * P], P,
                                  less_weighted(target, first) if k else weighted(first)))
        attention(core, units, HEAD ** -0.5, buffers)
        head_norm(core, mix[:, :, 512:1024], B_HEADS, view(14336, TB, 512), small,
                  factor=1.0 - LAMBDA_INIT)
        to_columns(core, mix)
        load("x_again", x, t["x"].rearrange("l (t p) d -> p (l t) d", p=P))
        add_product(core, 4, DC, x)
        if stop == "mixer":
            return finish_debug(core, x, out, out_stored)

        mem = view(4096, MB, D)
        kN, vN = view(8192, MB, D), view(6144, MB, D)
        kT = view(10240, DC, N_MEM)
        x_gains = view(12288, 2, X_HEAD)
        with ExitStack() as c:
            loaded = core.sem("loaded")
            block = core.stage(c)

            @block.sync
            def _(sp):
                sp.dma_start(mem, t["mem"].rearrange("l (t p) d -> p (l t) d", p=P)).then_inc(loaded, 16)
                sp.dma_start(x_gains[:, 0, :], over_partitions(t["g_xq"])).then_inc(loaded, 16)
                sp.dma_start(x_gains[:, 1, :], over_partitions(t["g_xk"])).then_inc(loaded, 16)
                sp.wait_ge(loaded, 48)

        to_columns(core, mem, g_mem, rows=MB, norm=(view(12800, MB, D), small))

        def rows_product(n_tiles, k_chunks, jobs, rows=TB, per=4):
            with ExitStack() as c:
                block = core.stage(c)

                @block.tensor
                def _(pe):
                    g = 0
                    for target, tiles, x0 in jobs:
                        g = core.products_by_rows(pe, g, k_chunks, tiles, rows=rows, x0=x0)

                core.stream(block, n_tiles)

                @block.scalar
                def _(act):
                    g = 0
                    done = 0
                    for target, tiles, x0 in jobs:
                        c_at = 0
                        for c0, n in tiles:
                            done += -(-k_chunks // per)
                            core.w.round_upto(act, core.tile0 + done - 1 + 2)
                            for tb in range(rows):
                                core.wait_group(act, g)
                                act.activation(target[:, tb, c_at:c_at + n], core.bank[g % BANKS][:, 0:n],
                                               ACT.Copy).then_inc(core.freed, 1)
                                g += 1
                            c_at += n
                    core.w.round_upto(act, core.ahead(n_tiles))

        rows_product(8, DC, ((kN, HALVES, 0), (vN, HALVES, 0)), rows=MB)
        head_norm(core, kN, X_HEADS, view(12800, MB, D), small, gain=x_gains[:, 1, :], rows=MB)
        turn_heads(core, [(lambda tb, q=q: kN[:, tb, q * P:(q + 1) * P], MB, kT[:, q, :])
                          for q in range(DC)])
        qN, qT = view(12800, TB, D), view(16896, DC, SEQ)
        to_columns(core, x, g_xattn, norm=(view(12800, TB, D), small))
        rows_product(4, DC, ((qN, HALVES, 0),))
        head_norm(core, qN, X_HEADS, view(16896, TB, D), small, gain=x_gains[:, 0, :])
        turn_heads(core, [(lambda tb, q=q: qN[:, tb, q * P:(q + 1) * P], TB, qT[:, q, :])
                          for q in range(DC)])
        o = view(12800, TB, D)
        units = []
        for b in range(TB):
            for h in range(X_HEADS):
                units.append(([(qT[:, 2 * h + k, b * P:(b + 1) * P], kT[:, 2 * h + k, :])
                               for k in range(2)], N_MEM, causal[:, 0:N_MEM],
                              lambda k, h=h: vN[:, k, h * X_HEAD:(h + 1) * X_HEAD], X_HEAD,
                              weighted(o[:, b, h * X_HEAD:(h + 1) * X_HEAD])))
        attention(core, units, X_HEAD ** -0.5, (view(20992, 3, BANK), view(22528, 2, BANK), small))
        to_columns(core, o)
        add_product(core, 4, DC, x)
        if stop == "cross":
            return finish_debug(core, x, out, out_stored)
        core.recycle()

        to_columns(core, x, g_ffn, norm=(spare, small))
        hidden = view(4096, FC, SEQ)
        conv, gelu = view(15360, 2, SEQ), view(16384, 2, SEQ)
        with ExitStack() as c:
            started, convolved, activated, step = (core.sem(s) for s in ("started", "convolved",
                                                                         "activated", "step"))
            block = core.stage(c)
            PAIRS = FC // 2

            @block.tensor
            def _(pe):
                for i in range(2 * PAIRS):
                    core.products_by_columns(pe, 2 * i, DC, 2 * P)

            core.stream(block, 2 * PAIRS)

            @block.scalar
            def _(act):
                for i in range(PAIRS):
                    core.w.round_upto(act, core.tile0 + 2 * i + 2)
                    for k in range(2):
                        ch = 2 * i + k
                        core.wait_group(act, 4 * i + k)
                        if i:
                            act.wait_ge(activated, 2 * i - 1 + k)
                        act.activation(conv[:, k, :], core.bank[(4 * i + k) % BANKS][:, :], ACT.Identity,
                                       scale=conv_w[:, 2 * FC + ch:2 * FC + ch + 1],
                                       bias=conv_b[:, ch:ch + 1]).then_inc(started, 1)
                    core.w.round_upto(act, core.tile0 + 2 * i + 3)
                    for k in range(2):
                        act.wait_ge(core.freed, core.groups_at_start + 4 * i + k + 1)
                        if i:
                            act.wait_ge(core.freed, core.groups_at_start + 4 * (i - 1) + 3 + k)
                        act.activation(gelu[:, k, :], conv[:, k, :], ACT.Gelu_apprx_tanh)\
                           .then_inc(activated, 1)
                core.w.round_upto(act, core.ahead(2 * PAIRS))

            @block.vector
            def _(dve):
                for i in range(PAIRS):
                    for k in range(2):
                        ch = 2 * i + k
                        a = core.bank[(4 * i + k) % BANKS]
                        dve.wait_ge(started, ch + 1)
                        w = lambda j: conv_w[:, j * FC + ch:j * FC + ch + 1]
                        dve.scalar_tensor_tensor(conv[:, k, 1:SEQ], a[:, 0:SEQ - 1], w(1),
                                                 conv[:, k, 1:SEQ], ALU.mult, ALU.add)\
                           .then_inc(step, 1)
                        dve.wait_ge(step, ch + 1)
                        dve.scalar_tensor_tensor(conv[:, k, 2:SEQ], a[:, 0:SEQ - 2], w(0),
                                                 conv[:, k, 2:SEQ], ALU.mult, ALU.add)\
                           .then_inc(core.freed, 1)
                    for k in range(2):
                        g = 4 * i + 2 + k
                        core.wait_group(dve, g)
                        dve.wait_ge(activated, 2 * i + k + 1)
                        dve.tensor_tensor(hidden[:, 2 * i + k, :], core.bank[g % BANKS][:, :],
                                          gelu[:, k, :], ALU.mult).then_inc(core.freed, 1)

        with ExitStack() as c:
            rounded, remainder = core.sem("rounded"), core.sem("remainder")
            block = core.stage(c)
            K_GROUPS = [(k0, min(4, FC - k0)) for k0 in range(0, FC, 4)]
            released = []

            @block.tensor
            def _(pe):
                for i, (k0, kn) in enumerate(K_GROUPS):
                    pe.wait_ge(remainder, i + 1)
                    for half in range(2):
                        hi, lo = core.w.take(pe, kn, 512)
                        for tb in range(TB):
                            for k in range(kn):
                                xs = (slice(None), i % 2 * 4 + k, slice(tb * P, (tb + 1) * P))
                                for a, b in ((core.xh, hi), (core.xh, lo), (core.xl, hi)):
                                    last = k == kn - 1 and a is core.xl
                                    first = k == 0 and a is core.xh and b is hi
                                    ins = pe.matmul(core.bank[half * TB + tb][:, :], a[xs], b[:, k, :],
                                                    start=(i == 0 and first),
                                                    stop=(k0 + kn == FC and last))
                            if k0 + kn == FC:
                                ins.then_inc(core.ready, 1)
                                core.groups += 1
                        if k0 + kn == FC:
                            core.w.release(ins, core.ready, core.groups)
                        else:
                            core.w.release(ins)
                    released.append(core.w.used_at[-1])

            core.stream(block, 2 * len(K_GROUPS))

            @block.scalar
            def _(act):
                for i, (k0, kn) in enumerate(K_GROUPS):
                    if i >= 2:
                        act.wait_ge(*released[i - 2])
                    act.activation(core.xh[:, i % 2 * 4:i % 2 * 4 + kn, :], hidden[:, k0:k0 + kn, :],
                                   ACT.Copy).then_inc(rounded, 1)
                    core.w.round_upto(act, core.tile0 + 2 * i + 2)
                core.w.round_upto(act, core.ahead(2 * len(K_GROUPS)))

            @block.vector
            def _(dve):
                for i, (k0, kn) in enumerate(K_GROUPS):
                    dve.wait_ge(rounded, i + 1)
                    part = (slice(None), slice(i % 2 * 4, i % 2 * 4 + kn))
                    dve.tensor_tensor(core.xl[part], hidden[:, k0:k0 + kn, :],
                                      core.xh[part].bitcast(F32), ALU.subtract).then_inc(remainder, 1)
                for g in range(2 * TB):
                    core.wait_group(dve, g)
                    target = x[:, g % TB, g // TB * 512:(g // TB + 1) * 512]
                    dve.tensor_tensor(target, core.bank[g][:, :], target, ALU.add)\
                       .then_inc(core.freed, 1)
        if stop == "ffn":
            return finish_debug(core, x, out, out_stored)

        to_columns(core, x, g_second, norm=(spare, small))
        saved_rows = lambda a: a.rearrange("(t p) d -> p t d", p=P)
        load("x_out", saved_rows(x_saved), x)
        Q, K, KI, KON, V = (view(4096 * i, n, 4096 // n) for i, n in enumerate((8, 8, 8, TB, TB)))
        scratch = view(20480, 6, SEQ)
        state = arena[:, 23552:23552 + HG_HEADS * P].rearrange("p (h v) -> p h v", h=HG_HEADS)
        with ExitStack() as c:
            sigmoid = core.sem("sigmoid")
            block = core.stage(c)

            @block.tensor
            def _(pe):
                for i in range(8):
                    core.products_by_columns(pe, 2 * i, DC, 2 * P)
                core.products_by_rows(pe, 16, DC, HALVES)

            core.stream(block, 12)

            @block.scalar
            def _(act):
                for g in range(16):
                    if g % 2 == 0:
                        core.w.round_upto(act, core.tile0 + g // 2 + 2)
                    core.wait_group(act, g)
                    if g >= 2:
                        act.wait_ge(core.freed, core.groups_at_start + g - 1)
                    dst = scratch[:, g % 2, :] if g < 8 else K[:, g - 8, :]
                    act.activation(dst, core.bank[g % BANKS][:, :], ACT.Sigmoid).then_inc(sigmoid, 1)
                core.w.round_upto(act, core.ahead(12))

            @block.vector
            def _(dve):
                for g in range(8):
                    dve.wait_ge(sigmoid, g + 1)
                    dve.tensor_tensor(Q[:, g, :], core.bank[g % BANKS][:, :], scratch[:, g % 2, :],
                                      ALU.mult).then_inc(core.freed, 1)
                for h in range(8):
                    dve.wait_ge(sigmoid, 8 + h + 1)
                    dve.tensor_scalar(K[:, h, :], K[:, h, :], lower[:, 8 + h:9 + h], lower[:, h:h + 1],
                                      ALU.mult, ALU.add).then_inc(core.freed, 1)
                for g in range(16, 24):
                    core.wait_group(dve, g)
                    half, tb = divmod(g - 16, TB)
                    dve.tensor_copy(V[:, tb, half * 512:(half + 1) * 512], core.bank[g % BANKS][:, :])\
                       .then_inc(core.freed, 1)
        keep = view(4096 * 3, SEQ)
        with ExitStack() as c:
            kept, logged, scanned, to_last, up, down, out_ = (core.sem(s) for s in (
                "kept", "logged", "scanned", "to_last", "exp_b", "exp_minus_b", "exp_to_last"))
            made_q, made_ki, made_k, turned, copied, one_less, decayed = (core.sem(s) for s in (
                "made_q", "made_ki", "made_k", "turned", "copied", "one_less", "decayed"))
            block = core.stage(c)
            b_ = KI

            @block.gpsimd
            def _(pool):
                pool.memset(keep, 1.0).then_inc(kept, 1)
                pool.wait_ge(kept, 1)
                k2 = keep.rearrange("p (n c) -> p n c", c=HG_CHUNK)
                pool.affine_select(out=k2, in_=k2, compare_op=ALU.not_equal, fill=0.0, base=0,
                                   pattern=[[0, SEQ // HG_CHUNK], [1, HG_CHUNK]], channel_multiplier=0)\
                    .then_inc(kept, 1)

            @block.scalar
            def _(act):
                for h in range(HG_HEADS):
                    act.activation(b_[:, h, :], K[:, h, :], ACT.Ln).then_inc(logged, 1)
                for h in range(HG_HEADS):
                    act.wait_ge(to_last, h + 1)
                    if h >= 2:
                        act.wait_ge(decayed, h - 1)
                    act.activation(scratch[:, h % 2, :], b_[:, h, :], ACT.Exp).then_inc(up, 1)
                    act.activation(scratch[:, 2 + h % 2, :], b_[:, h, :], ACT.Exp, scale=-1.0)\
                       .then_inc(down, 1)
                    d = scratch[:, 4 + h % 2, :]
                    act.activation(d, d, ACT.Exp).then_inc(out_, 1)

            @block.vector
            def _(dve):
                dve.wait_ge(kept, 2)
                for h in range(HG_HEADS):
                    dve.wait_ge(logged, h + 1)
                    dve.tensor_tensor_scan(b_[:, h, :], keep, b_[:, h, :], 0.0, ALU.mult, ALU.add)\
                       .then_inc(scanned, 1)
                    dve.tensor_scalar(K[:, h, :], K[:, h, :], -1.0, 1.0, ALU.mult, ALU.add)\
                       .then_inc(one_less, 1)

                def last_minus(h):
                    if h >= 2:
                        dve.wait_ge(made_k, h - 1)
                    dve.wait_ge(scanned, h + 1)
                    b3 = b_[:, h, :].rearrange("p (n c) -> p n c", c=HG_CHUNK)
                    d3 = scratch[:, 4 + h % 2, :].rearrange("p (n c) -> p n c", c=HG_CHUNK)
                    last = b3[:, :, HG_CHUNK - 1:HG_CHUNK].to_broadcast([P, SEQ // HG_CHUNK, HG_CHUNK])
                    dve.tensor_tensor(d3, last, b3, ALU.subtract).then_inc(to_last, 1)

                last_minus(0)
                for h in range(HG_HEADS):
                    if h + 1 < HG_HEADS:
                        last_minus(h + 1)
                    dve.wait_ge(one_less, h + 1)
                    dve.wait_ge(up, h + 1)
                    dve.tensor_tensor(Q[:, h, :], Q[:, h, :], scratch[:, h % 2, :], ALU.mult)\
                       .then_inc(made_q, 1)
                    e3 = scratch[:, h % 2, :].rearrange("p (n c) -> p n c", c=HG_CHUNK)
                    dve.tensor_copy(decay[:, h, :], e3[:, :, HG_CHUNK - 1]).then_inc(made_q, 1)
                    dve.wait_ge(down, h + 1)
                    dve.tensor_tensor(KI[:, h, :], K[:, h, :], scratch[:, 2 + h % 2, :], ALU.mult)\
                       .then_inc(decayed, 1)
                    dve.wait_ge(out_, h + 1)
                    dve.wait_ge(decayed, h + 1)
                    dve.tensor_tensor(K[:, h, :], K[:, h, :], scratch[:, 4 + h % 2, :], ALU.mult)\
                       .then_inc(made_k, 1)

        turn_heads(core, [(lambda tb, h=h: K[:, h, tb * P:(tb + 1) * P], TB,
                           KON[:, :, h * P:(h + 1) * P]) for h in range(HG_HEADS)])
        C = P // HG_CHUNK
        intra = view(20480, 2, HG_HEADS * P)
        o = view(4096, TB, D)
        with ExitStack() as c:
            cleared, scores_in, masked, intra_done, kv_done = (core.sem(s) for s in (
                "cleared", "scores_in", "masked", "intra_done", "kv_done"))
            updated, out_ready, out_read = (core.sem(s) for s in ("updated", "out_ready", "out_read"))
            block = core.stage(c)

            @block.tensor
            def _(pe):
                for tb in range(TB):
                    tok = slice(tb * P, (tb + 1) * P)
                    if tb >= 1:
                        pe.wait_ge(masked, 2 * tb)
                    for h in range(HG_HEADS):
                        ins = pe.matmul(core.bank[h // 4][:, h % 4 * P:(h % 4 + 1) * P],
                                        KI[:, h, tok], Q[:, h, tok], start=True, stop=True)
                        if h % 4 == 3:
                            ins.then_inc(scores_in, 1)
                    ob = core.bank[2 + tb % 2 * 2:4 + tb % 2 * 2]
                    if tb >= 2:
                        pe.wait_ge(out_read, 2 * (tb - 1))
                    for h in range(HG_HEADS):
                        pe.wait_ge(masked, 2 * tb + h // 4 + 1)
                        pe.matmul(ob[h // 4][:, h % 4 * P:(h % 4 + 1) * P],
                                  intra[:, tb % 2, h * P:(h + 1) * P], V[:, tb, h * P:(h + 1) * P],
                                  start=(h % 4 == 0), stop=False, skip_group_check=True)\
                          .then_inc(intra_done, 1)
                    for n in range(C):
                        step = tb * C + n
                        rows = slice(n * HG_CHUNK, (n + 1) * HG_CHUNK)
                        for g in range(2):
                            heads = range(4 * g, 4 * g + 4)
                            pe.wait_ge(updated, HG_HEADS * step + 4 * g + 4)
                            for h in heads:
                                ins = pe.matmul(ob[g][rows, h % 4 * P:(h % 4 + 1) * P],
                                                Q[:, h, tb * P + n * HG_CHUNK:tb * P + (n + 1) * HG_CHUNK],
                                                state[:, h, :], start=False, stop=(h % 4 == 3),
                                                skip_group_check=True)
                            if n == C - 1:
                                ins.then_inc(out_ready, 1)
                            if step < TB * C - 1:
                                for h in heads:
                                    ins = pe.matmul(core.bank[6 + g][:, h % 4 * P:(h % 4 + 1) * P],
                                                    KON[rows, tb, h * P:(h + 1) * P],
                                                    V[rows, tb, h * P:(h + 1) * P], start=True, stop=True)
                                ins.then_inc(kv_done, 1)

            @block.vector
            def _(dve):
                dve.memset(intra, 0.0).then_inc(cleared, 1)
                for h in range(HG_HEADS):
                    dve.memset(state[:, h, :], 0.0).then_inc(updated, 1)
                dve.wait_ge(cleared, 1)
                m = mask32[:, :].bitcast(I32).unsqueeze(1).to_broadcast([P, 4, P])

                def mask(tb):
                    if tb >= 2:
                        dve.wait_ge(intra_done, HG_HEADS * (tb - 1))
                    for g in range(2):
                        dve.wait_ge(scores_in, 2 * tb + g + 1)
                        dst = intra[:, tb % 2, g * BANK:(g + 1) * BANK].rearrange("p (h s) -> p h s", h=4)
                        dve.copy_predicated(dst, m, core.bank[g][:, :].rearrange("p (h s) -> p h s", h=4))\
                           .then_inc(masked, 1)

                for tb in range(TB):
                    mask(tb)
                    for n in range(C):
                        step = tb * C + n
                        if step == TB * C - 1:
                            break
                        for h in range(HG_HEADS):
                            dve.wait_ge(kv_done, 2 * step + h // 4 + 1)
                            dve.wait_ge(updated, HG_HEADS * step + h + 1)
                            dve.scalar_tensor_tensor(
                                state[:, h, :], state[:, h, :], decay[:, h, step:step + 1],
                                core.bank[6 + h // 4][:, h % 4 * P:(h % 4 + 1) * P],
                                ALU.mult, ALU.add).then_inc(updated, 1)

            @block.scalar
            def _(act):
                for tb in range(TB):
                    for g in range(2):
                        act.wait_ge(out_ready, 2 * tb + g + 1)
                        act.activation(o[:, tb, g * BANK:(g + 1) * BANK], core.bank[2 + tb % 2 * 2 + g][:, :],
                                       ACT.Copy).then_inc(out_read, 1)
        head_norm(core, o, HG_HEADS, view(0, TB, D), small, gain=hg_gain[:, :])

        def gated_product(n_tiles, target, func, gate_buf):
            with ExitStack() as c:
                gated = core.sem("gated")
                block = core.stage(c)

                @block.tensor
                def _(pe):
                    core.products_by_rows(pe, 0, DC, HALVES)

                core.stream(block, n_tiles)

                @block.scalar
                def _(act):
                    for g in range(2 * TB):
                        if g % TB == 0:
                            core.w.round_upto(act, core.tile0 + 2 * (g // TB) + 3)
                        core.wait_group(act, g)
                        if g >= 2:
                            act.wait_ge(core.freed, core.groups_at_start + g - 1)
                        act.activation(gate_buf[:, g % 2, :], core.bank[g][:, :], func)\
                           .then_inc(gated, 1)
                    core.w.round_upto(act, core.ahead(n_tiles))

                @block.vector
                def _(dve):
                    for g in range(2 * TB):
                        dve.wait_ge(gated, g + 1)
                        tt = target[:, g % TB, g // TB * 512:(g // TB + 1) * 512]
                        dve.tensor_tensor(tt, tt, gate_buf[:, g % 2, :], ALU.mult)\
                           .then_inc(core.freed, 1)

        gated_product(4, o, ACT.Silu, view(0, 2, 512))
        load("y_a_out", saved_rows(y_saved), o)
        core.recycle()

        qnT, knT, vN = view(0, 8, SEQ), view(4096, 8, SEQ), view(8192, TB, D)
        qpT, kpT = view(12288, 4, SEQ), view(14336, SEQ)
        cN = view(14848, TB, Q_LORA + KV_LORA + PE_DIM)
        qpN = view(17664, TB, 8 * PE_DIM)
        t1, t2 = view(19712, 1024), view(20736, 1024)
        kr_twice = view(21760, TB, P)
        rows_product(4, DC, ((cN, ((0, 384), (384, 320)), 0),))
        to_columns(core, cN[:, :, 0:Q_LORA], q_a_gain, norm=(view(17664, TB, Q_LORA), small),
                   width=Q_LORA)
        to_columns(core, cN[:, :, Q_LORA:Q_LORA + KV_LORA], kv_a_gain,
                   norm=(view(17664, TB, KV_LORA), small), width=KV_LORA, x0=3)
        with ExitStack() as c:
            rotated = core.sem("rotated")
            block = core.stage(c)

            @block.tensor
            def _(pe):
                g = core.products_by_columns(pe, 0, 3, 4 * NOPE)
                g = core.products_by_columns(pe, g, 3, 4 * NOPE)
                g = core.products_by_rows(pe, g, 3, ((0, 8 * PE_DIM),))
                g = core.products_by_columns(pe, g, 2, 8 * NOPE, x0=3)
                core.products_by_rows(pe, g, 2, HALVES, x0=3)

            core.stream(block, 6)

            @block.scalar
            def _(act):
                places = [(qnT[:, h, :], 0 if h < 4 else 1) for h in range(8)]
                places += [(qpN[:, tb, :], 2) for tb in range(TB)]
                places += [(knT[:, h, :], 3) for h in range(8)]
                places += [(vN[:, tb, 512 * half:512 * (half + 1)], 4 + half)
                           for half in range(2) for tb in range(TB)]
                for g, (dst, tile) in enumerate(places):
                    core.w.round_upto(act, core.tile0 + tile + 2)
                    core.wait_group(act, g)
                    act.activation(dst, core.bank[g % BANKS][:, :], ACT.Copy).then_inc(core.freed, 1)
                core.w.round_upto(act, core.ahead(6))

            @block.vector
            def _(dve):
                turn = Turn(dve, rotated)
                kr = cN[:, :, Q_LORA + KV_LORA:]
                rope(dve, turn, kr, 1, plain_tables(1), t1, t2)
                for half in range(2):
                    turn(dve.tensor_copy(kr_twice[:, :, half * HEAD:(half + 1) * HEAD], kr))
                dve.wait_ge(core.freed, core.groups_at_start + 12)
                rope(dve, turn, qpN, 8, plain_tables(1), t1, t2)

        turn_heads(core, [(lambda tb, q=q: qpN[:, tb, q * P:(q + 1) * P], TB, qpT[:, q, :])
                          for q in range(4)] + [(lambda tb: kr_twice[:, tb, :], TB, kpT)])
        y_b = view(14848, TB, D)
        units = []
        for b in range(TB):
            keys = (b + 1) * P
            q_tok = slice(b * P, (b + 1) * P)
            for h in range(MLA_HEADS):
                half = slice((h % 2) * HEAD, (h % 2 + 1) * HEAD)
                units.append(([(qnT[:, h, q_tok], knT[:, h, 0:keys]),
                               (qpT[half, h // 2, q_tok], kpT[half, 0:keys])], keys,
                              causal[:, BANK - keys:BANK],
                              lambda k, h=h: vN[:, k, h * P:(h + 1) * P], V_DIM,
                              weighted(y_b[:, b, h * P:(h + 1) * P])))
        attention(core, units, (NOPE + PE_DIM) ** -0.5, (view(18944, 3, BANK), view(20480, 2, BANK), small))

        x = view(10240, TB, D)
        load("x_again", x, saved_rows(x_saved))
        to_columns(core, x, g_second, norm=(view(18944, TB, D), small))
        gated_product(4, y_b, ACT.Silu, view(0, 2, 512))
        gates = arena[:, 0:8192].rearrange("p (n t d) -> p n t d", n=2, t=TB)
        gate_bias = view(8192, 2 * D)
        load("gate_bias", gate_bias, over_partitions(t["b_gate_2"]))
        with ExitStack() as c:
            biased, gated = core.sem("biased"), core.sem("gated")
            block = core.stage(c)

            @block.tensor
            def _(pe):
                core.products_by_rows(pe, 0, DC, [(0, 512)] * 4)

            core.stream(block, 8)

            @block.vector
            def _(dve):
                for g in range(4 * TB):
                    c_, tb = divmod(g, TB)
                    core.wait_group(dve, g)
                    dve.tensor_tensor(gates[:, c_ // 2, tb, c_ % 2 * 512:(c_ % 2 + 1) * 512],
                                      core.bank[g % BANKS][:, :], gate_bias[:, c_ * 512:(c_ + 1) * 512],
                                      ALU.add).then_inc(core.freed, 1)

            @block.scalar
            def _(act):
                for g in range(4 * TB):
                    c_, tb = divmod(g, TB)
                    if tb == 0:
                        core.w.round_upto(act, core.tile0 + 2 * c_ + 3)
                    act.wait_ge(core.freed, core.groups_at_start + g + 1)
                    part = gates[:, c_ // 2, tb, c_ % 2 * 512:(c_ % 2 + 1) * 512]
                    act.activation(part, part, ACT.Sigmoid).then_inc(gated, 1)
                core.w.round_upto(act, core.ahead(8))

        def gate_product(branch):
            with ExitStack() as c:
                step = core.sem("step")
                block = core.stage(c)

                @block.tensor
                def _(pe):
                    core.products_by_rows(pe, 0, DC, HALVES)

                core.stream(block, 4)

                @block.scalar
                def _(act):
                    core.w.round_upto(act, core.ahead(4))

                @block.vector
                def _(dve):
                    for g in range(2 * TB):
                        core.wait_group(dve, g)
                        part = (slice(None), branch, g % TB, slice(g // TB * 512, (g // TB + 1) * 512))
                        dve.tensor_tensor(gates[part], core.bank[g][:, :], gates[part], ALU.mult)\
                           .then_inc(core.freed, 1)
                        if branch:
                            first = (part[0], 0) + part[2:]
                            dve.wait_ge(core.freed, core.groups_at_start + g + 1)
                            dve.tensor_tensor(gates[first], gates[first], gates[part], ALU.add)\
                               .then_inc(step, 1)

        y_a = view(18944, TB, D)
        load("y_a_in", y_a, saved_rows(y_saved))
        to_columns(core, y_a)
        gate_product(0)
        to_columns(core, y_b)
        gate_product(1)
        to_columns(core, gates[:, 0])
        add_product(core, 4, DC, x)
        assert core.w.n_taken == len(core.w.tiles)

        final_gain, y = view(8192, D), view(0, TB, D)
        with ExitStack() as c:
            loaded, squared, mean, rooted, scaled, gained = (core.sem(s) for s in (
                "loaded", "squared", "mean", "rooted", "scaled", "gained"))
            block = core.stage(c)
            ss, rms, rstd = small[:, 0:TB], small[:, 4:4 + TB], small[:, 8:8 + TB]

            @block.scalar
            def _(act):
                for tb in range(TB):
                    act.activation(y[:, tb, :], x[:, tb, :], ACT.Square,
                                   accum_out=ss[:, tb:tb + 1]).then_inc(squared, 1)
                act.wait_ge(mean, 1)
                act.activation(rms, ss, ACT.Sqrt).then_inc(rooted, 1)

            @block.vector
            def _(dve):
                dve.wait_ge(squared, TB)
                dve.tensor_scalar(ss, ss, 1.0 / D, EPS, ALU.mult, ALU.add).then_inc(mean, 1)
                dve.wait_ge(rooted, 1)
                dve.reciprocal(rstd, rms).then_inc(mean, 1)
                dve.wait_ge(mean, 2)
                dve.wait_ge(loaded, 16)
                for tb in range(TB):
                    dve.scalar_tensor_tensor(y[:, tb, :], x[:, tb, :], rstd[:, tb:tb + 1],
                                             final_gain, ALU.mult, ALU.mult).then_inc(scaled, 1)

            @block.sync
            def _(sp):
                sp.dma_start(final_gain, t["final_norm_g_2"].partition_broadcast(P)).then_inc(loaded, 16)
                dst = out.rearrange("l (t p) d -> p (l t) d", p=P)
                for tb in range(TB):
                    sp.wait_ge(scaled, tb + 1)
                    sp.dma_start(dst[:, tb, :], y[:, tb, :]).then_inc(out_stored, 16)
                sp.wait_ge(out_stored, 16 * TB)


def finish_debug(core, x, out, out_stored):
    with ExitStack() as c:
        block = core.stage(c)

        @block.sync
        def _(sp):
            sp.dma_start(out.rearrange("l (t p) d -> p (l t) d", p=P), x).then_inc(out_stored, 16)
            sp.wait_ge(out_stored, 16)


INPUTS = ("x mem positions g_mix w_in g_qa g_ka g_qb g_kb lam_q1 lam_k1 lam_q2 lam_k2 w_out g_xattn "
          "g_mem w_xq w_xk w_xv w_xo g_xq g_xk g_ffn w_ffn_in conv_w conv_b w_ffn_out norm_g_2 w_in_2 "
          "b_gate_2 lb_logits_2 hg_norm_g_2 q_a_g_2 w_uq_2 kv_a_g_2 w_ukv_2 w_proj_a_2 w_proj_b_2 "
          "w_out_2 final_norm_g_2").split()
STOP = None


def kernel(**inputs):
    import numpy as _np
    import concourse.bacc as _bacc
    from concourse.bass_utils import run_bass_kernel_spmd as _run

    nc = _bacc.Bacc("TRN2", target_bir_lowering=False, num_devices=1)
    arrays, aps = {}, {}
    for name in INPUTS:
        a = _np.ascontiguousarray(inputs[name])
        arrays[f"in_{name}"] = a
        ap = nc.dram_tensor(f"in_{name}", a.shape, mybir.dt.from_np(a.dtype), kind="ExternalInput").ap()
        is_matrix = name.startswith("w_")
        aps[name] = ap[0] if is_matrix else ap
    out = nc.dram_tensor("out", (1, SEQ, D), F32, kind="ExternalOutput").ap()
    x_saved = nc.dram_tensor("x_saved", (SEQ, D), F32, kind="Internal").ap()
    y_saved = nc.dram_tensor("y_saved", (SEQ, D), F32, kind="Internal").ap()
    two_blocks(nc, aps, out, x_saved, y_saved, stop=STOP)
    r = _run(nc, [arrays], core_ids=[0])
    return r.results[0]["out"]
```

```python
import math
from contextlib import ExitStack

import concourse.bass as bass
from concourse import mybir

F32 = mybir.dt.float32
F32R = mybir.dt.float32r
I32 = mybir.dt.int32
ALU = mybir.AluOpType
ACT = mybir.ActivationFunctionType
AX = mybir.AxisListType

P = 128
D = 1024
DC = D // P
SEQ = 512
TB = SEQ // P
N_MEM = 256
MB = N_MEM // P
BANKS = 8
BANK = 512
EPS = 1e-6
HEAD = 64
HALF = HEAD // 2
A_HEADS, IDX_HEADS, B_HEADS = 8, 4, 4
TOPK = min(256, SEQ // 4)
X_HEADS, X_HEAD = 4, 256
D_FF = 2816
FC = D_FF // P
CONV_W = 3
LAMBDA_INIT = 0.8 - 0.6 * math.exp(-0.3 * 0)
HG_HEADS, HG_CHUNK = 8, 32
MLA_HEADS, NOPE, PE_DIM, V_DIM = 8, 128, 64, 128
Q_LORA, KV_LORA = 384, 256
NEG = -1.0e30
TAKEN = -3.0e38

IN_TILES = ((0, 512), (512, 452), (964, 512), (1476, 512), (1988, 512))
HQ, HF, HI, HZ, CQ, CKV, KR, MZ, GLOG = 0, 1024, 2048, 3072, 4096, 4480, 4736, 4800, 5824
HALVES = ((0, 512), (512, 512))


class Weights:
    RAW, SPLIT, SIZE = 2, 3, 2048

    def __init__(self, nc, ctx):
        sb = lambda name, n, dt: ctx.enter_context(nc.sbuf_tensor(name, [P, n, self.SIZE], dt))
        self.raw = sb("weights_raw", self.RAW, F32)
        self.hi = sb("weights_rounded", self.SPLIT, F32R)
        self.lo = sb("weights_remainder", self.SPLIT, F32R)
        sem = lambda name: ctx.enter_context(nc.semaphore(name))
        self.loaded = [sem(f"weight_loaded_{i}") for i in range(self.RAW)]
        self.rounded = sem("weight_rounded")
        self.split = sem("weight_split")
        self.used = sem("weight_used")
        self.tiles = []
        self.used_at = []
        self.need = []
        self.n_loaded = self.n_rounded = self.n_split = self.n_taken = 0
        self.n_used = 0

    def plan(self, chunks, cols, pieces):
        slot = len(self.tiles) % self.RAW
        before = self.need[-self.RAW] if len(self.tiles) >= self.RAW else 0
        self.tiles.append((chunks, cols, pieces))
        self.need.append(before + 16 * len(pieces))

    def plan_rows(self, w, k_chunks, col_tiles, per=4):
        for c0, n in col_tiles:
            for k0 in range(0, k_chunks, per):
                kn = min(per, k_chunks - k0)
                src = w[k0 * P:(k0 + kn) * P, c0:c0 + n].rearrange("(k p) n -> p k n", p=P)
                self.plan(kn, n, [(None, 0, n, src)])

    def last(self):
        return len(self.tiles) - 1

    def view(self, ring, i, slots):
        kn, n, _ = self.tiles[i]
        return ring[:, i % slots, 0:kn * n].rearrange("p (k n) -> p k n", k=kn)

    def load_upto(self, sp, last):
        while self.n_loaded <= min(last, self.last()):
            i = self.n_loaded
            if i >= self.RAW:
                sp.wait_ge(self.split, i - self.RAW + 1)
            raw = self.view(self.raw, i, self.RAW)
            for k, c0, n, src in self.tiles[i][2]:
                dst = raw[:, :, :] if k is None else raw[:, k, c0:c0 + n]
                if k is not None and len(src.shape) == 3:
                    dst = dst.rearrange("p (h c) -> p h c", h=src.shape[1])
                sp.dma_start(dst, src).then_inc(self.loaded[i % self.RAW], 16)
            self.n_loaded += 1

    def round_upto(self, act, last):
        while self.n_rounded <= min(last, self.last()):
            i = self.n_rounded
            act.wait_ge(self.loaded[i % self.RAW], self.need[i])
            if i >= self.SPLIT:
                act.wait_ge(*self.used_at[i - self.SPLIT])
            act.activation(self.view(self.hi, i, self.SPLIT), self.view(self.raw, i, self.RAW),
                           ACT.Copy).then_inc(self.rounded, 1)
            self.n_rounded += 1

    def split_upto(self, pool, last):
        while self.n_split <= min(last, self.last()):
            i = self.n_split
            pool.wait_ge(self.rounded, i + 1)
            pool.tensor_tensor(self.view(self.lo, i, self.SPLIT), self.view(self.raw, i, self.RAW),
                               self.view(self.hi, i, self.SPLIT).bitcast(F32),
                               ALU.subtract).then_inc(self.split, 1)
            self.n_split += 1

    def take(self, pe, chunks, cols):
        i = self.n_taken
        assert self.tiles[i][:2] == (chunks, cols), (i, self.tiles[i][:2], chunks, cols)
        pe.wait_ge(self.split, i + 1)
        self.n_taken += 1
        return self.view(self.hi, i, self.SPLIT), self.view(self.lo, i, self.SPLIT)

    def release(self, ins, sem=None, value=None):
        if sem is None:
            self.n_used += 1
            ins.then_inc(self.used, 1)
            sem, value = self.used, self.n_used
        self.used_at.append((sem, value))


class Core:

    def __init__(self, nc, ctx):
        self.nc = nc
        self.w = Weights(nc, ctx)
        self.bank = [ctx.enter_context(nc.psum_tensor(f"bank{i}", [P, BANK], F32))
                     for i in range(BANKS)]
        sem = lambda name: ctx.enter_context(nc.semaphore(name))
        self.ready = sem("product_ready")
        self.freed = sem("product_read")
        self.groups = 0
        self.xh = ctx.enter_context(nc.sbuf_tensor("columns_rounded", [P, DC, SEQ], F32R))
        self.xl = ctx.enter_context(nc.sbuf_tensor("columns_remainder", [P, DC, SEQ], F32R))
        self.sems = []
        self.n_phase = 0

    def sem(self, name):
        s = self.nc.alloc_semaphore(name=f"{name}_{self.n_phase}")
        self.sems.append(s)
        return s

    def recycle(self):
        self.nc.clear_and_free_semaphores(self.sems)
        self.sems = []
        self.nc.all_engine_barrier()

    def bank_of(self, g):
        return self.bank[self.first_bank + g % (BANKS - self.first_bank)]

    def wait_bank(self, pe, g):
        n = BANKS - self.first_bank
        if g >= n:
            pe.wait_ge(self.freed, self.groups_at_start + g - n + 1)

    def products_by_rows(self, pe, g, *args, **kw):
        for g in self.product_steps(pe, g, *args, **kw):
            pass
        return g

    def product_steps(self, pe, g, k_chunks, col_tiles, rows=TB, per=4, x0=0):
        for c0, n in col_tiles:
            for k0 in range(0, k_chunks, per):
                kn = min(per, k_chunks - k0)
                hi, lo = self.w.take(pe, kn, n)
                final = k0 + kn == k_chunks
                for tb in range(rows):
                    if k0 == 0:
                        self.wait_bank(pe, g + tb)
                    for k in range(kn):
                        xs = (slice(None), x0 + k0 + k, slice(tb * P, (tb + 1) * P))
                        for a, b in ((self.xh, hi), (self.xh, lo), (self.xl, hi)):
                            last = k == kn - 1 and b is hi and a is self.xl
                            ins = pe.matmul(self.bank_of(g + tb)[:, 0:n], a[xs], b[:, k, :],
                                            start=(k0 + k == 0 and b is hi and a is self.xh),
                                            stop=(final and last))
                    if final:
                        ins.then_inc(self.ready, 1)
                        self.groups += 1
                    if tb < rows - 1:
                        yield g
                if final:
                    self.w.release(ins, self.ready, self.groups)
                    g += rows
                else:
                    self.w.release(ins)
                yield g

    def copy_steps(self, act, g, k_chunks, jobs, rows=TB, per=4):
        done = 0
        parts = -(-k_chunks // per)
        late = None
        for target, tiles in jobs:
            at = 0
            for _, n in tiles:
                for k in range(parts):
                    self.w.round_upto(act, self.tile0 + done + 2)
                    for tb in range(rows):
                        if late is not None:
                            self.copy_group(act, *late)
                            late = None
                        if k == parts - 1:
                            late = (g, target[:, tb, at:at + n], n)
                            g += 1
                        yield
                    done += 1
                at += n
        self.copy_group(act, *late)
        self.w.round_upto(act, self.ahead(done))

    def copy_group(self, act, g, dst, n):
        self.wait_group(act, g)
        act.activation(dst, self.bank_of(g)[:, 0:n], ACT.Copy).then_inc(self.freed, 1)

    def products_by_columns(self, pe, g, k_chunks, cols, x0=0):
        hi, lo = self.w.take(pe, k_chunks, cols)
        for c in range(cols // P):
            self.wait_bank(pe, g)
            for k in range(k_chunks):
                ws = (slice(None), k, slice(c * P, (c + 1) * P))
                for n, (a, b) in enumerate(((hi, self.xh), (lo, self.xh), (hi, self.xl))):
                    ins = pe.matmul(self.bank_of(g)[:, :], a[ws], b[:, x0 + k, :],
                                    start=(k == 0 and n == 0), stop=(k == k_chunks - 1 and n == 2))
            ins.then_inc(self.ready, 1)
            self.groups += 1
            g += 1
        self.w.release(ins, self.ready, self.groups)
        return g

    def stage(self, ctx, first_bank=0):
        self.first_bank = first_bank
        self.n_phase += 1
        self.groups_at_start = self.groups
        self.tile0 = self.w.n_taken
        return ctx.enter_context(self.nc.Block())

    def ahead(self, n_tiles):
        return self.tile0 + n_tiles - 1 + self.w.SPLIT - 1

    def stream(self, block, n_tiles, moves=()):
        last = self.ahead(n_tiles)
        moved = self.sem("moved") if moves else None

        @block.sync
        def _(sp):
            for dst, src in moves:
                sp.dma_start(dst, src).then_inc(moved, 16)
            self.w.load_upto(sp, last + self.w.RAW)
            if moves:
                sp.wait_ge(moved, 16 * len(moves))

        @block.gpsimd
        def _(pool):
            self.w.split_upto(pool, last)

    def wait_group(self, eng, g):
        eng.wait_ge(self.ready, self.groups_at_start + g + 1)


def paced(steps, rounds):
    for _ in steps:
        for _round in range(rounds):
            yield


def together(*generators):
    running = list(generators)
    while running:
        running = [g for g in running if next(g, running) is not running]
        yield


class Turn:

    def __init__(self, eng, sem):
        self.eng, self.sem, self.n = eng, sem, 0

    def __call__(self, ins):
        ins.then_inc(self.sem, 1)
        self.n += 1
        return ins

    def wait(self):
        if self.n:
            self.eng.wait_ge(self.sem, self.n)


def transfer(core, block, moves):
    if not moves:
        return
    moved = core.sem("moved")

    @block.sync
    def _(sp):
        for dst, src in moves:
            sp.dma_start(dst, src).then_inc(moved, 16)
        sp.wait_ge(moved, 16 * len(moves))


def to_columns(core, src, gain=None, rows=TB, norm=None, width=D, x0=0, moves=(),
               by_head=False):
    nc, chunks = core.nc, width // P
    with ExitStack() as ctx:
        squared, mean, rooted, scaled = (core.sem(n) for n in ("squared", "mean", "rooted", "scaled"))
        turned, rounded, remainder = (core.sem(n) for n in ("turned", "rounded", "remainder"))
        block = core.stage(ctx)
        transfer(core, block, moves)
        if norm is not None:
            scratch, small = norm
            ss, rms, rstd = small[:, 0:rows], small[:, 4:4 + rows], small[:, 8:8 + rows]
            y = scratch
        else:
            y = src

        @block.tensor
        def _(pe):
            for c in range(chunks):
                for tb in range(rows):
                    if norm is not None and c == 0:
                        pe.wait_ge(scaled, tb + 1)
                    rows_in = y[:, c, tb * P:(tb + 1) * P] if by_head else y[:, tb, c * P:(c + 1) * P]
                    ins = pe.transpose(core.bank[c][:, tb * P:(tb + 1) * P], rows_in,
                                       core.ident[:, :])
                ins.then_inc(turned, 1)

        @block.scalar
        def _(act):
            if norm is not None:
                for tb in range(rows):
                    act.activation(scratch[:, tb, 0:width], src[:, tb, :], ACT.Square,
                                   accum_out=ss[:, tb:tb + 1]).then_inc(squared, 1)
                act.wait_ge(mean, 1)
                act.activation(rms, ss, ACT.Sqrt).then_inc(rooted, 1)
            for c in range(chunks):
                act.wait_ge(turned, c + 1)
                act.activation(core.xh[:, x0 + c, 0:rows * P], core.bank[c][:, 0:rows * P], ACT.Copy,
                               scale=1.0 if gain is None else gain[:, c:c + 1]).then_inc(rounded, 1)

        @block.vector
        def _(dve):
            if norm is not None:
                dve.wait_ge(squared, rows)
                dve.tensor_scalar(ss, ss, 1.0 / width, EPS, ALU.mult, ALU.add).then_inc(mean, 1)
                dve.wait_ge(rooted, 1)
                dve.reciprocal(rstd, rms).then_inc(mean, 1)
                dve.wait_ge(mean, 2)
                for tb in range(rows):
                    dve.tensor_scalar(y[:, tb, 0:width], src[:, tb, :], rstd[:, tb:tb + 1], None,
                                      ALU.mult).then_inc(scaled, 1)
            for c in range(chunks):
                dve.wait_ge(rounded, c + 1)
                hi = core.xh[:, x0 + c, 0:rows * P].bitcast(F32)
                lo = core.xl[:, x0 + c, 0:rows * P]
                if gain is None:
                    dve.tensor_tensor(lo, core.bank[c][:, 0:rows * P], hi,
                                      ALU.subtract).then_inc(remainder, 1)
                else:
                    dve.scalar_tensor_tensor(lo, core.bank[c][:, 0:rows * P], gain[:, c:c + 1], hi,
                                             ALU.mult, ALU.subtract).then_inc(remainder, 1)


def turn_heads(core, moves, gains=None, transfers=()):
    with ExitStack() as ctx:
        turned, by_act, by_dve = (core.sem(n) for n in ("turned", "copied_act", "copied_dve"))
        block = core.stage(ctx)
        transfer(core, block, transfers)

        @block.tensor
        def _(pe):
            for g, (src, blocks, _) in enumerate(moves):
                if g >= BANKS:
                    pe.wait_ge((by_act, by_dve)[g % 2], (g - BANKS) // 2 + 1)
                for tb in range(blocks):
                    ins = pe.transpose(core.bank[g % BANKS][:, tb * P:(tb + 1) * P], src(tb),
                                       core.ident[:, :])
                ins.then_inc(turned, 1)

        @block.scalar
        def _(act):
            for g in range(0, len(moves), 2):
                act.wait_ge(turned, g + 1)
                act.activation(moves[g][2], core.bank[g % BANKS][:, 0:moves[g][1] * P], ACT.Copy,
                               scale=1.0 if gains is None else gains[g]).then_inc(by_act, 1)

        @block.vector
        def _(dve):
            for g in range(1, len(moves), 2):
                dve.wait_ge(turned, g + 1)
                dve.tensor_scalar(moves[g][2], core.bank[g % BANKS][:, 0:moves[g][1] * P],
                                  1.0 if gains is None else gains[g], None, ALU.mult)\
                   .then_inc(by_dve, 1)


def attention(core, units, scale, buf, beside=None, transfers=()):
    probs, turned_sb, small = buf
    S_RING, T_RING = (3, 2) if beside is None else (2, 1)
    P_SLOTS, T_SLOTS = probs.shape[1], turned_sb.shape[1]
    n = len(units)
    S = core.bank[0:S_RING]
    T = core.bank[S_RING:S_RING + T_RING]
    O = core.bank[S_RING + T_RING:S_RING + 2 * T_RING]
    peak, sums = small[:, 0:n], small[:, n:2 * n]
    with ExitStack() as ctx:
        names = ("scores_ready", "biased", "peak_ready", "weights_ready", "turned_ready",
                 "turned_copied", "values_ready", "finished", "finish_step")
        (scores_ready, biased, peak_ready, weights_ready, turned_ready,
         turned_copied, values_ready, finished, finish_step) = (core.sem(x) for x in names)
        block = core.stage(ctx, first_bank=0 if beside is None else 4)
        more = beside or {}
        if "tiles" not in more:
            transfer(core, block, transfers)

        @block.tensor
        def _(pe):
            other = more["tensor"](pe) if "tensor" in more else iter(())
            for i in range(n + 3):
                if i < n:
                    pairs, keys = units[i][:2]
                    if i >= S_RING:
                        pe.wait_ge(biased, i - S_RING + 1)
                    for m, (q, k) in enumerate(pairs):
                        ins = pe.matmul(S[i % S_RING][:, 0:keys], q, k, start=(m == 0),
                                        stop=(m == len(pairs) - 1))
                    ins.then_inc(scores_ready, 1)
                j = i - 2
                if 0 <= j < n:
                    pe.wait_ge(weights_ready, j + 1)
                    if j >= T_RING:
                        pe.wait_ge(turned_copied, j - T_RING + 1)
                    for c in range(units[j][1] // P):
                        ins = pe.transpose(T[j % T_RING][:, c * P:(c + 1) * P],
                                           probs[:, j % P_SLOTS, c * P:(c + 1) * P], core.ident[:, :])
                    ins.then_inc(turned_ready, 1)
                j = i - 3
                if 0 <= j < n:
                    _, keys, _, values, width, _ = units[j]
                    pe.wait_ge(turned_copied, j + 1)
                    if j >= T_RING:
                        pe.wait_ge(finished, j - T_RING + 1)
                    for c in range(keys // P):
                        ins = pe.matmul(O[j % T_RING][:, 0:width],
                                        turned_sb[:, j % T_SLOTS, c * P:(c + 1) * P], values(c),
                                        start=(c == 0), stop=(c == keys // P - 1))
                    ins.then_inc(values_ready, 1)
                next(other, None)
            for _step in other:
                pass

        if "tiles" in more:
            core.stream(block, more["tiles"], moves=transfers)

        @block.vector
        def _(dve):
            turn = Turn(dve, finish_step)
            other = more["vector"](dve) if "vector" in more else iter(())
            for i in range(n + 3):
                if i < n:
                    keys, bias = units[i][1:3]
                    dve.wait_ge(scores_ready, i + 1)
                    if i >= P_SLOTS:
                        dve.wait_ge(turned_ready, i - P_SLOTS + 1)
                    dve.tensor_tensor_reduce(
                        out=probs[:, i % P_SLOTS, 0:keys], in0=S[i % S_RING][:, 0:keys], in1=bias,
                        scale=scale(i) if callable(scale) else scale, scalar=-3.0e38,
                        op0=ALU.add, op1=ALU.max, accum_out=peak[:, i:i + 1]).then_inc(biased, 1)
                    dve.wait_ge(biased, i + 1)
                    dve.tensor_scalar(peak[:, i:i + 1], peak[:, i:i + 1], -1.0, None,
                                      ALU.mult).then_inc(peak_ready, 1)
                j = i - 3
                if 0 <= j < n:
                    dve.wait_ge(values_ready, j + 1)
                    if j:
                        dve.wait_ge(finished, j)
                    ins = units[j][5](dve, turn, j, sums[:, j:j + 1],
                                      O[j % T_RING][:, 0:units[j][4]])
                    ins.then_inc(finished, 1)
                next(other, None)
            for _step in other:
                pass

        @block.scalar
        def _(act):
            other = more["scalar"](act) if "scalar" in more else iter(())
            for i in range(n + 3):
                if i < n:
                    keys = units[i][1]
                    act.wait_ge(peak_ready, i + 1)
                    p = probs[:, i % P_SLOTS, 0:keys]
                    act.activation(p, p, ACT.Exp, bias=peak[:, i:i + 1],
                                   accum_out=sums[:, i:i + 1]).then_inc(weights_ready, 1)
                j = i - 2
                if 0 <= j < n:
                    keys = units[j][1]
                    act.wait_ge(turned_ready, j + 1)
                    if j >= T_SLOTS:
                        act.wait_ge(values_ready, j - T_SLOTS + 1)
                    act.activation(turned_sb[:, j % T_SLOTS, 0:keys], T[j % T_RING][:, 0:keys],
                                   ACT.Copy).then_inc(turned_copied, 1)
                next(other, None)
            for _step in other:
                pass


def add_product(core, n_tiles, k_chunks, target, col_tiles=HALVES):
    with ExitStack() as ctx:
        block = core.stage(ctx)

        @block.tensor
        def _(pe):
            core.products_by_rows(pe, 0, k_chunks, col_tiles)

        core.stream(block, n_tiles)

        @block.scalar
        def _(act):
            core.w.round_upto(act, core.ahead(n_tiles))

        @block.vector
        def _(dve):
            g = 0
            for c0, n in col_tiles:
                for tb in range(TB):
                    core.wait_group(dve, g)
                    t = target[:, tb, c0:c0 + n]
                    dve.tensor_tensor(t, core.bank[g % BANKS][:, 0:n], t,
                                      ALU.add).then_inc(core.freed, 1)
                    g += 1


def head_norm(core, x, heads, squares, small, factor=1.0, gain=None, rows=TB):
    width = x.shape[2] // heads
    n = rows * heads
    mean, rms, rstd = small[:, 0:n], small[:, 32:32 + n], small[:, 64:64 + n]
    by_head = lambda a: a.rearrange("p t (h d) -> p t h d", h=heads)
    with ExitStack() as ctx:
        squared, meaned, rooted, normed = (core.sem(s) for s in ("squared", "mean", "rooted", "normed"))
        block = core.stage(ctx)

        @block.scalar
        def _(act):
            for tb in range(rows):
                act.activation(squares[:, tb, :], x[:, tb, :], ACT.Square).then_inc(squared, 1)
            act.wait_ge(meaned, rows + 1)
            act.activation(rms, mean, ACT.Sqrt).then_inc(rooted, 1)

        @block.vector
        def _(dve):
            for tb in range(rows):
                dve.wait_ge(squared, tb + 1)
                dve.tensor_reduce(mean[:, tb * heads:(tb + 1) * heads],
                                  squares[:, tb, :].rearrange("p (h d) -> p h d", h=heads),
                                  AX.X, ALU.add).then_inc(meaned, 1)
            dve.wait_ge(meaned, rows)
            dve.tensor_scalar(mean, mean, 1.0 / width, EPS, ALU.mult, ALU.add).then_inc(meaned, 1)
            dve.wait_ge(rooted, 1)
            dve.reciprocal(rstd, rms).then_inc(normed, 1)
            dve.wait_ge(normed, 1)
            done = 1
            for tb in range(rows):
                xt = x[:, tb, :].rearrange("p (h d) -> p h d", h=heads)
                r = rstd[:, tb * heads:(tb + 1) * heads].unsqueeze(2).to_broadcast([P, heads, width])
                dve.tensor_tensor(xt, xt, r, ALU.mult).then_inc(normed, 1)
                done += 1
                dve.wait_ge(normed, done)
                if gain is not None:
                    g = gain.unsqueeze(1).to_broadcast([P, heads, width])
                    dve.tensor_tensor(xt, xt, g, ALU.mult).then_inc(normed, 1)
                    done += 1
                if factor != 1.0:
                    dve.tensor_scalar(xt, xt, factor, None, ALU.mult).then_inc(normed, 1)
                    done += 1


def rope(dve, turn, x, heads, tables, t1, t2, rows=TB):
    ca, cb, sa, sb = tables
    v = x.rearrange("p t (h d) -> p t h d", h=heads)
    x1, x2 = v[:, :, :, 0:HALF], v[:, :, :, HALF:HEAD]
    wide = lambda a: a.unsqueeze(2).to_broadcast([P, rows, heads, HALF])
    t1 = t1[:, 0:rows * heads * HALF].rearrange("p (t h d) -> p t h d", t=rows, h=heads)
    t2 = t2[:, 0:rows * heads * HALF].rearrange("p (t h d) -> p t h d", t=rows, h=heads)
    turn.wait()
    turn(dve.tensor_tensor(t1, x2, wide(sb), ALU.mult))
    turn(dve.tensor_tensor(t2, x1, wide(sa), ALU.mult))
    turn(dve.tensor_tensor(x1, x1, wide(ca), ALU.mult))
    turn(dve.tensor_tensor(x2, x2, wide(cb), ALU.mult))
    turn.wait()
    turn(dve.tensor_tensor(x1, x1, t1, ALU.subtract))
    turn(dve.tensor_tensor(x2, x2, t2, ALU.add))
    turn.wait()


def plan_weights(w, t):
    w.plan_rows(t["w_in"], DC, IN_TILES)
    for name in ("w_xk", "w_xv", "w_out", "w_xq", "w_xo"):
        w.plan_rows(t[name], DC, HALVES)
    for c in range(FC // 2):
        for c0 in (c * 2 * P, D_FF + c * 2 * P):
            w.plan_rows(t["w_ffn_in"], DC, ((c0, 2 * P),), per=DC)
    for k0 in range(0, FC, 4):
        w.plan_rows(t["w_ffn_out"][k0 * P:min(FC, k0 + 4) * P, :], min(4, FC - k0), HALVES)
    w.plan_rows(t["w_in_2"], DC, [(c, 2 * P) for c in range(HQ, HI, 2 * P)], per=DC)
    w.plan_rows(t["w_in_2"], DC, ((HI, 512), (HI + 512, 512)))
    w.plan_rows(t["w_in_2"], DC, ((HZ, 512), (HZ + 512, 512)))
    w.plan_rows(t["w_in_2"], DC, ((CQ, 384), (CKV, 320)))
    uq = t["w_uq_2"].rearrange("(k p) (h c) -> p k h c", p=P, c=NOPE + PE_DIM)
    for h0 in (0, 4):
        w.plan(3, 4 * NOPE, [(k, 0, 4 * NOPE, uq[:, k, h0:h0 + 4, 0:NOPE]) for k in range(3)])
    w.plan(3, 8 * PE_DIM, [(k, 0, 8 * PE_DIM, uq[:, k, :, NOPE:NOPE + PE_DIM]) for k in range(3)])
    ukv = t["w_ukv_2"].rearrange("(k p) (h c) -> p k h c", p=P, c=NOPE + V_DIM)
    w.plan(2, 8 * NOPE, [(k, 0, 8 * NOPE, ukv[:, k, :, 0:NOPE]) for k in range(2)])
    for h0 in (0, 4):
        w.plan(2, 4 * V_DIM, [(k, 0, 4 * V_DIM, ukv[:, k, h0:h0 + 4, NOPE:NOPE + V_DIM])
                              for k in range(2)])
    w.plan_rows(t["w_in_2"], DC, ((MZ, 512), (MZ + 512, 512)))
    w.plan_rows(t["w_in_2"], DC, [(GLOG + 512 * c, 512) for c in range(4)])
    for name in ("w_proj_a_2", "w_proj_b_2", "w_out_2"):
        w.plan_rows(t[name], DC, HALVES)


def two_blocks(nc, t, out, x_saved, y_saved, stop=None):
    ctx = ExitStack()
    with ctx:
        sb = lambda name, shape, dt=F32: ctx.enter_context(nc.sbuf_tensor(name, shape, dt))
        core = Core(nc, ctx)
        plan_weights(core.w, t)
        ident = core.ident = sb("identity", [P, P])
        causal = sb("causal", [P, BANK])
        mask32 = sb("chunk_mask", [P, P])
        columns = sb("column_vectors", [P, 160])
        trig = sb("trig", [P, 2, 2 * TB * HALF])
        small = sb("small", [P, 160])
        lower = sb("lower_bound", [P, 2 * HG_HEADS])
        neg_lambda = sb("neg_lambda", [P, 4])
        decay = sb("decay", [P, HG_HEADS, SEQ // HG_CHUNK])
        arena = sb("arena", [P, 24704])
        out_stored = ctx.enter_context(nc.semaphore("out_stored"))

        def view(at, *dims):
            n = 1
            for d in dims:
                n *= d
            a = arena[:, at:at + n]
            if len(dims) == 2:
                return a.rearrange("p (a b) -> p a b", a=dims[0])
            return a

        g_mix, g_xattn, g_mem, g_ffn, g_second = (columns[:, 8 * i:8 * i + 8] for i in range(5))
        conv_w, conv_b = columns[:, 40:106], columns[:, 106:128]
        q_a_gain, kv_a_gain, lb_logits = columns[:, 128:131], columns[:, 131:133], columns[:, 133:149]
        hg_gain, xqk_gain = columns[:, 153:154], columns[:, 154:156]

        def by_chunk(name):
            return t[name].rearrange("l (c p) -> (l c) p", p=P)

        def over_partitions(v):
            return v[0, :].partition_broadcast(P)

        x = view(0, TB, D)
        spare = view(4096, TB, D)
        rows_v = view(8192, 2, P)
        position = arena[:, 8448:8456]
        positions_i = arena[:, 8456:8464].bitcast(I32)
        inv_freq = arena[:, 8464:8496]
        angle = view(8704, 2, 2 * TB * HALF)
        turns = view(9216, 2, 2 * TB * HALF)
        gains = view(10240, 4, HEAD)
        lams = view(10496, 4, HEAD)
        tables = arena[:, 14336:16384].rearrange("p (g k n) -> p g k n", g=4, k=4)
        with ExitStack() as c:
            loaded, made, step, ready_ang = (core.sem(s) for s in ("loaded", "made", "step", "angles"))
            x_in, turned, copied, sined = (core.sem(s) for s in ("x_in", "turned", "copied", "sined"))
            lam_exp, freq_set = core.sem("lam_exp"), core.sem("freq_set")
            block = core.stage(c)
            N_LOADS = 22

            @block.sync
            def _(sp):
                core.w.load_upto(sp, 1)
                sp.wait_ge(made, 1)
                at = 0
                for name, src in (("g_mix", by_chunk("g_mix")), ("g_xattn", by_chunk("g_xattn")),
                                  ("g_mem", by_chunk("g_mem")), ("g_ffn", by_chunk("g_ffn")),
                                  ("norm_g_2", by_chunk("norm_g_2")),
                                  ("conv_w", t["conv_w"].rearrange("l j (c p) -> (l j c) p", p=P)),
                                  ("conv_b", by_chunk("conv_b"))):
                    n = src.shape[0]
                    sp.dma_start(rows_v[at:at + n, 0, :], src).then_inc(loaded, 16)
                    at += n
                at = 0
                for name in ("q_a_g_2", "kv_a_g_2", "lb_logits_2", "g_xq", "g_xk", "hg_norm_g_2"):
                    src = by_chunk(name)
                    sp.dma_start(rows_v[at:at + src.shape[0], 1, :], src).then_inc(loaded, 16)
                    at += src.shape[0]
                core.w.load_upto(sp, core.w.SPLIT - 1 + core.w.RAW)

            @block.gpsimd
            def _(pool):
                pool.memset(rows_v, 0.0).then_inc(made, 1)
                pool.memset(ident[:, :], 0.0).then_inc(made, 1)
                pool.memset(causal[:, :], 0.0).then_inc(made, 1)
                pool.memset(mask32[:, :], 1.0).then_inc(made, 1)
                pool.wait_ge(made, 4)
                pool.affine_select(out=ident[:, :], in_=ident[:, :], compare_op=ALU.not_equal, fill=1.0,
                                   base=0, pattern=[[-1, P]], channel_multiplier=1).then_inc(made, 1)
                diagonal = causal[:, 3 * P:4 * P]
                pool.affine_select(out=diagonal, in_=diagonal, compare_op=ALU.is_ge, fill=NEG,
                                   base=0, pattern=[[-1, P]], channel_multiplier=1).then_inc(made, 1)
                pool.affine_select(out=mask32[:, :], in_=mask32[:, :], compare_op=ALU.is_ge, fill=0.0,
                                   base=0, pattern=[[1, P]], channel_multiplier=-1).then_inc(made, 1)
                pool.wait_ge(made, 7)
                m4 = mask32[:, :].rearrange("p (c s) -> p c s", s=HG_CHUNK)
                pool.affine_select(out=m4, in_=m4, compare_op=ALU.is_ge, fill=0.0, base=0,
                                   pattern=[[-HG_CHUNK, P // HG_CHUNK], [0, HG_CHUNK]],
                                   channel_multiplier=1).then_inc(made, 1)
                pool.iota(positions_i[:, 4:8], [[P, TB]], base=0, channel_multiplier=1)\
                    .then_inc(made, 1)
                for i in range(HALF):
                    pool.memset(inv_freq[:, i:i + 1], 10000.0 ** (-2.0 * i / HEAD)).then_inc(freq_set, 1)
                core.w.split_upto(pool, core.w.SPLIT - 1)

            @block.scalar
            def _(act):
                act.dma_start(x, t["x"].rearrange("l (t p) d -> p (l t) d", p=P)).then_inc(x_in, 16)
                act.dma_start(positions_i[:, 0:4], t["positions"].rearrange("l (t p) -> p (l t)", p=P),
                              allow_slow_non_contiguous=True)\
                   .then_inc(loaded, 16)
                for i, name in enumerate(("g_qa", "g_ka", "g_qb", "g_kb")):
                    act.dma_start(gains[:, i, :], over_partitions(t[name])).then_inc(loaded, 16)
                for i, name in enumerate(("lam_q1", "lam_k1", "lam_q2", "lam_k2")):
                    act.dma_start(lams[:, i, :], over_partitions(t[name])).then_inc(loaded, 16)
                core.w.round_upto(act, core.w.SPLIT - 1)
                act.wait_ge(ready_ang, 1)
                act.activation(trig[:, :, :], angle, ACT.Sin).then_inc(sined, 1)
                act.wait_ge(lam_exp, 1)
                act.activation(neg_lambda[:, 0:2], neg_lambda[:, 0:2], ACT.Exp).then_inc(sined, 1)
                act.activation(lb_logits, lb_logits, ACT.Exp).then_inc(sined, 1)
                act.wait_ge(x_in, 16)

            @block.tensor
            def _(pe):
                pe.wait_ge(made, 5)
                pe.wait_ge(loaded, 16 * N_LOADS)
                pe.transpose(core.bank[0][:, 0:P], rows_v[:, 0, :], ident[:, :])
                pe.transpose(core.bank[0][:, P:2 * P], rows_v[:, 1, :], ident[:, :]).then_inc(turned, 1)

            @block.vector
            def _(dve):
                turn = Turn(dve, step)
                dve.wait_ge(loaded, 16 * N_LOADS)
                dve.wait_ge(made, 9)
                dve.wait_ge(freq_set, HALF)
                turn(dve.tensor_copy(position, positions_i))
                turn.wait()
                ang = angle[:, 0, :].rearrange("p (t f) -> p t f", f=HALF)
                turn(dve.tensor_tensor(ang, position.unsqueeze(2).to_broadcast([P, 2 * TB, HALF]),
                                       inv_freq.unsqueeze(1).to_broadcast([P, 2 * TB, HALF]), ALU.mult))
                turn.wait()
                magic = 1.5 * 2.0 ** 23
                turn(dve.tensor_scalar(turns[:, 0, :], angle[:, 0, :], 0.5 / math.pi, None, ALU.mult))
                turn(dve.tensor_scalar(turns[:, 1, :], angle[:, 0, :], 0.5 / math.pi, 0.25,
                                       ALU.mult, ALU.add))
                turn(dve.tensor_copy(angle[:, 1, :], angle[:, 0, :]))
                turn.wait()
                turn(dve.tensor_scalar(turns, turns, magic, None, ALU.add))
                turn.wait()
                turn(dve.tensor_scalar(turns, turns, -magic, None, ALU.add))
                turn.wait()
                part1 = 6.28125
                part2 = 0.0019350051879882812
                part3 = 2.0 * math.pi - part1 - part2
                for part in (part1, part2, part3):
                    turn(dve.scalar_tensor_tensor(angle, turns, -part, angle, ALU.mult, ALU.add))
                    turn.wait()
                turn(dve.tensor_scalar(angle[:, 1, :], angle[:, 1, :], math.pi / 2, None, ALU.add))
                turn.wait()
                dve.tensor_scalar(angle, angle, 3.1415925, -3.1415925, ALU.min, ALU.max)\
                   .then_inc(ready_ang, 1)
                for i in range(2):
                    turn(dve.tensor_tensor(lams[:, 2 * i, :], lams[:, 2 * i, :], lams[:, 2 * i + 1, :],
                                           ALU.mult))
                    turn.wait()
                    turn(dve.tensor_reduce(neg_lambda[:, i:i + 1], lams[:, 2 * i, :], AX.X, ALU.add))
                dve.wait_ge(turned, 1)
                turn(dve.tensor_copy(columns[:, 0:154], core.bank[0][:, 0:154]))
                turn.wait()
                turn(dve.tensor_tensor(xqk_gain, columns[:, 149:151], columns[:, 151:153], ALU.mult))
                l0, l1 = lb_logits[:, 0:8], lb_logits[:, 8:16]
                top, total = small[:, 0:8], small[:, 8:16]
                turn(dve.tensor_tensor(top, l0, l1, ALU.max))
                turn.wait()
                turn(dve.tensor_tensor(l0, l0, top, ALU.subtract))
                dve.tensor_tensor(l1, l1, top, ALU.subtract).then_inc(lam_exp, 1)
                dve.wait_ge(sined, 3)
                turn(dve.tensor_tensor(neg_lambda[:, 2:3], neg_lambda[:, 1:2], neg_lambda[:, 0:1],
                                       ALU.subtract))
                turn(dve.tensor_tensor(total, l0, l1, ALU.add))
                turn.wait()
                turn(dve.tensor_scalar(neg_lambda[:, 2:3], neg_lambda[:, 2:3], -LAMBDA_INIT, None, ALU.add))
                turn(dve.reciprocal(total, total))
                turn.wait()
                turn(dve.tensor_tensor(lower[:, 0:8], l0, total, ALU.mult))
                turn(dve.tensor_tensor(lower[:, 8:16], l1, total, ALU.mult))
                sin1 = trig[:, 0, 0:TB * HALF].rearrange("p (t f) -> p t f", f=HALF)
                cos1 = trig[:, 1, 0:TB * HALF].rearrange("p (t f) -> p t f", f=HALF)
                for i in range(4):
                    for k, (tab, half) in enumerate(((cos1, 0), (cos1, 1), (sin1, 0), (sin1, 1))):
                        g = gains[:, i, half * HALF:(half + 1) * HALF].unsqueeze(1)\
                            .to_broadcast([P, TB, HALF])
                        turn(dve.tensor_tensor(tables[:, i, k, :].rearrange("p (t f) -> p t f", f=HALF),
                                               tab, g, ALU.mult))

        def table_views(i):
            return [tables[:, i, k, :].rearrange("p (t f) -> p t f", f=HALF) for k in range(4)]

        def plain_tables(which):
            s, c_ = (trig[:, k, which * TB * HALF:(which + 1) * TB * HALF]
                     .rearrange("p (t f) -> p t f", f=HALF) for k in (0, 1))
            return (c_, c_, s, s)

        to_columns(core, x, g_mix, norm=(spare, small))
        qa, mixed, qb, kb, vb = (view(at, TB, n) for at, n in
                                 ((0, 512), (2048, 452), (4096, 512), (6144, 512), (8192, 512)))
        squares = view(10240, TB, 512)
        t1, t2 = view(12288, 1024), view(13312, 1024)
        targets = (qa, mixed, qb, kb, vb)
        normed_heads = {0: (qa, 8), 1: (mixed[:, :, 0:HEAD], 1), 2: (qb, 8), 3: (kb, 8)}
        with ExitStack() as c:
            squared, meaned, rooted, step = (core.sem(s) for s in ("squared", "mean", "rooted", "step"))
            block = core.stage(c)

            @block.tensor
            def _(pe):
                core.products_by_rows(pe, 0, DC, IN_TILES)

            core.stream(block, 10)

            @block.scalar
            def _(act):
                for j, target in enumerate(targets):
                    core.w.round_upto(act, core.tile0 + 2 * j + 3)
                    for tb in range(TB):
                        core.wait_group(act, TB * j + tb)
                        act.activation(target[:, tb, :], core.bank[(TB * j + tb) % BANKS]
                                       [:, 0:IN_TILES[j][1]], ACT.Copy).then_inc(core.freed, 1)
                    if j in normed_heads:
                        src, heads = normed_heads[j]
                        act.wait_ge(core.freed, core.groups_at_start + TB * (j + 1))
                        if j:
                            act.wait_ge(meaned, 2 * j)
                        act.activation(squares[:, :, 0:heads * HEAD], src, ACT.Square)\
                           .then_inc(squared, 1)
                    if j - 1 in normed_heads:
                        n, at = TB * normed_heads[j - 1][1], (j - 1) % 2 * 32
                        act.wait_ge(meaned, 2 * j)
                        act.activation(small[:, 64 + at:64 + at + n], small[:, at:at + n], ACT.Sqrt)\
                           .then_inc(rooted, 1)
                core.w.round_upto(act, core.ahead(10))

            @block.vector
            def _(dve):
                turn = Turn(dve, step)

                def finish(j):
                    src, heads = normed_heads[j]
                    n, at = TB * heads, j % 2 * 32
                    dve.wait_ge(rooted, j + 1)
                    turn(dve.reciprocal(small[:, 128:128 + n], small[:, 64 + at:64 + at + n]))
                    turn.wait()
                    r = small[:, 128:128 + n].rearrange("p (t h) -> p t h", t=TB)
                    v = src.rearrange("p t (h d) -> p t h d", h=heads)
                    turn(dve.tensor_tensor(v, v, r.unsqueeze(3).to_broadcast([P, TB, heads, HEAD]),
                                           ALU.mult))
                    rope(dve, turn, src, heads, table_views(j), t1, t2)
                    if j == 1:
                        rope(dve, turn, mixed[:, :, 2 * HEAD:7 * HEAD], 5, plain_tables(0), t1, t2)

                for j in range(4):
                    src, heads = normed_heads[j]
                    mean = small[:, j % 2 * 32:j % 2 * 32 + TB * heads]
                    dve.wait_ge(squared, j + 1)
                    dve.tensor_reduce(mean, squares[:, :, 0:heads * HEAD]
                                      .rearrange("p t (h d) -> p t h d", h=heads), AX.X, ALU.add)\
                       .then_inc(meaned, 1)
                    dve.wait_ge(meaned, 2 * j + 1)
                    dve.tensor_scalar(mean, mean, 1.0 / HEAD, EPS, ALU.mult, ALU.add)\
                       .then_inc(meaned, 1)
                    if j == 0:
                        continue
                    finish(j - 1)
                finish(3)
                for src, dst in ((0, 0), (6, 1)):
                    for half in range(2):
                        turn(dve.tensor_copy(view(10240 + 512 * dst, TB, P)[:, :, half * HEAD:(half + 1) * HEAD],
                                             mixed[:, :, src * HEAD:(src + 1) * HEAD]))
        qaT, qbT, kbT = view(16384, 4, SEQ), view(18432, 4, SEQ), view(20480, 4, SEQ)
        kaT, kiT, qiT = view(22528, SEQ), view(23040, SEQ), view(23552, 2, SEQ)
        keys_twice = [view(10240 + 512 * i, TB, P) for i in range(2)]
        moves = [(lambda tb, s=src, q=q: s[:, tb, q * P:(q + 1) * P], TB, dst[:, q, :])
                 for src, dst in ((qa, qaT), (qb, qbT), (kb, kbT)) for q in range(4)]
        moves += [(lambda tb, s=keys_twice[0]: s[:, tb, :], TB, kaT),
                  (lambda tb, s=keys_twice[1]: s[:, tb, :], TB, kiT)]
        moves += [(lambda tb, q=q: mixed[:, tb, (2 + 2 * q) * HEAD:(4 + 2 * q) * HEAD], TB, qiT[:, q, :])
                  for q in range(2)]
        turn_heads(core, moves)

        relu, select = view(12288, 4, BANK), view(14336, 4, BANK)
        mem, mem_scratch = view(4096, MB, D), view(6144, MB, D)
        with ExitStack() as c:
            scored, rectified, step, summed = (core.sem(s) for s in ("scored", "rectified", "step", "summed"))
            block = core.stage(c)
            transfer(core, block, [(mem, t["mem"].rearrange("l (t p) d -> p (l t) d", p=P))])

            @block.tensor
            def _(pe):
                for b in range(1, TB):
                    keys = (b + 1) * P
                    for h in range(IDX_HEADS):
                        half = slice((h % 2) * HEAD, (h % 2 + 1) * HEAD)
                        if b == 3:
                            pe.wait_ge(rectified, h + 1)
                        pe.matmul(core.bank[(b - 1) % 2 * 4 + h][:, 0:keys],
                                  qiT[half, h // 2, b * P:(b + 1) * P], kiT[half, 0:keys],
                                  start=True, stop=True).then_inc(scored, 1)

            @block.scalar
            def _(act):
                for b in range(1, TB):
                    keys = (b + 1) * P
                    if b > 1:
                        act.wait_ge(summed, b - 1)
                    for h in range(IDX_HEADS):
                        act.wait_ge(scored, (b - 1) * 4 + h + 1)
                        act.activation(relu[:, h, 0:keys], core.bank[(b - 1) % 2 * 4 + h][:, 0:keys],
                                       ACT.Relu).then_inc(rectified, 1)

            @block.vector
            def _(dve):
                turn = Turn(dve, step)
                w_idx = mixed[:, :, 7 * HEAD:7 * HEAD + IDX_HEADS]
                turn(dve.tensor_scalar(w_idx, w_idx, IDX_HEADS ** -0.5 * HEAD ** -0.5, None, ALU.mult))
                turn.wait()
                for b in range(1, TB):
                    keys = (b + 1) * P
                    s = select[:, b, 0:keys]
                    dve.wait_ge(rectified, 4 * b)
                    turn(dve.tensor_scalar(s, relu[:, 0, 0:keys], w_idx[:, b, 0:1], None, ALU.mult))
                    for h in range(1, IDX_HEADS):
                        turn.wait()
                        ins = dve.scalar_tensor_tensor(s, relu[:, h, 0:keys], w_idx[:, b, h:h + 1], s,
                                                       ALU.mult, ALU.add)
                        if h < IDX_HEADS - 1:
                            turn(ins)
                    ins.then_inc(summed, 1)
                    dve.wait_ge(summed, b)
                    turn(dve.tensor_tensor(s, s, causal[:, BANK - keys:BANK], ALU.add))

        chosen = core.sem("chosen")
        top8 = small[:, 96:104]

        def choose_steps(dve):
            turn = Turn(dve, chosen)
            for b in range(1, TB):
                s = select[:, b, 0:(b + 1) * P]
                for i in range(TOPK // 8):
                    turn.wait()
                    turn(dve.max(top8, s))
                    turn.wait()
                    turn(dve.match_replace(s, top8, s, TAKEN))
                    if i % 3 < 2:
                        yield
                turn.wait()
                turn(dve.tensor_scalar(s, s, TAKEN, None, ALU.is_equal))
                turn.wait()
                turn(dve.tensor_scalar(s, s, -1.0, -NEG, ALU.add, ALU.mult))
                yield

        mix = view(4096, TB, D)
        buffers = (view(0, 3, BANK), view(10240, 2, BANK), small)
        kN, vN = view(12288, MB, D), view(8192, MB, D)

        def memory_product(target, vector, scalar=None):
            def scalar_steps(act):
                copies = paced(core.copy_steps(act, 0, DC, ((target, HALVES),), rows=MB), 4)
                return together(copies, scalar(act)) if scalar is not None else copies
            return dict(tiles=4, vector=vector, scalar=scalar_steps,
                        tensor=lambda pe: paced(core.product_steps(pe, 0, DC, HALVES, rows=MB), 4))

        def weighted(target):
            def finish(dve, turn, j, sums, values):
                turn(dve.reciprocal(sums, sums))
                turn.wait()
                return dve.tensor_scalar(target, values, sums, None, ALU.mult)
            return finish

        def less_weighted(target, first):
            def finish(dve, turn, j, sums, values):
                turn(dve.reciprocal(sums, sums))
                turn.wait()
                turn(dve.tensor_scalar(sums, sums, neg_lambda[:, 2:3], None, ALU.mult))
                turn.wait()
                return dve.scalar_tensor_tensor(target, values, sums, first, ALU.mult, ALU.add)
            return finish

        to_columns(core, mem, g_mem, rows=MB, norm=(mem_scratch, small))
        units = []
        for b in range(TB):
            keys = (b + 1) * P
            for h in range(B_HEADS):
                first = view(11264, 2, P)[:, h % 2, :]
                target = mix[:, b, 512 + h * P:512 + (h + 1) * P]
                for k in range(2):
                    half = slice(k * HEAD, (k + 1) * HEAD)
                    units.append(([(qbT[half, h, b * P:(b + 1) * P], kbT[half, h, 0:keys])], keys,
                                  causal[:, BANK - keys:BANK],
                                  lambda c_, h=h: vb[:, c_, h * P:(h + 1) * P], P,
                                  less_weighted(target, first) if k else weighted(first)))
        attention(core, units, HEAD ** -0.5, buffers, beside=memory_product(kN, choose_steps))

        out_b = mix[:, :, 512:1024]
        squares_b = view(23040, 2, 512)
        mean_b, rms_b, rstd_b = small[:, 64:80], small[:, 80:96], small[:, 104:120]
        squared_b, mean_step, rooted_b, normed_b = (core.sem(s) for s in (
            "squared_b", "mean_b", "rooted_b", "normed_b"))

        def square_steps(act):
            for tb in range(TB):
                if tb >= 2:
                    act.wait_ge(mean_step, tb - 1)
                act.activation(squares_b[:, tb % 2, :], out_b[:, tb, :], ACT.Square)\
                   .then_inc(squared_b, 1)
                yield
            yield
            act.wait_ge(mean_step, TB + 1)
            act.activation(rms_b, mean_b, ACT.Sqrt).then_inc(rooted_b, 1)
            yield

        def norm_steps(dve):
            for tb in range(TB):
                dve.wait_ge(squared_b, tb + 1)
                dve.tensor_reduce(mean_b[:, tb * B_HEADS:(tb + 1) * B_HEADS],
                                  squares_b[:, tb % 2, :].rearrange("p (h d) -> p h d", h=B_HEADS),
                                  AX.X, ALU.add).then_inc(mean_step, 1)
                yield
            dve.wait_ge(mean_step, TB)
            dve.tensor_scalar(mean_b, mean_b, 1.0 / P, EPS, ALU.mult, ALU.add).then_inc(mean_step, 1)
            yield
            yield
            dve.wait_ge(rooted_b, 1)
            dve.reciprocal(rstd_b, rms_b).then_inc(normed_b, 1)
            dve.wait_ge(normed_b, 1)
            dve.tensor_scalar(rstd_b, rstd_b, 1.0 - LAMBDA_INIT, None, ALU.mult).then_inc(normed_b, 1)
            dve.wait_ge(normed_b, 2)
            for tb in range(TB):
                xt = out_b[:, tb, :].rearrange("p (h d) -> p h d", h=B_HEADS)
                r = rstd_b[:, tb * B_HEADS:(tb + 1) * B_HEADS].unsqueeze(2)\
                    .to_broadcast([P, B_HEADS, P])
                dve.tensor_tensor(xt, xt, r, ALU.mult).then_inc(normed_b, 1)
                yield

        x = view(18432, TB, D)
        x_rows = t["x"].rearrange("l (t p) d -> p (l t) d", p=P)
        units = []
        for b in range(TB):
            keys = (b + 1) * P
            for h in range(A_HEADS):
                half = slice((h % 2) * HEAD, (h % 2 + 1) * HEAD)
                bias = select[:, b, 0:keys] if b else causal[:, 3 * P:4 * P]
                units.append(([(qaT[half, h // 2, b * P:(b + 1) * P], kaT[half, 0:keys])], keys, bias,
                              lambda k: mixed[:, k, HEAD:2 * HEAD], HEAD,
                              weighted(mix[:, b, h * HEAD:(h + 1) * HEAD])))
        attention(core, units, HEAD ** -0.5, buffers, transfers=[(x, x_rows)],
                  beside=memory_product(vN, norm_steps, square_steps))
        to_columns(core, mix)
        add_product(core, 4, DC, x)
        if stop == "mixer":
            return finish_debug(core, x, out, out_stored)

        kT = view(10240, DC, N_MEM)

        def rows_product(n_tiles, k_chunks, target, tiles, moves=()):
            with ExitStack() as c:
                block = core.stage(c)

                @block.tensor
                def _(pe):
                    core.products_by_rows(pe, 0, k_chunks, tiles)

                core.stream(block, n_tiles, moves)

                @block.scalar
                def _(act):
                    for _step in core.copy_steps(act, 0, k_chunks, ((target, tiles),)):
                        pass

        head_norm(core, kN, X_HEADS, view(14336, MB, D), small, rows=MB)
        turn_heads(core, [(lambda tb, q=q: kN[:, tb, q * P:(q + 1) * P], MB, kT[:, q, :])
                          for q in range(DC)],
                   gains=[xqk_gain[:, q % 2:q % 2 + 1] for q in range(DC)])
        qN, qT = view(14336, TB, D), view(0, DC, SEQ)
        to_columns(core, x, g_xattn, norm=(view(0, TB, D), small))
        q_mean, q_rms, q_scale = small[:, 64:80], small[:, 80:96], small[:, 104:120]
        squares = view(4096, 2 * TB, BANK)
        with ExitStack() as c:
            squared, meaned, rooted, scaled = (core.sem(s) for s in ("squared", "mean", "rooted", "scaled"))
            block = core.stage(c)

            @block.tensor
            def _(pe):
                core.products_by_rows(pe, 0, DC, HALVES)

            core.stream(block, 4)

            @block.scalar
            def _(act):
                for g in range(2 * TB):
                    half, tb = divmod(g, TB)
                    if tb == 0:
                        core.w.round_upto(act, core.tile0 + 2 * half + 3)
                    core.wait_group(act, g)
                    for i in range(2):
                        at = tb * X_HEADS + 2 * half + i
                        act.activation(squares[:, g, i * X_HEAD:(i + 1) * X_HEAD],
                                       core.bank_of(g)[:, i * X_HEAD:(i + 1) * X_HEAD], ACT.Square,
                                       accum_out=q_mean[:, at:at + 1]).then_inc(squared, 1)
                act.wait_ge(meaned, 1)
                act.activation(q_rms, q_mean, ACT.Sqrt).then_inc(rooted, 1)
                core.w.round_upto(act, core.ahead(4))

            @block.vector
            def _(dve):
                for g in range(2 * TB):
                    half, tb = divmod(g, TB)
                    dve.wait_ge(squared, 2 * g + 2)
                    dve.tensor_copy(qN[:, tb, half * 512:(half + 1) * 512], core.bank_of(g)[:, :])\
                       .then_inc(core.freed, 1)
                dve.tensor_scalar(q_mean, q_mean, 1.0 / X_HEAD, EPS, ALU.mult, ALU.add)\
                   .then_inc(meaned, 1)
                dve.wait_ge(rooted, 1)
                dve.reciprocal(q_scale, q_rms).then_inc(scaled, 1)
                dve.wait_ge(scaled, 1)
                dve.tensor_scalar(q_scale, q_scale, X_HEAD ** -0.5, None, ALU.mult).then_inc(scaled, 1)

        turn_heads(core, [(lambda tb, q=q: qN[:, tb, q * P:(q + 1) * P], TB, qT[:, q, :])
                          for q in range(DC)])
        o = view(14336, TB, D)
        units = []
        for b in range(TB):
            for h in range(X_HEADS):
                units.append(([(qT[:, 2 * h + k, b * P:(b + 1) * P], kT[:, 2 * h + k, :])
                               for k in range(2)], N_MEM, causal[:, 0:N_MEM],
                              lambda k, h=h: vN[:, k, h * X_HEAD:(h + 1) * X_HEAD], X_HEAD,
                              weighted(o[:, b, h * X_HEAD:(h + 1) * X_HEAD])))
        attention(core, units, lambda i: q_scale[:, i:i + 1],
                  (view(4096, 3, BANK), view(5632, 2, BANK), small))
        to_columns(core, o)
        add_product(core, 4, DC, x)
        if stop == "cross":
            return finish_debug(core, x, out, out_stored)
        core.recycle()

        to_columns(core, x, g_ffn, norm=(view(0, TB, D), small))
        hidden = view(0, FC, SEQ)
        conv, gelu = view(11264, 2, SEQ), view(12288, 2, SEQ)
        with ExitStack() as c:
            started, convolved, activated, step = (core.sem(s) for s in ("started", "convolved",
                                                                         "activated", "step"))
            block = core.stage(c)
            PAIRS = FC // 2

            @block.tensor
            def _(pe):
                for i in range(2 * PAIRS):
                    core.products_by_columns(pe, 2 * i, DC, 2 * P)

            core.stream(block, 2 * PAIRS)

            @block.scalar
            def _(act):
                for i in range(PAIRS):
                    core.w.round_upto(act, core.tile0 + 2 * i + 2)
                    for k in range(2):
                        ch = 2 * i + k
                        core.wait_group(act, 4 * i + k)
                        if i:
                            act.wait_ge(activated, 2 * i - 1 + k)
                        act.activation(conv[:, k, :], core.bank[(4 * i + k) % BANKS][:, :], ACT.Identity,
                                       scale=conv_w[:, 2 * FC + ch:2 * FC + ch + 1],
                                       bias=conv_b[:, ch:ch + 1]).then_inc(started, 1)
                    core.w.round_upto(act, core.tile0 + 2 * i + 3)
                    for k in range(2):
                        act.wait_ge(core.freed, core.groups_at_start + 4 * i + k + 1)
                        if i:
                            act.wait_ge(core.freed, core.groups_at_start + 4 * (i - 1) + 3 + k)
                        act.activation(gelu[:, k, :], conv[:, k, :], ACT.Gelu_apprx_tanh)\
                           .then_inc(activated, 1)
                core.w.round_upto(act, core.ahead(2 * PAIRS))

            @block.vector
            def _(dve):
                for i in range(PAIRS):
                    for k in range(2):
                        ch = 2 * i + k
                        a = core.bank[(4 * i + k) % BANKS]
                        dve.wait_ge(started, ch + 1)
                        w = lambda j: conv_w[:, j * FC + ch:j * FC + ch + 1]
                        dve.scalar_tensor_tensor(conv[:, k, 1:SEQ], a[:, 0:SEQ - 1], w(1),
                                                 conv[:, k, 1:SEQ], ALU.mult, ALU.add)\
                           .then_inc(step, 1)
                        dve.wait_ge(step, ch + 1)
                        dve.scalar_tensor_tensor(conv[:, k, 2:SEQ], a[:, 0:SEQ - 2], w(0),
                                                 conv[:, k, 2:SEQ], ALU.mult, ALU.add)\
                           .then_inc(core.freed, 1)
                    for k in range(2):
                        g = 4 * i + 2 + k
                        core.wait_group(dve, g)
                        dve.wait_ge(activated, 2 * i + k + 1)
                        dve.tensor_tensor(hidden[:, 2 * i + k, :], core.bank[g % BANKS][:, :],
                                          gelu[:, k, :], ALU.mult).then_inc(core.freed, 1)

        with ExitStack() as c:
            rounded, remainder = core.sem("rounded"), core.sem("remainder")
            block = core.stage(c)
            K_GROUPS = [(k0, min(4, FC - k0)) for k0 in range(0, FC, 4)]
            released = []

            @block.tensor
            def _(pe):
                for i, (k0, kn) in enumerate(K_GROUPS):
                    pe.wait_ge(remainder, i + 1)
                    for half in range(2):
                        hi, lo = core.w.take(pe, kn, 512)
                        for tb in range(TB):
                            for k in range(kn):
                                xs = (slice(None), i % 2 * 4 + k, slice(tb * P, (tb + 1) * P))
                                for a, b in ((core.xh, hi), (core.xh, lo), (core.xl, hi)):
                                    last = k == kn - 1 and a is core.xl
                                    first = k == 0 and a is core.xh and b is hi
                                    ins = pe.matmul(core.bank[half * TB + tb][:, :], a[xs], b[:, k, :],
                                                    start=(i == 0 and first),
                                                    stop=(k0 + kn == FC and last))
                            if k0 + kn == FC:
                                ins.then_inc(core.ready, 1)
                                core.groups += 1
                        if k0 + kn == FC:
                            core.w.release(ins, core.ready, core.groups)
                        else:
                            core.w.release(ins)
                    released.append(core.w.used_at[-1])

            core.stream(block, 2 * len(K_GROUPS))

            @block.scalar
            def _(act):
                for i, (k0, kn) in enumerate(K_GROUPS):
                    if i >= 2:
                        act.wait_ge(*released[i - 2])
                    act.activation(core.xh[:, i % 2 * 4:i % 2 * 4 + kn, :], hidden[:, k0:k0 + kn, :],
                                   ACT.Copy).then_inc(rounded, 1)
                    core.w.round_upto(act, core.tile0 + 2 * i + 2)
                core.w.round_upto(act, core.ahead(2 * len(K_GROUPS)))

            @block.vector
            def _(dve):
                for i, (k0, kn) in enumerate(K_GROUPS):
                    dve.wait_ge(rounded, i + 1)
                    part = (slice(None), slice(i % 2 * 4, i % 2 * 4 + kn))
                    dve.tensor_tensor(core.xl[part], hidden[:, k0:k0 + kn, :],
                                      core.xh[part].bitcast(F32), ALU.subtract).then_inc(remainder, 1)
                for g in range(2 * TB):
                    core.wait_group(dve, g)
                    target = x[:, g % TB, g // TB * 512:(g // TB + 1) * 512]
                    dve.tensor_tensor(target, core.bank[g][:, :], target, ALU.add)\
                       .then_inc(core.freed, 1)
        if stop == "ffn":
            return finish_debug(core, x, out, out_stored)

        saved_rows = lambda a: a.rearrange("(t p) d -> p t d", p=P)
        to_columns(core, x, g_second, norm=(view(0, TB, D), small), moves=[(saved_rows(x_saved), x)])
        Q, K, KI, KON, V = (view(4096 * i, n, 4096 // n) for i, n in enumerate((8, 8, 8, TB, TB)))
        scratch = view(20480, 6, SEQ)
        state = arena[:, 23552:23552 + HG_HEADS * P].rearrange("p (h v) -> p h v", h=HG_HEADS)
        with ExitStack() as c:
            sigmoid = core.sem("sigmoid")
            block = core.stage(c)

            @block.tensor
            def _(pe):
                for i in range(8):
                    core.products_by_columns(pe, 2 * i, DC, 2 * P)

            core.stream(block, 8)

            @block.scalar
            def _(act):
                for g in range(16):
                    if g % 2 == 0:
                        core.w.round_upto(act, core.tile0 + g // 2 + 2)
                    core.wait_group(act, g)
                    if g >= 2:
                        act.wait_ge(core.freed, core.groups_at_start + g - 1)
                    dst = scratch[:, g % 2, :] if g < 8 else K[:, g - 8, :]
                    act.activation(dst, core.bank[g % BANKS][:, :], ACT.Sigmoid).then_inc(sigmoid, 1)
                core.w.round_upto(act, core.ahead(8))

            @block.vector
            def _(dve):
                for g in range(8):
                    dve.wait_ge(sigmoid, g + 1)
                    dve.tensor_tensor(Q[:, g, :], core.bank[g % BANKS][:, :], scratch[:, g % 2, :],
                                      ALU.mult).then_inc(core.freed, 1)
                for h in range(8):
                    dve.wait_ge(sigmoid, 8 + h + 1)
                    dve.tensor_scalar(K[:, h, :], K[:, h, :], lower[:, 8 + h:9 + h], lower[:, h:h + 1],
                                      ALU.mult, ALU.add).then_inc(core.freed, 1)
        keep = view(4096 * 3, SEQ)
        with ExitStack() as c:
            kept, logged, scanned, to_last, up, down, out_ = (core.sem(s) for s in (
                "kept", "logged", "scanned", "to_last", "exp_b", "exp_minus_b", "exp_to_last"))
            made_q, made_ki, made_k, turned, copied, one_less, decayed = (core.sem(s) for s in (
                "made_q", "made_ki", "made_k", "turned", "copied", "one_less", "decayed"))
            block = core.stage(c)
            b_ = KI

            @block.tensor
            def _(pe):
                core.products_by_rows(pe, 0, DC, HALVES)

            @block.sync
            def _(sp):
                core.w.load_upto(sp, core.ahead(4) + core.w.RAW)

            @block.gpsimd
            def _(pool):
                pool.memset(keep, 1.0).then_inc(kept, 1)
                pool.wait_ge(kept, 1)
                k2 = keep.rearrange("p (n c) -> p n c", c=HG_CHUNK)
                pool.affine_select(out=k2, in_=k2, compare_op=ALU.not_equal, fill=0.0, base=0,
                                   pattern=[[0, SEQ // HG_CHUNK], [1, HG_CHUNK]], channel_multiplier=0)\
                    .then_inc(kept, 1)
                core.w.split_upto(pool, core.ahead(4))

            @block.scalar
            def _(act):
                for h in range(HG_HEADS):
                    act.activation(b_[:, h, :], K[:, h, :], ACT.Ln).then_inc(logged, 1)
                core.w.round_upto(act, core.tile0 + 2)
                for h in range(HG_HEADS):
                    if h == 2:
                        core.w.round_upto(act, core.tile0 + 3)
                    act.wait_ge(to_last, h + 1)
                    if h >= 2:
                        act.wait_ge(decayed, h - 1)
                    act.activation(scratch[:, h % 2, :], b_[:, h, :], ACT.Exp).then_inc(up, 1)
                    act.activation(scratch[:, 2 + h % 2, :], b_[:, h, :], ACT.Exp, scale=-1.0)\
                       .then_inc(down, 1)
                    d = scratch[:, 4 + h % 2, :]
                    act.activation(d, d, ACT.Exp).then_inc(out_, 1)
                for g in range(2 * TB):
                    half, tb = divmod(g, TB)
                    if tb == 0:
                        core.w.round_upto(act, core.tile0 + 4 + half)
                    core.copy_group(act, g, V[:, tb, half * 512:(half + 1) * 512], 512)

            @block.vector
            def _(dve):
                dve.wait_ge(kept, 2)
                for h in range(HG_HEADS):
                    dve.wait_ge(logged, h + 1)
                    dve.tensor_tensor_scan(b_[:, h, :], keep, b_[:, h, :], 0.0, ALU.mult, ALU.add)\
                       .then_inc(scanned, 1)
                    dve.tensor_scalar(K[:, h, :], K[:, h, :], -1.0, 1.0, ALU.mult, ALU.add)\
                       .then_inc(one_less, 1)

                def last_minus(h):
                    if h >= 2:
                        dve.wait_ge(made_k, h - 1)
                    dve.wait_ge(scanned, h + 1)
                    b3 = b_[:, h, :].rearrange("p (n c) -> p n c", c=HG_CHUNK)
                    d3 = scratch[:, 4 + h % 2, :].rearrange("p (n c) -> p n c", c=HG_CHUNK)
                    last = b3[:, :, HG_CHUNK - 1:HG_CHUNK].to_broadcast([P, SEQ // HG_CHUNK, HG_CHUNK])
                    dve.tensor_tensor(d3, last, b3, ALU.subtract).then_inc(to_last, 1)

                last_minus(0)
                for h in range(HG_HEADS):
                    if h + 1 < HG_HEADS:
                        last_minus(h + 1)
                    dve.wait_ge(one_less, h + 1)
                    dve.wait_ge(up, h + 1)
                    dve.tensor_tensor(Q[:, h, :], Q[:, h, :], scratch[:, h % 2, :], ALU.mult)\
                       .then_inc(made_q, 1)
                    e3 = scratch[:, h % 2, :].rearrange("p (n c) -> p n c", c=HG_CHUNK)
                    dve.tensor_copy(decay[:, h, :], e3[:, :, HG_CHUNK - 1]).then_inc(made_q, 1)
                    dve.wait_ge(down, h + 1)
                    dve.tensor_tensor(KI[:, h, :], K[:, h, :], scratch[:, 2 + h % 2, :], ALU.mult)\
                       .then_inc(decayed, 1)
                    dve.wait_ge(out_, h + 1)
                    dve.wait_ge(decayed, h + 1)
                    dve.tensor_tensor(K[:, h, :], K[:, h, :], scratch[:, 4 + h % 2, :], ALU.mult)\
                       .then_inc(made_k, 1)

        turn_heads(core, [(lambda tb, h=h: K[:, h, tb * P:(tb + 1) * P], TB,
                           KON[:, :, h * P:(h + 1) * P]) for h in range(HG_HEADS)])
        C = P // HG_CHUNK
        intra = view(20480, 2, HG_HEADS * P)
        o = view(4096, TB, D)
        with ExitStack() as c:
            cleared, scores_in, masked, intra_done, kv_done = (core.sem(s) for s in (
                "cleared", "scores_in", "masked", "intra_done", "kv_done"))
            updated, out_ready, out_read = (core.sem(s) for s in ("updated", "out_ready", "out_read"))
            block = core.stage(c)

            @block.tensor
            def _(pe):
                for tb in range(TB):
                    tok = slice(tb * P, (tb + 1) * P)
                    if tb >= 1:
                        pe.wait_ge(masked, 2 * tb)
                    for h in range(HG_HEADS):
                        ins = pe.matmul(core.bank[h // 4][:, h % 4 * P:(h % 4 + 1) * P],
                                        KI[:, h, tok], Q[:, h, tok], start=True, stop=True)
                        if h % 4 == 3:
                            ins.then_inc(scores_in, 1)
                    ob = core.bank[2 + tb % 2 * 2:4 + tb % 2 * 2]
                    if tb >= 2:
                        pe.wait_ge(out_read, 2 * (tb - 1))
                    for h in range(HG_HEADS):
                        pe.wait_ge(masked, 2 * tb + h // 4 + 1)
                        pe.matmul(ob[h // 4][:, h % 4 * P:(h % 4 + 1) * P],
                                  intra[:, tb % 2, h * P:(h + 1) * P], V[:, tb, h * P:(h + 1) * P],
                                  start=(h % 4 == 0), stop=False, skip_group_check=True)\
                          .then_inc(intra_done, 1)
                    for n in range(C):
                        step = tb * C + n
                        rows = slice(n * HG_CHUNK, (n + 1) * HG_CHUNK)
                        for g in range(2):
                            heads = range(4 * g, 4 * g + 4)
                            pe.wait_ge(updated, HG_HEADS * step + 4 * g + 4)
                            for h in heads:
                                ins = pe.matmul(ob[g][rows, h % 4 * P:(h % 4 + 1) * P],
                                                Q[:, h, tb * P + n * HG_CHUNK:tb * P + (n + 1) * HG_CHUNK],
                                                state[:, h, :], start=False, stop=(h % 4 == 3),
                                                skip_group_check=True)
                            if n == C - 1:
                                ins.then_inc(out_ready, 1)
                            if step < TB * C - 1:
                                for h in heads:
                                    ins = pe.matmul(core.bank[6 + g][:, h % 4 * P:(h % 4 + 1) * P],
                                                    KON[rows, tb, h * P:(h + 1) * P],
                                                    V[rows, tb, h * P:(h + 1) * P], start=True, stop=True)
                                ins.then_inc(kv_done, 1)

            @block.vector
            def _(dve):
                dve.memset(intra, 0.0).then_inc(cleared, 1)
                for h in range(HG_HEADS):
                    dve.memset(state[:, h, :], 0.0).then_inc(updated, 1)
                dve.wait_ge(cleared, 1)
                m = mask32[:, :].bitcast(I32).unsqueeze(1).to_broadcast([P, 4, P])

                def mask(tb):
                    if tb >= 2:
                        dve.wait_ge(intra_done, HG_HEADS * (tb - 1))
                    for g in range(2):
                        dve.wait_ge(scores_in, 2 * tb + g + 1)
                        dst = intra[:, tb % 2, g * BANK:(g + 1) * BANK].rearrange("p (h s) -> p h s", h=4)
                        dve.copy_predicated(dst, m, core.bank[g][:, :].rearrange("p (h s) -> p h s", h=4))\
                           .then_inc(masked, 1)

                for tb in range(TB):
                    mask(tb)
                    for n in range(C):
                        step = tb * C + n
                        if step == TB * C - 1:
                            break
                        for h in range(HG_HEADS):
                            dve.wait_ge(kv_done, 2 * step + h // 4 + 1)
                            dve.wait_ge(updated, HG_HEADS * step + h + 1)
                            dve.scalar_tensor_tensor(
                                state[:, h, :], state[:, h, :], decay[:, h, step:step + 1],
                                core.bank[6 + h // 4][:, h % 4 * P:(h % 4 + 1) * P],
                                ALU.mult, ALU.add).then_inc(updated, 1)

            @block.scalar
            def _(act):
                for tb in range(TB):
                    for g in range(2):
                        act.wait_ge(out_ready, 2 * tb + g + 1)
                        act.activation(o[:, tb, g * BANK:(g + 1) * BANK], core.bank[2 + tb % 2 * 2 + g][:, :],
                                       ACT.Copy).then_inc(out_read, 1)

        def gated_product(target, gate_buf, norm=None):
            with ExitStack() as c:
                gated, squared, meaned, rooted, normed = (core.sem(s) for s in (
                    "gated", "squared", "mean", "rooted", "normed"))
                block = core.stage(c)
                n = TB * HG_HEADS
                mean, rms, rstd = small[:, 0:n], small[:, 32:32 + n], small[:, 64:64 + n]

                @block.tensor
                def _(pe):
                    core.products_by_rows(pe, 0, DC, HALVES)

                core.stream(block, 4)

                @block.scalar
                def _(act):
                    if norm is not None:
                        for tb in range(TB):
                            act.activation(norm[1][:, tb, :], norm[0][:, tb, :], ACT.Square)\
                               .then_inc(squared, 1)
                        core.w.round_upto(act, core.tile0 + 2)
                        act.wait_ge(meaned, TB + 1)
                        act.activation(rms, mean, ACT.Sqrt).then_inc(rooted, 1)
                    for g in range(2 * TB):
                        if g % TB == 0:
                            core.w.round_upto(act, core.tile0 + 2 * (g // TB) + 3)
                        core.wait_group(act, g)
                        if g >= 2:
                            act.wait_ge(core.freed, core.groups_at_start + g - 1)
                        act.activation(gate_buf[:, g % 2, :], core.bank_of(g)[:, :], ACT.Silu)\
                           .then_inc(gated, 1)
                    core.w.round_upto(act, core.ahead(4))

                @block.vector
                def _(dve):
                    if norm is not None:
                        for tb in range(TB):
                            dve.wait_ge(squared, tb + 1)
                            dve.tensor_reduce(mean[:, tb * HG_HEADS:(tb + 1) * HG_HEADS],
                                              norm[1][:, tb, :].rearrange("p (h d) -> p h d", d=P),
                                              AX.X, ALU.add).then_inc(meaned, 1)
                        dve.wait_ge(meaned, TB)
                        dve.tensor_scalar(mean, mean, 1.0 / P, EPS, ALU.mult, ALU.add)\
                           .then_inc(meaned, 1)
                        dve.wait_ge(rooted, 1)
                        dve.reciprocal(rstd, rms).then_inc(normed, 1)
                        dve.wait_ge(normed, 1)
                        for tb in range(TB):
                            xt = norm[0][:, tb, :].rearrange("p (h d) -> p h d", d=P)
                            r = rstd[:, tb * HG_HEADS:(tb + 1) * HG_HEADS].unsqueeze(2)\
                                .to_broadcast([P, HG_HEADS, P])
                            dve.tensor_tensor(xt, xt, r, ALU.mult).then_inc(normed, 1)
                        dve.wait_ge(normed, 1 + TB)
                    for g in range(2 * TB):
                        dve.wait_ge(gated, g + 1)
                        tt = target(g % TB, g // TB)
                        gate = gate_buf[:, g % 2, :].rearrange("p (h d) -> p h d", d=P)
                        dve.tensor_tensor(tt, tt, gate, ALU.mult).then_inc(core.freed, 1)

        def rows_of(a):
            return lambda tb, half: a[:, tb, half * 512:(half + 1) * 512]\
                .rearrange("p (h d) -> p h d", d=P)

        gated_product(rows_of(o), view(8192, 2, 512), norm=(o, view(0, TB, D)))
        core.recycle()

        qnT, knT, vN = view(0, 8, SEQ), view(4096, 8, SEQ), view(8192, TB, D)
        qpT, kpT = view(12288, 4, SEQ), view(14336, SEQ)
        cN = view(14848, TB, Q_LORA + KV_LORA + PE_DIM)
        qpN = view(17664, TB, 8 * PE_DIM)
        t1, t2 = view(19712, 1024), view(20736, 1024)
        kr_twice = view(21760, TB, P)
        rows_product(4, DC, cN, ((0, 384), (384, 320)), moves=[(saved_rows(y_saved), o)])
        to_columns(core, cN[:, :, 0:Q_LORA], q_a_gain, norm=(view(17664, TB, Q_LORA), small),
                   width=Q_LORA)
        to_columns(core, cN[:, :, Q_LORA:Q_LORA + KV_LORA], kv_a_gain,
                   norm=(view(17664, TB, KV_LORA), small), width=KV_LORA, x0=3)
        with ExitStack() as c:
            rotated = core.sem("rotated")
            block = core.stage(c)

            @block.tensor
            def _(pe):
                g = core.products_by_columns(pe, 0, 3, 4 * NOPE)
                g = core.products_by_columns(pe, g, 3, 4 * NOPE)
                g = core.products_by_rows(pe, g, 3, ((0, 8 * PE_DIM),))
                g = core.products_by_columns(pe, g, 2, 8 * NOPE, x0=3)
                core.products_by_rows(pe, g, 2, HALVES, x0=3)

            core.stream(block, 6)

            @block.scalar
            def _(act):
                places = [(qnT[:, h, :], 0 if h < 4 else 1) for h in range(8)]
                places += [(qpN[:, tb, :], 2) for tb in range(TB)]
                places += [(knT[:, h, :], 3) for h in range(8)]
                places += [(vN[:, tb, 512 * half:512 * (half + 1)], 4 + half)
                           for half in range(2) for tb in range(TB)]
                for g, (dst, tile) in enumerate(places):
                    core.w.round_upto(act, core.tile0 + tile + 2)
                    core.wait_group(act, g)
                    act.activation(dst, core.bank[g % BANKS][:, :], ACT.Copy).then_inc(core.freed, 1)
                core.w.round_upto(act, core.ahead(6))

            @block.vector
            def _(dve):
                turn = Turn(dve, rotated)
                kr = cN[:, :, Q_LORA + KV_LORA:]
                rope(dve, turn, kr, 1, plain_tables(1), t1, t2)
                for half in range(2):
                    turn(dve.tensor_copy(kr_twice[:, :, half * HEAD:(half + 1) * HEAD], kr))
                dve.wait_ge(core.freed, core.groups_at_start + 12)
                rope(dve, turn, qpN, 8, plain_tables(1), t1, t2)

        turn_heads(core, [(lambda tb, q=q: qpN[:, tb, q * P:(q + 1) * P], TB, qpT[:, q, :])
                          for q in range(4)] + [(lambda tb: kr_twice[:, tb, :], TB, kpT)])
        y_b = qnT
        x = view(14848, TB, D)
        units = []
        for b in range(TB):
            keys = (b + 1) * P
            q_tok = slice(b * P, (b + 1) * P)
            for h in range(MLA_HEADS):
                half = slice((h % 2) * HEAD, (h % 2 + 1) * HEAD)
                units.append(([(qnT[:, h, q_tok], knT[:, h, 0:keys]),
                               (qpT[half, h // 2, q_tok], kpT[half, 0:keys])], keys,
                              causal[:, BANK - keys:BANK],
                              lambda k, h=h: vN[:, k, h * P:(h + 1) * P], V_DIM,
                              weighted(y_b[:, h, q_tok])))
        attention(core, units, (NOPE + PE_DIM) ** -0.5, (view(18944, 3, BANK), view(20480, 2, BANK), small),
                  transfers=[(x, saved_rows(x_saved))])

        gates = arena[:, 4096:12288].rearrange("p (n t d) -> p n t d", n=2, t=TB)
        gate_bias = view(12288, 2 * D)
        y_a = view(18944, TB, D)
        to_columns(core, x, g_second, norm=(view(4096, TB, D), small),
                   moves=[(y_a, saved_rows(y_saved)), (gate_bias, over_partitions(t["b_gate_2"]))])
        gated_product(lambda tb, half: y_b[:, 4 * half:4 * half + 4, tb * P:(tb + 1) * P],
                      view(4096, 2, 512))
        with ExitStack() as c:
            biased, gated = core.sem("biased"), core.sem("gated")
            block = core.stage(c)

            @block.tensor
            def _(pe):
                core.products_by_rows(pe, 0, DC, [(0, 512)] * 4)

            core.stream(block, 8)

            @block.vector
            def _(dve):
                for g in range(4 * TB):
                    c_, tb = divmod(g, TB)
                    core.wait_group(dve, g)
                    dve.tensor_tensor(gates[:, c_ // 2, tb, c_ % 2 * 512:(c_ % 2 + 1) * 512],
                                      core.bank[g % BANKS][:, :], gate_bias[:, c_ * 512:(c_ + 1) * 512],
                                      ALU.add).then_inc(core.freed, 1)

            @block.scalar
            def _(act):
                for g in range(4 * TB):
                    c_, tb = divmod(g, TB)
                    if tb == 0:
                        core.w.round_upto(act, core.tile0 + 2 * c_ + 3)
                    act.wait_ge(core.freed, core.groups_at_start + g + 1)
                    part = gates[:, c_ // 2, tb, c_ % 2 * 512:(c_ % 2 + 1) * 512]
                    act.activation(part, part, ACT.Sigmoid).then_inc(gated, 1)
                core.w.round_upto(act, core.ahead(8))

        def gate_product(branch):
            with ExitStack() as c:
                step = core.sem("step")
                block = core.stage(c)

                @block.tensor
                def _(pe):
                    core.products_by_rows(pe, 0, DC, HALVES)

                core.stream(block, 4)

                @block.scalar
                def _(act):
                    core.w.round_upto(act, core.ahead(4))

                @block.vector
                def _(dve):
                    for g in range(2 * TB):
                        core.wait_group(dve, g)
                        part = (slice(None), branch, g % TB, slice(g // TB * 512, (g // TB + 1) * 512))
                        dve.tensor_tensor(gates[part], core.bank[g][:, :], gates[part], ALU.mult)\
                           .then_inc(core.freed, 1)
                        if branch:
                            first = (part[0], 0) + part[2:]
                            dve.wait_ge(core.freed, core.groups_at_start + g + 1)
                            dve.tensor_tensor(gates[first], gates[first], gates[part], ALU.add)\
                               .then_inc(step, 1)

        to_columns(core, y_a, hg_gain.to_broadcast([P, HG_HEADS]))
        gate_product(0)
        to_columns(core, y_b, by_head=True)
        gate_product(1)
        to_columns(core, gates[:, 0])
        add_product(core, 4, DC, x)
        assert core.w.n_taken == len(core.w.tiles)

        final_gain, y = view(4096, D), view(0, TB, D)
        with ExitStack() as c:
            loaded, squared, mean, rooted, scaled, gained = (core.sem(s) for s in (
                "loaded", "squared", "mean", "rooted", "scaled", "gained"))
            block = core.stage(c)
            ss, rms, rstd = small[:, 0:TB], small[:, 4:4 + TB], small[:, 8:8 + TB]

            @block.scalar
            def _(act):
                for tb in range(TB):
                    act.activation(y[:, tb, :], x[:, tb, :], ACT.Square,
                                   accum_out=ss[:, tb:tb + 1]).then_inc(squared, 1)
                act.wait_ge(mean, 1)
                act.activation(rms, ss, ACT.Sqrt).then_inc(rooted, 1)

            @block.vector
            def _(dve):
                dve.wait_ge(squared, TB)
                dve.tensor_scalar(ss, ss, 1.0 / D, EPS, ALU.mult, ALU.add).then_inc(mean, 1)
                dve.wait_ge(rooted, 1)
                dve.reciprocal(rstd, rms).then_inc(mean, 1)
                dve.wait_ge(mean, 2)
                dve.wait_ge(loaded, 16)
                for tb in range(TB):
                    dve.scalar_tensor_tensor(y[:, tb, :], x[:, tb, :], rstd[:, tb:tb + 1],
                                             final_gain, ALU.mult, ALU.mult).then_inc(scaled, 1)

            @block.sync
            def _(sp):
                sp.dma_start(final_gain, t["final_norm_g_2"].partition_broadcast(P)).then_inc(loaded, 16)
                dst = out.rearrange("l (t p) d -> p (l t) d", p=P)
                for tb in range(TB):
                    sp.wait_ge(scaled, tb + 1)
                    sp.dma_start(dst[:, tb, :], y[:, tb, :]).then_inc(out_stored, 16)
                sp.wait_ge(out_stored, 16 * TB)


def finish_debug(core, x, out, out_stored):
    with ExitStack() as c:
        block = core.stage(c)

        @block.sync
        def _(sp):
            sp.dma_start(out.rearrange("l (t p) d -> p (l t) d", p=P), x).then_inc(out_stored, 16)
            sp.wait_ge(out_stored, 16)


INPUTS = ("x mem positions g_mix w_in g_qa g_ka g_qb g_kb lam_q1 lam_k1 lam_q2 lam_k2 w_out g_xattn "
          "g_mem w_xq w_xk w_xv w_xo g_xq g_xk g_ffn w_ffn_in conv_w conv_b w_ffn_out norm_g_2 w_in_2 "
          "b_gate_2 lb_logits_2 hg_norm_g_2 q_a_g_2 w_uq_2 kv_a_g_2 w_ukv_2 w_proj_a_2 w_proj_b_2 "
          "w_out_2 final_norm_g_2").split()
STOP = None


def kernel(**inputs):
    import numpy as _np
    import concourse.bacc as _bacc
    from concourse.bass_utils import run_bass_kernel_spmd as _run

    nc = _bacc.Bacc("TRN2", target_bir_lowering=False, num_devices=1)
    arrays, aps = {}, {}
    for name in INPUTS:
        a = _np.ascontiguousarray(inputs[name])
        arrays[f"in_{name}"] = a
        ap = nc.dram_tensor(f"in_{name}", a.shape, mybir.dt.from_np(a.dtype), kind="ExternalInput").ap()
        is_matrix = name.startswith("w_")
        aps[name] = ap[0] if is_matrix else ap
    out = nc.dram_tensor("out", (1, SEQ, D), F32, kind="ExternalOutput").ap()
    x_saved = nc.dram_tensor("x_saved", (SEQ, D), F32, kind="Internal").ap()
    y_saved = nc.dram_tensor("y_saved", (SEQ, D), F32, kind="Internal").ap()
    two_blocks(nc, aps, out, x_saved, y_saved, stop=STOP)
    r = _run(nc, [arrays], core_ids=[0])
    return r.results[0]["out"]
```

```python
import math
from contextlib import ExitStack

import concourse.bass as bass
from concourse import mybir

F32 = mybir.dt.float32
F32R = mybir.dt.float32r
I32 = mybir.dt.int32
ALU = mybir.AluOpType
ACT = mybir.ActivationFunctionType
AX = mybir.AxisListType

P = 128
D = 1024
DC = D // P
SEQ = 512
TB = SEQ // P
N_MEM = 256
MB = N_MEM // P
BANKS = 8
BANK = 512
EPS = 1e-6
HEAD = 64
HALF = HEAD // 2
A_HEADS, IDX_HEADS, B_HEADS = 8, 4, 4
TOPK = min(256, SEQ // 4)
X_HEADS, X_HEAD = 4, 256
D_FF = 2816
FC = D_FF // P
CONV_W = 3
LAMBDA_INIT = 0.8 - 0.6 * math.exp(-0.3 * 0)
HG_HEADS, HG_CHUNK = 8, 32
MLA_HEADS, NOPE, PE_DIM, V_DIM = 8, 128, 64, 128
Q_LORA, KV_LORA = 384, 256
LORA_CHUNKS = (Q_LORA + KV_LORA) // P
NEG = -1.0e30
TAKEN = -3.0e38

IN_TILES = ((0, 512), (512, 452), (964, 512), (1476, 512), (1988, 512))
HQ, HF, HI, HZ, CQ, CKV, KR, MZ, GLOG = 0, 1024, 2048, 3072, 4096, 4480, 4736, 4800, 5824
HALVES = ((0, 512), (512, 512))


class Weights:
    RAW, SPLIT, SIZE = 2, 3, 2048

    def __init__(self, nc, ctx):
        sb = lambda name, n, dt: ctx.enter_context(nc.sbuf_tensor(name, [P, n, self.SIZE], dt))
        self.raw = sb("weights_raw", self.RAW, F32)
        self.hi = sb("weights_rounded", self.SPLIT, F32R)
        self.lo = sb("weights_remainder", self.SPLIT, F32R)
        sem = lambda name: ctx.enter_context(nc.semaphore(name))
        self.loaded = [sem(f"weight_loaded_{i}") for i in range(self.RAW)]
        self.rounded = sem("weight_rounded")
        self.split = sem("weight_split")
        self.used = sem("weight_used")
        self.tiles = []
        self.used_at = []
        self.need = []
        self.n_loaded = self.n_rounded = self.n_split = self.n_taken = 0
        self.n_used = 0

    def plan(self, chunks, cols, pieces):
        slot = len(self.tiles) % self.RAW
        before = self.need[-self.RAW] if len(self.tiles) >= self.RAW else 0
        self.tiles.append((chunks, cols, pieces))
        self.need.append(before + 16 * len(pieces))

    def plan_rows(self, w, k_chunks, col_tiles, per=4):
        for c0, n in col_tiles:
            for k0 in range(0, k_chunks, per):
                kn = min(per, k_chunks - k0)
                src = w[k0 * P:(k0 + kn) * P, c0:c0 + n].rearrange("(k p) n -> p k n", p=P)
                self.plan(kn, n, [(None, 0, n, src)])

    def last(self):
        return len(self.tiles) - 1

    def view(self, ring, i, slots):
        kn, n, _ = self.tiles[i]
        return ring[:, i % slots, 0:kn * n].rearrange("p (k n) -> p k n", k=kn)

    def load_upto(self, sp, last):
        while self.n_loaded <= min(last, self.last()):
            i = self.n_loaded
            if i >= self.RAW:
                sp.wait_ge(self.split, i - self.RAW + 1)
            raw = self.view(self.raw, i, self.RAW)
            for k, c0, n, src in self.tiles[i][2]:
                dst = raw[:, :, :] if k is None else raw[:, k, c0:c0 + n]
                if k is not None and len(src.shape) == 3:
                    dst = dst.rearrange("p (h c) -> p h c", h=src.shape[1])
                sp.dma_start(dst, src).then_inc(self.loaded[i % self.RAW], 16)
            self.n_loaded += 1

    def round_upto(self, act, last):
        while self.n_rounded <= min(last, self.last()):
            i = self.n_rounded
            act.wait_ge(self.loaded[i % self.RAW], self.need[i])
            if i >= self.SPLIT:
                act.wait_ge(*self.used_at[i - self.SPLIT])
            act.activation(self.view(self.hi, i, self.SPLIT), self.view(self.raw, i, self.RAW),
                           ACT.Copy).then_inc(self.rounded, 1)
            self.n_rounded += 1

    def split_upto(self, pool, last):
        while self.n_split <= min(last, self.last()):
            i = self.n_split
            pool.wait_ge(self.rounded, i + 1)
            pool.tensor_tensor(self.view(self.lo, i, self.SPLIT), self.view(self.raw, i, self.RAW),
                               self.view(self.hi, i, self.SPLIT).bitcast(F32),
                               ALU.subtract).then_inc(self.split, 1)
            self.n_split += 1

    def take(self, pe, chunks, cols):
        i = self.n_taken
        assert self.tiles[i][:2] == (chunks, cols), (i, self.tiles[i][:2], chunks, cols)
        pe.wait_ge(self.split, i + 1)
        self.n_taken += 1
        return self.view(self.hi, i, self.SPLIT), self.view(self.lo, i, self.SPLIT)

    def release(self, ins, sem=None, value=None):
        if sem is None:
            self.n_used += 1
            ins.then_inc(self.used, 1)
            sem, value = self.used, self.n_used
        self.used_at.append((sem, value))


class Core:

    def __init__(self, nc, ctx):
        self.nc = nc
        self.w = Weights(nc, ctx)
        self.bank = [ctx.enter_context(nc.psum_tensor(f"bank{i}", [P, BANK], F32))
                     for i in range(BANKS)]
        sem = lambda name: ctx.enter_context(nc.semaphore(name))
        self.ready = sem("product_ready")
        self.freed = sem("product_read")
        self.groups = 0
        self.xh = ctx.enter_context(nc.sbuf_tensor("columns_rounded", [P, DC, SEQ], F32R))
        self.xl = ctx.enter_context(nc.sbuf_tensor("columns_remainder", [P, DC, SEQ], F32R))
        self.sems = []
        self.n_sems = 0

    def sem(self, name):
        self.n_sems += 1
        s = self.nc.alloc_semaphore(name=f"{name}_{self.n_sems}")
        self.sems.append(s)
        return s

    def recycle(self):
        self.nc.clear_and_free_semaphores(self.sems)
        self.sems = []
        self.nc.all_engine_barrier()

    def bank_of(self, g):
        return self.bank[self.first_bank + g % (BANKS - self.first_bank)]

    def wait_bank(self, pe, g):
        n = BANKS - self.first_bank
        if g >= n:
            pe.wait_ge(self.freed, self.groups_at_start + g - n + 1)

    def products_by_rows(self, pe, g, *args, **kw):
        for g in self.product_steps(pe, g, *args, **kw):
            pass
        return g

    def product_steps(self, pe, g, k_chunks, col_tiles, rows=TB, per=4, x0=0, columns=None):
        for c0, n in col_tiles:
            for k0 in range(0, k_chunks, per):
                kn = min(per, k_chunks - k0)
                hi, lo = self.w.take(pe, kn, n)
                final = k0 + kn == k_chunks
                for tb in range(rows):
                    if k0 == 0:
                        self.wait_bank(pe, g + tb)
                    for k in range(kn):
                        if columns is not None and c0 == col_tiles[0][0] and tb == 0:
                            pe.wait_ge(columns.remainder, k0 + k + 1)
                        xs = (slice(None), x0 + k0 + k, slice(tb * P, (tb + 1) * P))
                        for a, b in ((self.xh, hi), (self.xh, lo), (self.xl, hi)):
                            last = k == kn - 1 and b is hi and a is self.xl
                            ins = pe.matmul(self.bank_of(g + tb)[:, 0:n], a[xs], b[:, k, :],
                                            start=(k0 + k == 0 and b is hi and a is self.xh),
                                            stop=(final and last))
                        if k < kn - 1:
                            yield g
                    if final:
                        ins.then_inc(self.ready, 1)
                        self.groups += 1
                    if tb < rows - 1:
                        yield g
                if final:
                    self.w.release(ins, self.ready, self.groups)
                    g += rows
                else:
                    self.w.release(ins)
                yield g

    def copy_steps(self, act, g, k_chunks, jobs, rows=TB, per=4):
        done = 0
        parts = -(-k_chunks // per)
        late = None
        for target, tiles in jobs:
            at = 0
            for _, n in tiles:
                for k in range(parts):
                    self.w.round_upto(act, self.tile0 + done + 2)
                    for tb in range(rows):
                        if late is not None:
                            self.copy_group(act, *late)
                            late = None
                        if k == parts - 1:
                            late = (g, target[:, tb, at:at + n], n)
                            g += 1
                        yield
                    done += 1
                at += n
        self.copy_group(act, *late)
        self.w.round_upto(act, self.ahead(done))

    def copy_group(self, act, g, dst, n):
        self.wait_group(act, g)
        act.activation(dst, self.bank_of(g)[:, 0:n], ACT.Copy).then_inc(self.freed, 1)

    def products_by_columns(self, pe, g, k_chunks, cols, x0=0, columns=None):
        hi, lo = self.w.take(pe, k_chunks, cols)
        for c in range(cols // P):
            self.wait_bank(pe, g)
            for k in range(k_chunks):
                if columns is not None and c == 0:
                    pe.wait_ge(columns.remainder, k + 1)
                ws = (slice(None), k, slice(c * P, (c + 1) * P))
                for n, (a, b) in enumerate(((hi, self.xh), (lo, self.xh), (hi, self.xl))):
                    ins = pe.matmul(self.bank_of(g)[:, :], a[ws], b[:, x0 + k, :],
                                    start=(k == 0 and n == 0), stop=(k == k_chunks - 1 and n == 2))
            ins.then_inc(self.ready, 1)
            self.groups += 1
            g += 1
        self.w.release(ins, self.ready, self.groups)
        return g

    def stage(self, ctx, first_bank=0):
        self.first_bank = first_bank
        self.groups_at_start = self.groups
        self.tile0 = self.w.n_taken
        return ctx.enter_context(self.nc.Block())

    def ahead(self, n_tiles):
        return self.tile0 + n_tiles - 1 + self.w.SPLIT - 1

    def stream(self, block, n_tiles, moves=()):
        last = self.ahead(n_tiles)
        moved = self.sem("moved") if moves else None

        @block.sync
        def _(sp):
            for dst, src in moves:
                sp.dma_start(dst, src).then_inc(moved, 16)
            self.w.load_upto(sp, last + self.w.RAW)
            if moves:
                sp.wait_ge(moved, 16 * len(moves))

        @block.gpsimd
        def _(pool):
            self.w.split_upto(pool, last)

    def wait_group(self, eng, g):
        eng.wait_ge(self.ready, self.groups_at_start + g + 1)


def paced(steps, rounds):
    for _ in steps:
        for _round in range(rounds):
            yield


def together(*generators):
    running = list(generators)
    while running:
        running = [g for g in running if next(g, running) is not running]
        yield


class Turn:

    def __init__(self, eng, sem):
        self.eng, self.sem, self.n = eng, sem, 0

    def __call__(self, ins):
        ins.then_inc(self.sem, 1)
        self.n += 1
        return ins

    def wait(self):
        if self.n:
            self.eng.wait_ge(self.sem, self.n)


def transfer(core, block, moves):
    if not moves:
        return
    moved = core.sem("moved")

    @block.sync
    def _(sp):
        for dst, src in moves:
            sp.dma_start(dst, src).then_inc(moved, 16)
        sp.wait_ge(moved, 16 * len(moves))


class Columns:

    def __init__(self, core, src, gain=None, rows=TB, norm=None, width=D, x0=0, by_head=False,
                 first_bank=0, bank_wait=None, rows_ready=None):
        self.core, self.src, self.gain, self.rows, self.width = core, src, gain, rows, width
        self.x0, self.by_head, self.norm, self.chunks = x0, by_head, norm, width // P
        self.per_bank = TB // rows
        n = rows * P
        self.bank = lambda c: core.bank[(first_bank + c // self.per_bank) % BANKS]\
            [:, c % self.per_bank * n:(c % self.per_bank + 1) * n]
        self.bank_wait = bank_wait
        self.rows_ready = rows_ready
        self.turned, self.rounded, self.remainder = (core.sem(n) for n in (
            "turned", "rounded", "remainder"))
        self.y = src
        if norm is not None:
            self.squared, self.mean, self.rooted, self.scaled = (core.sem(n) for n in (
                "squared", "mean", "rooted", "scaled"))
            self.y, small = norm
            self.rows_ready = (self.scaled, 0)
            self.ss, self.rms, self.rstd = (small[:, 4 * i:4 * i + rows] for i in range(3))

    def tensor(self, pe):
        for c in range(self.chunks):
            if self.bank_wait is not None:
                self.bank_wait(pe, c)
            for tb in range(self.rows):
                if self.rows_ready is not None and c == 0:
                    pe.wait_ge(self.rows_ready[0], self.rows_ready[1] + tb + 1)
                rows_in = self.y[:, c, tb * P:(tb + 1) * P] if self.by_head \
                    else self.y[:, tb, c * P:(c + 1) * P]
                ins = pe.transpose(self.bank(c)[:, tb * P:(tb + 1) * P], rows_in,
                                   self.core.ident[:, :])
            ins.then_inc(self.turned, 1)

    def scalar_norm(self, act):
        for tb in range(self.rows):
            act.activation(self.y[:, tb, 0:self.width], self.src[:, tb, :], ACT.Square,
                           accum_out=self.ss[:, tb:tb + 1]).then_inc(self.squared, 1)
        act.wait_ge(self.mean, 1)
        act.activation(self.rms, self.ss, ACT.Sqrt).then_inc(self.rooted, 1)

    def scalar(self, act):
        if self.norm is not None:
            self.scalar_norm(act)
        self.scalar_round(act)

    def scalar_round(self, act):
        for c in range(self.chunks):
            act.wait_ge(self.turned, (c // self.per_bank + 1) * self.per_bank)
            act.activation(self.core.xh[:, self.x0 + c, 0:self.rows * P], self.bank(c), ACT.Copy,
                           scale=1.0 if self.gain is None else self.gain[:, c:c + 1])\
               .then_inc(self.rounded, 1)

    def vector_norm(self, dve):
        dve.wait_ge(self.squared, self.rows)
        dve.tensor_scalar(self.ss, self.ss, 1.0 / self.width, EPS, ALU.mult, ALU.add)\
           .then_inc(self.mean, 1)
        dve.wait_ge(self.rooted, 1)
        dve.reciprocal(self.rstd, self.rms).then_inc(self.mean, 1)
        dve.wait_ge(self.mean, 2)
        for tb in range(self.rows):
            dve.tensor_scalar(self.y[:, tb, 0:self.width], self.src[:, tb, :],
                              self.rstd[:, tb:tb + 1], None, ALU.mult).then_inc(self.scaled, 1)

    def vector(self, dve):
        if self.norm is not None:
            self.vector_norm(dve)
        self.vector_split(dve)

    def vector_split(self, dve):
        for c in range(self.chunks):
            dve.wait_ge(self.rounded, (c // self.per_bank + 1) * self.per_bank)
            hi = self.core.xh[:, self.x0 + c, 0:self.rows * P].bitcast(F32)
            lo = self.core.xl[:, self.x0 + c, 0:self.rows * P]
            bank = self.bank(c)
            if self.gain is None:
                dve.tensor_tensor(lo, bank, hi, ALU.subtract).then_inc(self.remainder, 1)
            else:
                dve.scalar_tensor_tensor(lo, bank, self.gain[:, c:c + 1], hi,
                                         ALU.mult, ALU.subtract).then_inc(self.remainder, 1)


class RowNorm:

    def __init__(self, core, x, y, small, gain=None):
        self.core, self.x, self.y, self.gain = core, x, y, gain
        self.added, self.at_start = core.freed, core.groups_at_start
        self.ss, self.mean, self.rms, self.rstd = (
            small[:, 0:8], small[:, 8:12], small[:, 12:16], small[:, 16:20])
        self.warm = small[:, 20:21]
        self.squared, self.halfway, self.meaned, self.rooted, self.inverse, self.scaled = (
            core.sem(n) for n in ("squared", "halfway", "mean", "rooted", "inverse", "scaled"))

    def scalar(self, act, half):
        for tb in range(TB):
            g = half * TB + tb
            cols = slice(half * BANK, (half + 1) * BANK)
            act.wait_ge(self.added, self.at_start + g + 1)
            act.activation(self.y[:, tb, cols], self.x[:, tb, cols], ACT.Square,
                           accum_out=self.ss[:, g:g + 1]).then_inc(self.squared, 1)
            if half and tb:
                self._root(act, tb - 1)
        if half:
            self._root(act, TB - 1)
        else:
            act.activation(self.warm, self.core.ident[:, 0:1], ACT.Sqrt)

    def _root(self, act, tb):
        act.wait_ge(self.meaned, tb + 1)
        act.activation(self.rms[:, tb:tb + 1], self.mean[:, tb:tb + 1], ACT.Sqrt).then_inc(self.rooted, 1)

    def vector_halfway(self, dve):
        dve.wait_ge(self.squared, TB)
        dve.tensor_scalar(self.ss[:, 0:TB], self.ss[:, 0:TB], 1.0 / D, EPS, ALU.mult, ALU.add)\
           .then_inc(self.halfway, 1)
        dve.wait_ge(self.halfway, 1)

    def vector_mean(self, dve, tb):
        dve.wait_ge(self.squared, TB + tb + 1)
        dve.scalar_tensor_tensor(self.mean[:, tb:tb + 1], self.ss[:, TB + tb:TB + tb + 1], 1.0 / D,
                                 self.ss[:, tb:tb + 1], ALU.mult, ALU.add).then_inc(self.meaned, 1)

    def vector_scale(self, dve, tb):
        dve.wait_ge(self.rooted, tb + 1)
        rstd = self.rstd[:, tb:tb + 1]
        dve.reciprocal(rstd, self.rms[:, tb:tb + 1]).then_inc(self.inverse, 1)
        dve.wait_ge(self.inverse, tb + 1)
        if self.gain is None:
            dve.tensor_scalar(self.y[:, tb, :], self.x[:, tb, :], rstd, None,
                              ALU.mult).then_inc(self.scaled, 1)
        else:
            dve.scalar_tensor_tensor(self.y[:, tb, :], self.x[:, tb, :], rstd, self.gain,
                                     ALU.mult, ALU.mult).then_inc(self.scaled, 1)


def add_groups(core, dve, target, norm=None):
    for g in range(2 * TB):
        half, tb = divmod(g, TB)
        core.wait_group(dve, g)
        t = target[:, tb, half * BANK:(half + 1) * BANK]
        dve.tensor_tensor(t, core.bank_of(g)[:, :], t, ALU.add).then_inc(core.freed, 1)
        if norm is None or not half:
            continue
        if tb == 0:
            norm.vector_halfway(dve)
        else:
            norm.vector_mean(dve, tb - 1)
        if tb >= 2:
            norm.vector_scale(dve, tb - 2)
    if norm is not None:
        norm.vector_mean(dve, TB - 1)
        norm.vector_scale(dve, TB - 2)
        norm.vector_scale(dve, TB - 1)


class Turns:

    def __init__(self, core, moves, gains=None, groups=0):
        self.core, self.moves, self.groups = core, moves, groups
        self.gains = gains or [1.0] * len(moves)
        self.turned, self.by_act, self.by_dve = (core.sem(n) for n in (
            "turned", "copied_act", "copied_dve"))

    def bank(self, m):
        return self.core.bank[(self.groups + m) % BANKS]

    def tensor(self, pe, ready=None):
        for m, (src, blocks, _) in enumerate(self.moves):
            if m >= BANKS:
                pe.wait_ge((self.by_act, self.by_dve)[m % 2], (m - BANKS) // 2 + 1)
            elif self.groups:
                pe.wait_ge(self.core.freed, self.core.groups_at_start + self.groups - BANKS + m + 1)
            if ready is not None:
                ready(pe, m)
            for tb in range(blocks):
                ins = pe.transpose(self.bank(m)[:, tb * P:(tb + 1) * P], src(tb), self.core.ident[:, :])
            ins.then_inc(self.turned, 1)

    def scalar(self, act):
        for m in range(0, len(self.moves), 2):
            act.wait_ge(self.turned, m + 1)
            act.activation(self.moves[m][2], self.bank(m)[:, 0:self.moves[m][1] * P], ACT.Copy,
                           scale=self.gains[m]).then_inc(self.by_act, 1)

    def vector(self, dve):
        for m in range(1, len(self.moves), 2):
            dve.wait_ge(self.turned, m + 1)
            dve.tensor_scalar(self.moves[m][2], self.bank(m)[:, 0:self.moves[m][1] * P],
                              self.gains[m], None, ALU.mult).then_inc(self.by_dve, 1)


def turn_heads(core, moves, clear=()):
    with ExitStack() as ctx:
        block = core.stage(ctx)
        turns, cleared = Turns(core, moves), core.sem("cleared")

        @block.gpsimd
        def _(pool):
            for part in clear:
                pool.memset(part, 0.0).then_inc(cleared, 1)

        @block.tensor
        def _(pe):
            turns.tensor(pe)

        @block.scalar
        def _(act):
            turns.scalar(act)

        @block.vector
        def _(dve):
            turns.vector(dve)


def attention(core, units, scale, buf, beside=None, transfers=(), bias_ready=None):
    probs, turned_sb, small = buf
    S_RING, T_RING = (3, 2) if beside is None else (2, 2)
    P_SLOTS, T_SLOTS = probs.shape[1], turned_sb.shape[1]
    n = len(units)
    S = core.bank[0:S_RING]
    T = core.bank[S_RING:S_RING + T_RING]
    O = core.bank[S_RING + T_RING:S_RING + 2 * T_RING]
    peak, sums = small[:, 0:n], small[:, n:2 * n]
    with ExitStack() as ctx:
        names = ("scores_ready", "biased", "peak_ready", "weights_ready", "turned_ready",
                 "turned_copied", "values_ready", "finished", "finish_step")
        (scores_ready, biased, peak_ready, weights_ready, turned_ready,
         turned_copied, values_ready, finished, finish_step) = (core.sem(x) for x in names)
        block = core.stage(ctx, first_bank=0 if beside is None else 6)
        more = beside or {}
        if "tiles" not in more:
            transfer(core, block, transfers)

        @block.tensor
        def _(pe):
            other = more["tensor"](pe) if "tensor" in more else iter(())
            for i in range(n + 3):
                for s in ((0, 1) if i == 0 else (i + 1,)):
                    if s >= n:
                        continue
                    pairs, keys = units[s][:2]
                    if s >= S_RING:
                        pe.wait_ge(biased, s - S_RING + 1)
                    for m, (q, k) in enumerate(pairs):
                        ins = pe.matmul(S[s % S_RING][:, 0:keys], q, k, start=(m == 0),
                                        stop=(m == len(pairs) - 1))
                    ins.then_inc(scores_ready, 1)
                j = i - 2
                if 0 <= j < n:
                    pe.wait_ge(weights_ready, j + 1)
                    if j >= T_RING:
                        pe.wait_ge(turned_copied, j - T_RING + 1)
                    for c in range(units[j][1] // P):
                        ins = pe.transpose(T[j % T_RING][:, c * P:(c + 1) * P],
                                           probs[:, j % P_SLOTS, c * P:(c + 1) * P], core.ident[:, :])
                    ins.then_inc(turned_ready, 1)
                j = i - 3
                if 0 <= j < n:
                    _, keys, _, values, width, _ = units[j]
                    pe.wait_ge(turned_copied, j + 1)
                    if j >= T_RING:
                        pe.wait_ge(finished, j - T_RING + 1)
                    for c in range(keys // P):
                        ins = pe.matmul(O[j % T_RING][:, 0:width],
                                        turned_sb[:, j % T_SLOTS, c * P:(c + 1) * P], values(c),
                                        start=(c == 0), stop=(c == keys // P - 1))
                    ins.then_inc(values_ready, 1)
                next(other, None)
            for _step in other:
                pass

        if "tiles" in more:
            core.stream(block, more["tiles"], moves=transfers)

        @block.vector
        def _(dve):
            turn = Turn(dve, finish_step)
            other = more["vector"](dve) if "vector" in more else iter(())
            for i in range(n + 3):
                if i < n:
                    keys, bias = units[i][1:3]
                    if bias_ready is not None:
                        bias_ready(dve, i)
                    dve.wait_ge(scores_ready, i + 1)
                    if i >= P_SLOTS:
                        dve.wait_ge(turned_ready, i - P_SLOTS + 1)
                    dve.tensor_tensor_reduce(
                        out=probs[:, i % P_SLOTS, 0:keys], in0=S[i % S_RING][:, 0:keys], in1=bias,
                        scale=scale(i) if callable(scale) else scale, scalar=-3.0e38,
                        op0=ALU.add, op1=ALU.max, accum_out=peak[:, i:i + 1]).then_inc(biased, 1)
                    dve.wait_ge(biased, i + 1)
                    dve.tensor_scalar(peak[:, i:i + 1], peak[:, i:i + 1], -1.0, None,
                                      ALU.mult).then_inc(peak_ready, 1)
                j = i - 3
                if 0 <= j < n:
                    dve.wait_ge(values_ready, j + 1)
                    if j:
                        dve.wait_ge(finished, j)
                    ins = units[j][5](dve, turn, j, sums[:, j:j + 1],
                                      O[j % T_RING][:, 0:units[j][4]])
                    ins.then_inc(finished, 1)
                next(other, None)
            for _step in other:
                pass

        @block.scalar
        def _(act):
            other = more["scalar"](act) if "scalar" in more else iter(())
            for i in range(n + 3):
                j = i - 2
                if 0 <= j < n:
                    keys = units[j][1]
                    act.wait_ge(turned_ready, j + 1)
                    if j >= T_SLOTS:
                        act.wait_ge(values_ready, j - T_SLOTS + 1)
                    act.activation(turned_sb[:, j % T_SLOTS, 0:keys], T[j % T_RING][:, 0:keys],
                                   ACT.Copy).then_inc(turned_copied, 1)
                if i < n:
                    keys = units[i][1]
                    act.wait_ge(peak_ready, i + 1)
                    p = probs[:, i % P_SLOTS, 0:keys]
                    act.activation(p, p, ACT.Exp, bias=peak[:, i:i + 1],
                                   accum_out=sums[:, i:i + 1]).then_inc(weights_ready, 1)
                next(other, None)
            for _step in other:
                pass


def add_product(core, source, target, norm=None, final=None):
    with ExitStack() as ctx:
        block = core.stage(ctx)
        columns = Columns(core, *source[0], **source[1])
        rows_norm = RowNorm(core, target, *norm, gain=final and final[0]) if norm else None

        @block.tensor
        def _(pe):
            columns.tensor(pe)
            core.products_by_rows(pe, 0, DC, HALVES, columns=columns)

        if final is None:
            core.stream(block, 4)
        else:
            gain, gain_source, out, out_stored = final
            gain_in = core.sem("gain_in")

            @block.sync
            def _(sp):
                sp.dma_start(gain, gain_source).then_inc(gain_in, 16)
                core.w.load_upto(sp, core.ahead(4) + core.w.RAW)
                for tb in range(TB):
                    sp.wait_ge(rows_norm.scaled, tb + 1)
                    sp.dma_start(out[:, tb, :], rows_norm.y[:, tb, :]).then_inc(out_stored, 16)
                sp.wait_ge(out_stored, 16 * TB)

            @block.gpsimd
            def _(pool):
                core.w.split_upto(pool, core.ahead(4))

        @block.scalar
        def _(act):
            columns.scalar(act)
            core.w.round_upto(act, core.tile0 + 3)
            if rows_norm is not None:
                rows_norm.scalar(act, 0)
            core.w.round_upto(act, core.ahead(4))
            if rows_norm is not None:
                rows_norm.scalar(act, 1)

        @block.vector
        def _(dve):
            columns.vector(dve)
            if final is not None:
                dve.wait_ge(gain_in, 16)
            add_groups(core, dve, target, rows_norm)


class LowRank:

    def __init__(self, core, small, g0, rows, gain, x0, first_bank, at):
        self.core, self.g0, self.rows, self.width = core, g0, rows, rows.shape[2]
        self.squared, self.meaned, self.rooted, self.inverse = (
            core.sem(s) for s in ("squared", "mean", "rooted", "inverse"))
        self.ss, self.rms, self.rstd = (small[:, at + 4 * i:at + 4 * i + 4] for i in range(3))
        self.columns = Columns(core, rows, gain, width=self.width, x0=x0,
                               first_bank=first_bank,
                               rows_ready=(core.freed, core.groups_at_start + g0))

    def square(self, act, tb):
        self.core.wait_group(act, self.g0 + tb)
        act.activation(self.rows[:, tb, :], self.core.bank_of(self.g0 + tb)[:, 0:self.width],
                       ACT.Square, accum_out=self.ss[:, tb:tb + 1]).then_inc(self.squared, 1)

    def root(self, act):
        act.wait_ge(self.meaned, 1)
        act.activation(self.rms, self.ss, ACT.Sqrt).then_inc(self.rooted, 1)

    def scale(self, dve):
        dve.wait_ge(self.squared, TB)
        dve.tensor_scalar(self.ss, self.ss, 1.0 / self.width, EPS, ALU.mult, ALU.add)\
           .then_inc(self.meaned, 1)
        dve.wait_ge(self.rooted, 1)
        dve.reciprocal(self.rstd, self.rms).then_inc(self.inverse, 1)
        dve.wait_ge(self.inverse, 1)
        for tb in range(TB):
            dve.tensor_scalar(self.rows[:, tb, :], self.core.bank_of(self.g0 + tb)[:, 0:self.width],
                              self.rstd[:, tb:tb + 1], None, ALU.mult).then_inc(self.core.freed, 1)


def rope(dve, turn, x, heads, tables, t1, t2, rows=TB, done=None):
    ca, cb, sa, sb = tables
    v = x.rearrange("p t (h d) -> p t h d", h=heads)
    x1, x2 = v[:, :, :, 0:HALF], v[:, :, :, HALF:HEAD]
    wide = lambda a: a.unsqueeze(2).to_broadcast([P, rows, heads, HALF])
    t1 = t1[:, 0:rows * heads * HALF].rearrange("p (t h d) -> p t h d", t=rows, h=heads)
    t2 = t2[:, 0:rows * heads * HALF].rearrange("p (t h d) -> p t h d", t=rows, h=heads)
    turn.wait()
    turn(dve.tensor_tensor(t1, x2, wide(sb), ALU.mult))
    turn(dve.tensor_tensor(t2, x1, wide(sa), ALU.mult))
    turn(dve.tensor_tensor(x1, x1, wide(ca), ALU.mult))
    turn(dve.tensor_tensor(x2, x2, wide(cb), ALU.mult))
    turn.wait()
    done = done or turn
    done(dve.tensor_tensor(x1, x1, t1, ALU.subtract))
    done(dve.tensor_tensor(x2, x2, t2, ALU.add))
    done.wait()


def plan_weights(w, t):
    w.plan_rows(t["w_in"], DC, IN_TILES)
    for name in ("w_xk", "w_xv", "w_out", "w_xq", "w_xo"):
        w.plan_rows(t[name], DC, HALVES)
    for c in range(FC // 2):
        for c0 in (c * 2 * P, D_FF + c * 2 * P):
            w.plan_rows(t["w_ffn_in"], DC, ((c0, 2 * P),), per=DC)
    for k0 in range(0, FC, 4):
        w.plan_rows(t["w_ffn_out"][k0 * P:min(FC, k0 + 4) * P, :], min(4, FC - k0), HALVES)
    w.plan_rows(t["w_in_2"], DC, [(c, 2 * P) for c in range(HQ, HI, 2 * P)], per=DC)
    w.plan_rows(t["w_in_2"], DC, ((HI, 512), (HI + 512, 512)))
    w.plan_rows(t["w_in_2"], DC, ((HZ, 512), (HZ + 512, 512)))
    w.plan_rows(t["w_in_2"], DC, ((CQ, 384), (CKV, 320)))
    uq = t["w_uq_2"].rearrange("(k p) (h c) -> p k h c", p=P, c=NOPE + PE_DIM)
    for h0 in (0, 4):
        w.plan(3, 4 * NOPE, [(k, 0, 4 * NOPE, uq[:, k, h0:h0 + 4, 0:NOPE]) for k in range(3)])
    w.plan(3, 8 * PE_DIM, [(k, 0, 8 * PE_DIM, uq[:, k, :, NOPE:NOPE + PE_DIM]) for k in range(3)])
    ukv = t["w_ukv_2"].rearrange("(k p) (h c) -> p k h c", p=P, c=NOPE + V_DIM)
    w.plan(2, 8 * NOPE, [(k, 0, 8 * NOPE, ukv[:, k, :, 0:NOPE]) for k in range(2)])
    for h0 in (0, 4):
        w.plan(2, 4 * V_DIM, [(k, 0, 4 * V_DIM, ukv[:, k, h0:h0 + 4, NOPE:NOPE + V_DIM])
                              for k in range(2)])
    w.plan_rows(t["w_in_2"], DC, ((MZ, 512), (MZ + 512, 512)))
    w.plan_rows(t["w_in_2"], DC, [(GLOG + 512 * c, 512) for c in range(4)])
    for name in ("w_proj_a_2", "w_proj_b_2", "w_out_2"):
        w.plan_rows(t[name], DC, HALVES)


def two_blocks(nc, t, out, x_saved, y_saved, columns_saved):
    ctx = ExitStack()
    with ctx:
        sb = lambda name, shape, dt=F32: ctx.enter_context(nc.sbuf_tensor(name, shape, dt))
        core = Core(nc, ctx)
        plan_weights(core.w, t)
        ident = core.ident = sb("identity", [P, P])
        causal = sb("causal", [P, BANK])
        mask32 = sb("chunk_mask", [P, P])
        vectors = sb("column_vectors", [P, 160])
        trig = sb("trig", [P, 2, 2 * TB * HALF])
        small = sb("small", [P, 160])
        lower = sb("lower_bound", [P, 2 * HG_HEADS])
        neg_lambda = sb("neg_lambda", [P, 4])
        decay = sb("decay", [P, HG_HEADS, SEQ // HG_CHUNK])
        arena = sb("arena", [P, 24704])
        out_stored = ctx.enter_context(nc.semaphore("out_stored"))

        def view(at, *dims):
            n = 1
            for d in dims:
                n *= d
            a = arena[:, at:at + n]
            if len(dims) == 2:
                return a.rearrange("p (a b) -> p a b", a=dims[0])
            return a

        g_mix, g_xattn, g_mem, g_ffn, g_second = (vectors[:, 8 * i:8 * i + 8] for i in range(5))
        conv_w, conv_b = vectors[:, 40:106], vectors[:, 106:128]
        q_a_gain, kv_a_gain, lb_logits = vectors[:, 128:131], vectors[:, 131:133], vectors[:, 133:149]
        hg_gain, xqk_gain = vectors[:, 153:154], vectors[:, 154:156]

        def by_chunk(name):
            return t[name].rearrange("l (c p) -> (l c) p", p=P)

        def over_partitions(v):
            return v[0, :].partition_broadcast(P)

        x = view(0, TB, D)
        x_normed = view(4096, TB, D)
        rows_g, rows_v = view(20992, P), view(21120, 2, P)
        position = arena[:, 8576:8584]
        positions_i = arena[:, 8584:8592].bitcast(I32)
        inv_freq = arena[:, 8592:8624]
        angle = view(8704, 2, 2 * TB * HALF)
        angle_turns = view(9216, 2, 2 * TB * HALF)
        logit_numbers = arena[:, 3856:3872]
        gains = view(20480, 4, HEAD)
        lams = view(20736, 4, HEAD)
        tables = arena[:, 14336:16384].rearrange("p (g k n) -> p g k n", g=4, k=4)

        def table_views(i):
            return [tables[:, i, k, :].rearrange("p (t f) -> p t f", f=HALF) for k in range(4)]

        def plain_tables(which):
            s, c_ = (trig[:, k, which * TB * HALF:(which + 1) * TB * HALF]
                     .rearrange("p (t f) -> p t f", f=HALF) for k in (0, 1))
            return (c_, c_, s, s)

        qa, mixed, qb, kb, vb = (view(at, TB, n) for at, n in
                                 ((0, 512), (2048, 452), (4096, 512), (6144, 512), (8192, 512)))
        squares = view(10240, TB, 512)
        t1, t2 = view(12288, 1024), view(13312, 1024)
        targets = (qa, mixed, qb, kb, vb)
        normed_heads = {0: (qa, 8), 1: (mixed[:, :, 0:HEAD], 1), 2: (qb, 8), 3: (kb, 8)}
        qaT, qbT, kbT = view(16384, 4, SEQ), view(18432, 4, SEQ), view(20480, 4, SEQ)
        kaT, kiT, qiT = view(22528, SEQ), view(23040, SEQ), view(23552, 2, SEQ)
        mem, mem_scratch = view(10240, MB, D), view(6144, MB, D)
        keys_twice = [view(24576 - 1024 + 512 * i, TB, P) for i in range(2)]
        with ExitStack() as c:
            squared, meaned, rooted, step = (core.sem(s) for s in ("squared", "mean", "rooted", "step"))
            rotated, twice, turned, copied, mem_in = (core.sem(s) for s in (
                "rotated", "twice", "turned", "copied", "mem_in"))
            loaded, made, ready_ang, sined, lam_exp, exped, freq_set, cleared = (core.sem(s) for s in (
                "loaded", "made", "angles", "sined", "lam_exp", "exped", "freq_set", "cleared"))
            g_in, g_turned, g_copied = (core.sem(s) for s in ("g_mix_in", "g_mix_turned", "g_mix_copied"))
            x_in = [core.sem(f"x_in_{tb}") for tb in range(TB)]
            x_squared, x_mean, x_rooted, x_inverse, x_scaled = (core.sem(s) for s in (
                "x_squared", "x_mean", "x_rooted", "x_inverse", "x_scaled"))
            N_LOADS = 21
            block = core.stage(c)
            columns = Columns(core, x_normed, g_mix, rows_ready=(x_scaled, 0),
                              bank_wait=lambda pe, c_: c_ or pe.wait_ge(g_copied, 1))
            turns = [(rows_v, vectors[:, 8:154], (loaded, 16 * N_LOADS))]
            turns += [(qa[:, :, q * P:(q + 1) * P], qaT[:, q, :], (rotated, 2)) for q in range(4)]
            turns += [(keys_twice[i], dst, (twice, 4)) for i, dst in enumerate((kaT, kiT))]
            turns += [(mixed[:, :, (2 + 2 * q) * HEAD:(4 + 2 * q) * HEAD], qiT[:, q, :], (rotated, 6))
                      for q in range(2)]
            turns += [(qb[:, :, q * P:(q + 1) * P], qbT[:, q, :], (rotated, 8)) for q in range(4)]
            turns += [(kb[:, :, q * P:(q + 1) * P], kbT[:, q, :], (rotated, 10)) for q in range(4)]

            @block.tensor
            def _(pe):
                pe.wait_ge(made, 2)
                pe.wait_ge(g_in, 16)
                pe.transpose(core.bank[BANKS - 1][:, 0:P], rows_g, ident[:, :]).then_inc(g_turned, 1)
                columns.tensor(pe)
                core.products_by_rows(pe, 0, DC, IN_TILES, columns=columns)
                groups = TB * len(IN_TILES)
                for i, (src, _, rows_ready) in enumerate(turns):
                    pe.wait_ge(*rows_ready)
                    if i < BANKS:
                        pe.wait_ge(core.freed, core.groups_at_start + groups - BANKS + i + 1)
                    else:
                        pe.wait_ge(copied, i - BANKS + 1)
                    for tb in range(src.shape[1]):
                        ins = pe.transpose(core.bank[(groups + i) % BANKS][:, tb * P:(tb + 1) * P],
                                           src[:, tb, :], ident[:, :])
                    ins.then_inc(turned, 1)

            @block.sync
            def _(sp):
                core.w.load_upto(sp, 0)
                sp.wait_ge(cleared, 1)
                sp.dma_start(rows_g[0:DC, :], by_chunk("g_mix")).then_inc(g_in, 16)
                sp.wait_ge(x_in[TB - 1], 16)
                core.w.load_upto(sp, 1)
                sp.dma_start(positions_i[:, 0:4], t["positions"].rearrange("l (t p) -> p (l t)", p=P),
                              allow_slow_non_contiguous=True)\
                   .then_inc(loaded, 16)
                for i, name in enumerate(("g_qa", "g_ka", "g_qb", "g_kb")):
                    sp.dma_start(gains[:, i, :], over_partitions(t[name])).then_inc(loaded, 16)
                for i, name in enumerate(("lam_q1", "lam_k1", "lam_q2", "lam_k2")):
                    sp.dma_start(lams[:, i, :], over_partitions(t[name])).then_inc(loaded, 16)
                at = DC
                for name, src in (("g_xattn", by_chunk("g_xattn")),
                                  ("g_mem", by_chunk("g_mem")), ("g_ffn", by_chunk("g_ffn")),
                                  ("norm_g_2", by_chunk("norm_g_2")),
                                  ("conv_w", t["conv_w"].rearrange("l j (c p) -> (l j c) p", p=P)),
                                  ("conv_b", by_chunk("conv_b"))):
                    n = src.shape[0]
                    sp.dma_start(rows_v[at:at + n, 0, :], src).then_inc(loaded, 16)
                    at += n
                at = 0
                for name in ("q_a_g_2", "kv_a_g_2", "lb_logits_2", "g_xq", "g_xk", "hg_norm_g_2"):
                    src = by_chunk(name)
                    sp.dma_start(rows_v[at:at + src.shape[0], 1, :], src).then_inc(loaded, 16)
                    at += src.shape[0]
                core.w.load_upto(sp, core.tile0 + 9)
                sp.wait_ge(meaned, 7)
                sp.dma_start(mem, t["mem"].rearrange("l (t p) d -> p (l t) d", p=P)).then_inc(mem_in, 16)
                core.w.load_upto(sp, core.ahead(10) + core.w.RAW)
                sp.wait_ge(mem_in, 16)

            @block.gpsimd
            def _(pool):
                pool.memset(ident[:, :], 0.0).then_inc(made, 1)
                pool.wait_ge(made, 1)
                pool.affine_select(out=ident[:, :], in_=ident[:, :], compare_op=ALU.not_equal, fill=1.0,
                                   base=0, pattern=[[-1, P]], channel_multiplier=1).then_inc(made, 1)
                pool.memset(causal[:, :], 0.0).then_inc(made, 1)
                pool.memset(mask32[:, :], 1.0).then_inc(made, 1)
                pool.wait_ge(made, 4)
                diagonal = causal[:, 3 * P:4 * P]
                pool.affine_select(out=diagonal, in_=diagonal, compare_op=ALU.is_ge, fill=NEG,
                                   base=0, pattern=[[-1, P]], channel_multiplier=1).then_inc(made, 1)
                pool.affine_select(out=mask32[:, :], in_=mask32[:, :], compare_op=ALU.is_ge, fill=0.0,
                                   base=0, pattern=[[1, P]], channel_multiplier=-1).then_inc(made, 1)
                pool.wait_ge(made, 6)
                m4 = mask32[:, :].rearrange("p (c s) -> p c s", s=HG_CHUNK)
                pool.affine_select(out=m4, in_=m4, compare_op=ALU.is_ge, fill=0.0, base=0,
                                   pattern=[[-HG_CHUNK, P // HG_CHUNK], [0, HG_CHUNK]],
                                   channel_multiplier=1).then_inc(made, 1)
                pool.iota(positions_i[:, 4:8], [[P, TB]], base=0, channel_multiplier=1)\
                    .then_inc(made, 1)
                for i in range(HALF):
                    pool.memset(inv_freq[:, i:i + 1], 10000.0 ** (-2.0 * i / HEAD)).then_inc(freq_set, 1)
                core.w.split_upto(pool, core.ahead(10))

            @block.scalar
            def _(act):
                x_rows = t["x"].rearrange("l (t p) d -> p (l t) d", p=P)
                for tb in range(TB):
                    act.dma_start(x[:, tb, :], x_rows[:, tb, :]).then_inc(x_in[tb], 16)
                act.wait_ge(made, 2)
                act.activation(small[:, 20:21], ident[:, 0:1], ACT.Sqrt)

                def root(tb):
                    act.wait_ge(x_mean, tb + 1)
                    act.activation(small[:, 8 + tb:9 + tb], small[:, 4 + tb:5 + tb], ACT.Sqrt)\
                       .then_inc(x_rooted, 1)

                for tb in range(TB):
                    act.wait_ge(x_in[tb], 16)
                    act.activation(x_normed[:, tb, :], x[:, tb, :], ACT.Square,
                                   accum_out=small[:, tb:tb + 1]).then_inc(x_squared, 1)
                    if tb:
                        root(tb - 1)
                    if tb == 1:
                        core.w.round_upto(act, 0)
                root(TB - 1)
                act.wait_ge(g_copied, 1)
                columns.scalar(act)
                for j, target in enumerate(targets):
                    core.w.round_upto(act, core.tile0 + 2 * j + 2 + (j > 0))
                    if j == 0:
                        act.wait_ge(ready_ang, 1)
                        act.activation(trig[:, :, :], angle, ACT.Sin).then_inc(sined, 1)
                    for tb in range(TB):
                        core.wait_group(act, TB * j + tb)
                        act.activation(target[:, tb, :], core.bank[(TB * j + tb) % BANKS]
                                       [:, 0:IN_TILES[j][1]], ACT.Copy).then_inc(core.freed, 1)
                    if j in normed_heads:
                        src, heads = normed_heads[j]
                        act.wait_ge(core.freed, core.groups_at_start + TB * (j + 1))
                        if j:
                            act.wait_ge(meaned, 2 * j)
                        act.activation(squares[:, :, 0:heads * HEAD], src, ACT.Square)\
                           .then_inc(squared, 1)
                    for i in {1: (0,), 2: (1,), 3: (2, 3)}.get(j, ()):
                        n, at = TB * normed_heads[i][1], i % 2 * 32
                        act.wait_ge(meaned, 2 * i + 2)
                        act.activation(small[:, 64 + at:64 + at + n], small[:, at:at + n], ACT.Sqrt)\
                           .then_inc(rooted, 1)
                core.w.round_upto(act, core.ahead(10))
                for i, (_, dst, _) in enumerate(turns):
                    act.wait_ge(turned, i + 1)
                    bank = core.bank[(TB * len(IN_TILES) + i) % BANKS]
                    source = bank[:, :] if i else bank[:, 8:154]
                    act.activation(dst, source, ACT.Copy).then_inc(copied, 1)
                act.wait_ge(lam_exp, 1)
                act.activation(neg_lambda[:, 0:2], neg_lambda[:, 0:2], ACT.Exp).then_inc(exped, 1)
                act.activation(lb_logits, lb_logits, ACT.Exp).then_inc(exped, 1)

            @block.vector
            def _(dve):
                turn = Turn(dve, step)
                rotated_halves = Turn(dve, rotated)
                dve.memset(view(20992, 3 * P), 0.0).then_inc(cleared, 1)
                dve.wait_ge(g_turned, 1)
                dve.tensor_copy(vectors[:, 0:8], core.bank[BANKS - 1][:, 0:8]).then_inc(g_copied, 1)
                for tb in range(TB):
                    mean, rms, rstd = (small[:, 4 * i + tb:4 * i + tb + 1] for i in (1, 2, 3))
                    dve.wait_ge(x_squared, tb + 1)
                    dve.tensor_scalar(mean, small[:, tb:tb + 1], 1.0 / D, EPS, ALU.mult, ALU.add)\
                       .then_inc(x_mean, 1)
                    dve.wait_ge(x_rooted, tb + 1)
                    dve.reciprocal(rstd, rms).then_inc(x_inverse, 1)
                    dve.wait_ge(x_inverse, tb + 1)
                    dve.tensor_scalar(x_normed[:, tb, :], x[:, tb, :], rstd, None, ALU.mult)\
                       .then_inc(x_scaled, 1)
                columns.vector(dve)
                dve.wait_ge(loaded, 16 * N_LOADS)
                dve.wait_ge(made, 8)
                dve.wait_ge(freq_set, HALF)
                turn(dve.tensor_copy(position, positions_i))
                turn.wait()
                ang = angle[:, 0, :].rearrange("p (t f) -> p t f", f=HALF)
                turn(dve.tensor_tensor(ang, position.unsqueeze(2).to_broadcast([P, 2 * TB, HALF]),
                                       inv_freq.unsqueeze(1).to_broadcast([P, 2 * TB, HALF]), ALU.mult))
                turn.wait()
                magic = 1.5 * 2.0 ** 23
                turn(dve.tensor_scalar(angle_turns[:, 0, :], angle[:, 0, :], 0.5 / math.pi, None, ALU.mult))
                turn(dve.tensor_scalar(angle_turns[:, 1, :], angle[:, 0, :], 0.5 / math.pi, 0.25,
                                       ALU.mult, ALU.add))
                turn(dve.tensor_copy(angle[:, 1, :], angle[:, 0, :]))
                turn.wait()
                turn(dve.tensor_scalar(angle_turns, angle_turns, magic, None, ALU.add))
                turn.wait()
                turn(dve.tensor_scalar(angle_turns, angle_turns, -magic, None, ALU.add))
                turn.wait()
                part1 = 6.28125
                part2 = 0.0019350051879882812
                part3 = 2.0 * math.pi - part1 - part2
                for part in (part1, part2, part3):
                    turn(dve.scalar_tensor_tensor(angle, angle_turns, -part, angle, ALU.mult, ALU.add))
                    turn.wait()
                turn(dve.tensor_scalar(angle[:, 1, :], angle[:, 1, :], math.pi / 2, None, ALU.add))
                turn.wait()
                dve.tensor_scalar(angle, angle, 3.1415925, -3.1415925, ALU.min, ALU.max)\
                   .then_inc(ready_ang, 1)
                for i in range(2):
                    turn(dve.tensor_tensor(lams[:, 2 * i, :], lams[:, 2 * i, :], lams[:, 2 * i + 1, :],
                                           ALU.mult))
                    turn.wait()
                    turn(dve.tensor_reduce(neg_lambda[:, i:i + 1], lams[:, 2 * i, :], AX.X, ALU.add))
                dve.wait_ge(sined, 1)
                sin1 = trig[:, 0, 0:TB * HALF].rearrange("p (t f) -> p t f", f=HALF)
                cos1 = trig[:, 1, 0:TB * HALF].rearrange("p (t f) -> p t f", f=HALF)
                for i in range(4):
                    for k, (tab, half) in enumerate(((cos1, 0), (cos1, 1), (sin1, 0), (sin1, 1))):
                        g = gains[:, i, half * HALF:(half + 1) * HALF].unsqueeze(1)\
                            .to_broadcast([P, TB, HALF])
                        turn(dve.tensor_tensor(tables[:, i, k, :].rearrange("p (t f) -> p t f", f=HALF),
                                               tab, g, ALU.mult))


                def finish(j):
                    src, heads = normed_heads[j]
                    n, at = TB * heads, j % 2 * 32
                    dve.wait_ge(rooted, j + 1)
                    turn(dve.reciprocal(small[:, 128:128 + n], small[:, 64 + at:64 + at + n]))
                    turn.wait()
                    r = small[:, 128:128 + n].rearrange("p (t h) -> p t h", t=TB)
                    v = src.rearrange("p t (h d) -> p t h d", h=heads)
                    turn(dve.tensor_tensor(v, v, r.unsqueeze(3).to_broadcast([P, TB, heads, HEAD]),
                                           ALU.mult))
                    rope(dve, turn, src, heads, table_views(j), t1, t2, done=rotated_halves)
                    if j == 1:
                        rope(dve, turn, mixed[:, :, 2 * HEAD:7 * HEAD], 5, plain_tables(0), t1, t2,
                             done=rotated_halves)
                        for src, dst in ((0, 0), (6, 1)):
                            for half in range(2):
                                dve.tensor_copy(keys_twice[dst][:, :, half * HEAD:(half + 1) * HEAD],
                                                mixed[:, :, src * HEAD:(src + 1) * HEAD])\
                                   .then_inc(twice, 1)

                for j in range(4):
                    src, heads = normed_heads[j]
                    mean = small[:, j % 2 * 32:j % 2 * 32 + TB * heads]
                    dve.wait_ge(squared, j + 1)
                    dve.tensor_reduce(mean, squares[:, :, 0:heads * HEAD]
                                      .rearrange("p t (h d) -> p t h d", h=heads), AX.X, ALU.add)\
                       .then_inc(meaned, 1)
                    dve.wait_ge(meaned, 2 * j + 1)
                    dve.tensor_scalar(mean, mean, 1.0 / HEAD, EPS, ALU.mult, ALU.add)\
                       .then_inc(meaned, 1)
                    if j == 0:
                        continue
                    finish(j - 1)
                finish(3)
                dve.wait_ge(copied, 1)
                turn(dve.tensor_tensor(xqk_gain, vectors[:, 149:151], vectors[:, 151:153], ALU.mult))
                l0, l1 = lb_logits[:, 0:8], lb_logits[:, 8:16]
                top, total = logit_numbers[:, 0:8], logit_numbers[:, 8:16]
                turn(dve.tensor_tensor(top, l0, l1, ALU.max))
                turn.wait()
                turn(dve.tensor_tensor(l0, l0, top, ALU.subtract))
                dve.tensor_tensor(l1, l1, top, ALU.subtract).then_inc(lam_exp, 1)
                dve.wait_ge(exped, 2)
                turn(dve.tensor_tensor(neg_lambda[:, 2:3], neg_lambda[:, 1:2], neg_lambda[:, 0:1],
                                       ALU.subtract))
                turn(dve.tensor_tensor(total, l0, l1, ALU.add))
                turn.wait()
                turn(dve.tensor_scalar(neg_lambda[:, 2:3], neg_lambda[:, 2:3], -LAMBDA_INIT, None, ALU.add))
                turn(dve.reciprocal(total, total))
                turn.wait()
                turn(dve.tensor_tensor(lower[:, 0:8], l0, total, ALU.mult))
                turn(dve.tensor_tensor(lower[:, 8:16], l1, total, ALU.mult))

        relu, select = view(12288, 4, BANK), view(14336, 4, BANK)
        with ExitStack() as c:
            scored, rectified, step, summed = (core.sem(s) for s in ("scored", "rectified", "step", "summed"))
            block = core.stage(c)
            columns = Columns(core, mem, g_mem, rows=MB, norm=(mem_scratch, small), first_bank=4)

            @block.tensor
            def _(pe):
                for b in range(1, TB):
                    keys = (b + 1) * P
                    for h in range(IDX_HEADS):
                        half = slice((h % 2) * HEAD, (h % 2 + 1) * HEAD)
                        if b > 1:
                            pe.wait_ge(rectified, (b - 2) * 4 + h + 1)
                        pe.matmul(core.bank[h][:, 0:keys],
                                  qiT[half, h // 2, b * P:(b + 1) * P], kiT[half, 0:keys],
                                  start=True, stop=True).then_inc(scored, 1)
                    if b == 2:
                        columns.tensor(pe)

            @block.scalar
            def _(act):
                columns.scalar_norm(act)
                for b in range(1, TB):
                    keys = (b + 1) * P
                    if b > 1:
                        act.wait_ge(summed, b - 1)
                    for h in range(IDX_HEADS):
                        act.wait_ge(scored, (b - 1) * 4 + h + 1)
                        act.activation(relu[:, h, 0:keys], core.bank[h][:, 0:keys],
                                       ACT.Relu).then_inc(rectified, 1)
                    if b == 2:
                        columns.scalar_round(act)

            @block.vector
            def _(dve):
                turn = Turn(dve, step)
                w_idx = mixed[:, :, 7 * HEAD:7 * HEAD + IDX_HEADS]
                turn(dve.tensor_scalar(w_idx, w_idx, IDX_HEADS ** -0.5 * HEAD ** -0.5, None, ALU.mult))
                turn.wait()
                columns.vector_norm(dve)
                for b in range(1, TB):
                    keys = (b + 1) * P
                    s = select[:, b, 0:keys]
                    dve.wait_ge(rectified, 4 * b)
                    turn(dve.tensor_scalar(s, relu[:, 0, 0:keys], w_idx[:, b, 0:1], None, ALU.mult))
                    for h in range(1, IDX_HEADS):
                        turn.wait()
                        ins = dve.scalar_tensor_tensor(s, relu[:, h, 0:keys], w_idx[:, b, h:h + 1], s,
                                                       ALU.mult, ALU.add)
                        if h < IDX_HEADS - 1:
                            turn(ins)
                    ins.then_inc(summed, 1)
                    dve.wait_ge(summed, b)
                    turn(dve.tensor_tensor(s, s, causal[:, BANK - keys:BANK], ALU.add))
                    if b == 2:
                        columns.vector_split(dve)

        chosen = core.sem("chosen")
        top8 = small[:, 96:104]
        choice = Turn(None, chosen)

        def choose_steps(dve, parts):
            choice.eng = dve
            for b, first, last, rounds in parts:
                s = select[:, b, 0:(b + 1) * P]
                for i in range(last - first):
                    choice.wait()
                    choice(dve.max(top8, s))
                    choice.wait()
                    choice(dve.match_replace(s, top8, s, TAKEN))
                    if (i + 1) * rounds // (last - first) > i * rounds // (last - first):
                        yield
                if last == TOPK // 8:
                    choice.wait()
                    choice(dve.tensor_scalar(s, s, TAKEN, None, ALU.is_equal))
                    choice.wait()
                    choice(dve.tensor_scalar(s, s, -1.0, -NEG, ALU.add, ALU.mult))
            yield

        here, later = ((1, 0, 16, 8), (2, 0, 16, 12), (3, 0, 9, 13)), ((3, 9, 16, 9),)

        mix = view(4096, TB, D)
        buffers = (view(0, 3, BANK), view(10240, 2, BANK), small)
        kN, vN = view(12288, MB, D), view(8192, MB, D)

        def memory_product(target, vector, scalar=None):
            def scalar_steps(act):
                copies = paced(core.copy_steps(act, 0, DC, ((target, HALVES),), rows=MB), 4)
                return together(copies, scalar(act)) if scalar is not None else copies
            return dict(tiles=4, vector=vector, scalar=scalar_steps,
                        tensor=lambda pe: core.product_steps(pe, 0, DC, HALVES, rows=MB))

        def weighted(target):
            def finish(dve, turn, j, sums, values):
                turn(dve.reciprocal(sums, sums))
                turn.wait()
                return dve.tensor_scalar(target, values, sums, None, ALU.mult)
            return finish

        def less_weighted(target, first):
            def finish(dve, turn, j, sums, values):
                turn(dve.reciprocal(sums, sums))
                turn.wait()
                turn(dve.tensor_scalar(sums, sums, neg_lambda[:, 2:3], None, ALU.mult))
                turn.wait()
                return dve.scalar_tensor_tensor(target, values, sums, first, ALU.mult, ALU.add)
            return finish

        units = []
        for b in range(TB):
            keys = (b + 1) * P
            for h in range(B_HEADS):
                first = view(11264, 2, P)[:, h % 2, :]
                target = mix[:, b, 512 + h * P:512 + (h + 1) * P]
                for k in range(2):
                    half = slice(k * HEAD, (k + 1) * HEAD)
                    units.append(([(qbT[half, h, b * P:(b + 1) * P], kbT[half, h, 0:keys])], keys,
                                  causal[:, BANK - keys:BANK],
                                  lambda c_, h=h: vb[:, c_, h * P:(h + 1) * P], P,
                                  less_weighted(target, first) if k else weighted(first)))
        attention(core, units, HEAD ** -0.5, buffers, beside=memory_product(kN, lambda dve: choose_steps(dve, here)))

        out_b = mix[:, :, 512:1024]
        squares_b = view(23040, 2, 512)
        mean_b, rms_b, rstd_b = small[:, 64:80], small[:, 80:96], small[:, 104:120]
        squared_b, mean_step, rooted_b, normed_b = (core.sem(s) for s in (
            "squared_b", "mean_b", "rooted_b", "normed_b"))

        def square_steps(act):
            for tb in range(TB):
                if tb >= 2:
                    act.wait_ge(mean_step, tb - 1)
                act.activation(squares_b[:, tb % 2, :], out_b[:, tb, :], ACT.Square)\
                   .then_inc(squared_b, 1)
                yield
            yield
            act.wait_ge(mean_step, TB + 1)
            act.activation(rms_b, mean_b, ACT.Sqrt).then_inc(rooted_b, 1)
            yield

        def norm_steps(dve):
            for tb in range(TB):
                dve.wait_ge(squared_b, tb + 1)
                dve.tensor_reduce(mean_b[:, tb * B_HEADS:(tb + 1) * B_HEADS],
                                  squares_b[:, tb % 2, :].rearrange("p (h d) -> p h d", h=B_HEADS),
                                  AX.X, ALU.add).then_inc(mean_step, 1)
                yield
            dve.wait_ge(mean_step, TB)
            dve.tensor_scalar(mean_b, mean_b, 1.0 / P, EPS, ALU.mult, ALU.add).then_inc(mean_step, 1)
            yield
            yield
            dve.wait_ge(rooted_b, 1)
            dve.reciprocal(rstd_b, rms_b).then_inc(normed_b, 1)
            dve.wait_ge(normed_b, 1)
            dve.tensor_scalar(rstd_b, rstd_b, 1.0 - LAMBDA_INIT, None, ALU.mult).then_inc(normed_b, 1)
            dve.wait_ge(normed_b, 2)
            for tb in range(TB):
                xt = out_b[:, tb, :].rearrange("p (h d) -> p h d", h=B_HEADS)
                r = rstd_b[:, tb * B_HEADS:(tb + 1) * B_HEADS].unsqueeze(2)\
                    .to_broadcast([P, B_HEADS, P])
                dve.tensor_tensor(xt, xt, r, ALU.mult).then_inc(normed_b, 1)
                yield

        mean_k, rms_k, rstd_k = small[:, 120:128], small[:, 128:136], small[:, 136:144]
        squares_k = view(11264, 4, X_HEAD)
        squared_k, mean_step_k, rooted_k, normed_k = (core.sem(s) for s in (
            "squared_k", "mean_k", "rooted_k", "normed_k"))

        def key_square_steps(act):
            for i in range(MB * X_HEADS):
                tb, h = divmod(i, X_HEADS)
                if i >= 4:
                    act.wait_ge(squared_k, i - 3)
                act.activation(squares_k[:, i % 4, :], kN[:, tb, h * X_HEAD:(h + 1) * X_HEAD],
                               ACT.Square, accum_out=mean_k[:, i:i + 1]).then_inc(squared_k, 1)
                if i % 2:
                    yield
            yield
            act.wait_ge(mean_step_k, 1)
            act.activation(rms_k, mean_k, ACT.Sqrt).then_inc(rooted_k, 1)
            yield

        def key_norm_steps(dve):
            for _ in range(MB * X_HEADS // 2):
                yield
            dve.wait_ge(squared_k, MB * X_HEADS)
            dve.tensor_scalar(mean_k, mean_k, 1.0 / X_HEAD, EPS, ALU.mult, ALU.add)\
               .then_inc(mean_step_k, 1)
            yield
            dve.wait_ge(rooted_k, 1)
            dve.reciprocal(rstd_k, rms_k).then_inc(normed_k, 1)
            dve.wait_ge(normed_k, 1)
            for tb in range(MB):
                xt = kN[:, tb, :].rearrange("p (h d) -> p h d", h=X_HEADS)
                r = rstd_k[:, tb * X_HEADS:(tb + 1) * X_HEADS].unsqueeze(2)\
                    .to_broadcast([P, X_HEADS, X_HEAD])
                dve.tensor_tensor(xt, xt, r, ALU.mult).then_inc(normed_k, 1)
                yield

        x = view(18432, TB, D)
        units = []
        for b in range(TB):
            keys = (b + 1) * P
            for h in range(A_HEADS):
                half = slice((h % 2) * HEAD, (h % 2 + 1) * HEAD)
                bias = select[:, b, 0:keys] if b else causal[:, 3 * P:4 * P]
                units.append(([(qaT[half, h // 2, b * P:(b + 1) * P], kaT[half, 0:keys])], keys, bias,
                              lambda k: mixed[:, k, HEAD:2 * HEAD], HEAD,
                              weighted(mix[:, b, h * HEAD:(h + 1) * HEAD])))
        last_block = (TB - 1) * A_HEADS
        attention(core, units, HEAD ** -0.5, buffers,
                  bias_ready=lambda dve, i: choice.wait() if i == last_block else None,
                  transfers=[(x, t["x"].rearrange("l (t p) d -> p (l t) d", p=P))],
                  beside=memory_product(vN, lambda dve: together(choose_steps(dve, later), norm_steps(dve),
                                                             key_norm_steps(dve)),
                                        lambda act: together(square_steps(act), key_square_steps(act))))
        normed = view(0, TB, D)
        add_product(core, ((mix,), {}), x, norm=(normed, small))

        kT = view(10240, DC, N_MEM)

        qN, qT = view(14336, TB, D), view(0, DC, SEQ)
        q_mean, q_rms, q_scale = small[:, 64:80], small[:, 80:96], small[:, 104:120]
        squares = view(4096, 2 * TB, BANK)
        with ExitStack() as c:
            squared, meaned, rooted, scaled = (core.sem(s) for s in ("squared", "mean", "rooted", "scaled"))
            block = core.stage(c)
            columns = Columns(core, normed, g_xattn)
            turns = Turns(core, [(lambda tb, q=q: kN[:, tb, q * P:(q + 1) * P], MB, kT[:, q, :])
                                 for q in range(DC)] +
                          [(lambda tb, q=q: qN[:, tb, q * P:(q + 1) * P], TB, qT[:, q, :])
                           for q in range(DC)],
                          gains=[xqk_gain[:, q % 2:q % 2 + 1] for q in range(DC)] + [1.0] * DC,
                          groups=2 * TB)

            @block.tensor
            def _(pe):
                columns.tensor(pe)
                core.products_by_rows(pe, 0, DC, HALVES, columns=columns)
                turns.tensor(pe, lambda pe, m: pe.wait_ge(core.freed, core.groups_at_start + 2 * TB)
                             if m == DC else None)

            core.stream(block, 4)

            @block.scalar
            def _(act):
                columns.scalar(act)
                for g in range(2 * TB):
                    half, tb = divmod(g, TB)
                    if tb == 0:
                        core.w.round_upto(act, core.tile0 + 2 * half + 3)
                    core.wait_group(act, g)
                    for i in range(2):
                        at = tb * X_HEADS + 2 * half + i
                        act.activation(squares[:, g, i * X_HEAD:(i + 1) * X_HEAD],
                                       core.bank_of(g)[:, i * X_HEAD:(i + 1) * X_HEAD], ACT.Square,
                                       accum_out=q_mean[:, at:at + 1]).then_inc(squared, 1)
                act.wait_ge(meaned, 1)
                act.activation(q_rms, q_mean, ACT.Sqrt).then_inc(rooted, 1)
                turns.scalar(act)
                core.w.round_upto(act, core.ahead(4))

            @block.vector
            def _(dve):
                columns.vector(dve)
                for g in range(2 * TB):
                    half, tb = divmod(g, TB)
                    dve.wait_ge(squared, 2 * g + 2)
                    dve.tensor_copy(qN[:, tb, half * 512:(half + 1) * 512], core.bank_of(g)[:, :])\
                       .then_inc(core.freed, 1)
                dve.tensor_scalar(q_mean, q_mean, 1.0 / X_HEAD, EPS, ALU.mult, ALU.add)\
                   .then_inc(meaned, 1)
                dve.wait_ge(rooted, 1)
                dve.reciprocal(q_scale, q_rms).then_inc(scaled, 1)
                dve.wait_ge(scaled, 1)
                dve.tensor_scalar(q_scale, q_scale, X_HEAD ** -0.5, None, ALU.mult).then_inc(scaled, 1)
                turns.vector(dve)

        o = view(14336, TB, D)
        units = []
        for b in range(TB):
            for h in range(X_HEADS):
                units.append(([(qT[:, 2 * h + k, b * P:(b + 1) * P], kT[:, 2 * h + k, :])
                               for k in range(2)], N_MEM, causal[:, 0:N_MEM],
                              lambda k, h=h: vN[:, k, h * X_HEAD:(h + 1) * X_HEAD], X_HEAD,
                              weighted(o[:, b, h * X_HEAD:(h + 1) * X_HEAD])))
        attention(core, units, lambda i: q_scale[:, i:i + 1],
                  (view(4096, 3, BANK), view(5632, 2, BANK), small))
        add_product(core, ((o,), {}), x, norm=(normed, small))
        core.recycle()

        hidden = view(0, FC, SEQ)
        conv, gelu = view(11264, 2, SEQ), view(12288, 2, SEQ)
        with ExitStack() as c:
            started, convolved, activated, step = (core.sem(s) for s in ("started", "convolved",
                                                                         "activated", "step"))
            block = core.stage(c)
            columns = Columns(core, normed, g_ffn)
            PAIRS = FC // 2

            @block.tensor
            def _(pe):
                columns.tensor(pe)
                for i in range(2 * PAIRS):
                    core.products_by_columns(pe, 2 * i, DC, 2 * P, columns=None if i else columns)

            core.stream(block, 2 * PAIRS)

            @block.scalar
            def _(act):
                columns.scalar(act)
                for i in range(PAIRS):
                    core.w.round_upto(act, core.tile0 + 2 * i + 2)
                    for k in range(2):
                        ch = 2 * i + k
                        core.wait_group(act, 4 * i + k)
                        if i:
                            act.wait_ge(activated, 2 * i - 1 + k)
                        act.activation(conv[:, k, :], core.bank[(4 * i + k) % BANKS][:, :], ACT.Identity,
                                       scale=conv_w[:, 2 * FC + ch:2 * FC + ch + 1],
                                       bias=conv_b[:, ch:ch + 1]).then_inc(started, 1)
                    core.w.round_upto(act, core.tile0 + 2 * i + 3)
                    for k in range(2):
                        act.wait_ge(core.freed, core.groups_at_start + 4 * i + k + 1)
                        if i:
                            act.wait_ge(core.freed, core.groups_at_start + 4 * (i - 1) + 3 + k)
                        act.activation(gelu[:, k, :], conv[:, k, :], ACT.Gelu_apprx_tanh)\
                           .then_inc(activated, 1)
                core.w.round_upto(act, core.ahead(2 * PAIRS))

            @block.vector
            def _(dve):
                columns.vector(dve)
                for i in range(PAIRS):
                    for k in range(2):
                        ch = 2 * i + k
                        a = core.bank[(4 * i + k) % BANKS]
                        dve.wait_ge(started, ch + 1)
                        w = lambda j: conv_w[:, j * FC + ch:j * FC + ch + 1]
                        dve.scalar_tensor_tensor(conv[:, k, 1:SEQ], a[:, 0:SEQ - 1], w(1),
                                                 conv[:, k, 1:SEQ], ALU.mult, ALU.add)\
                           .then_inc(step, 1)
                        dve.wait_ge(step, ch + 1)
                        dve.scalar_tensor_tensor(conv[:, k, 2:SEQ], a[:, 0:SEQ - 2], w(0),
                                                 conv[:, k, 2:SEQ], ALU.mult, ALU.add)\
                           .then_inc(core.freed, 1)
                    for k in range(2):
                        g = 4 * i + 2 + k
                        core.wait_group(dve, g)
                        dve.wait_ge(activated, 2 * i + k + 1)
                        dve.tensor_tensor(hidden[:, 2 * i + k, :], core.bank[g % BANKS][:, :],
                                          gelu[:, k, :], ALU.mult).then_inc(core.freed, 1)

        with ExitStack() as c:
            rounded, remainder = core.sem("rounded"), core.sem("remainder")
            block = core.stage(c)
            K_GROUPS = [(k0, min(4, FC - k0)) for k0 in range(0, FC, 4)]
            released = []
            normed = view(12288, TB, D)
            rows_norm = RowNorm(core, x, normed, small)

            @block.tensor
            def _(pe):
                for i, (k0, kn) in enumerate(K_GROUPS):
                    for half in range(2):
                        hi, lo = core.w.take(pe, kn, 512)
                        for tb in range(TB):
                            for k in range(kn):
                                if half == 0 and tb == 0:
                                    pe.wait_ge(remainder, k0 + k + 1)
                                xs = (slice(None), i % 2 * 4 + k, slice(tb * P, (tb + 1) * P))
                                for a, b in ((core.xh, hi), (core.xh, lo), (core.xl, hi)):
                                    last = k == kn - 1 and a is core.xl
                                    first = k == 0 and a is core.xh and b is hi
                                    ins = pe.matmul(core.bank[half * TB + tb][:, :], a[xs], b[:, k, :],
                                                    start=(i == 0 and first),
                                                    stop=(k0 + kn == FC and last))
                            if k0 + kn == FC:
                                ins.then_inc(core.ready, 1)
                                core.groups += 1
                        if k0 + kn == FC:
                            core.w.release(ins, core.ready, core.groups)
                        else:
                            core.w.release(ins)
                    released.append(core.w.used_at[-1])

            core.stream(block, 2 * len(K_GROUPS))

            @block.scalar
            def _(act):
                for i, (k0, kn) in enumerate(K_GROUPS):
                    if i >= 2:
                        act.wait_ge(*released[i - 2])
                    for k in range(kn):
                        act.activation(core.xh[:, i % 2 * 4 + k, :], hidden[:, k0 + k, :],
                                       ACT.Copy).then_inc(rounded, 1)
                    core.w.round_upto(act, core.tile0 + 2 * i + 2)
                core.w.round_upto(act, core.tile0 + 2 * len(K_GROUPS) - 1)
                rows_norm.scalar(act, 0)
                core.w.round_upto(act, core.ahead(2 * len(K_GROUPS)))
                rows_norm.scalar(act, 1)

            @block.vector
            def _(dve):
                for i, (k0, kn) in enumerate(K_GROUPS):
                    for k in range(kn):
                        dve.wait_ge(rounded, k0 + k + 1)
                        part = (slice(None), i % 2 * 4 + k)
                        dve.tensor_tensor(core.xl[part], hidden[:, k0 + k, :],
                                          core.xh[part].bitcast(F32), ALU.subtract)\
                           .then_inc(remainder, 1)
                add_groups(core, dve, x, rows_norm)

        saved_rows = lambda a: a.rearrange("(t p) d -> p t d", p=P)
        Q, K, KI, KON, V = (view(4096 * i, n, 4096 // n) for i, n in enumerate((8, 8, 8, TB, TB)))
        scratch = view(20480, 6, SEQ)
        state = arena[:, 23552:23552 + HG_HEADS * P].rearrange("p (h v) -> p h v", h=HG_HEADS)
        with ExitStack() as c:
            sigmoid = core.sem("sigmoid")
            block = core.stage(c)
            columns = Columns(core, normed, g_second)
            sigmoids = view(16384, 2, SEQ)

            @block.tensor
            def _(pe):
                columns.tensor(pe)
                for i in range(8):
                    core.products_by_columns(pe, 2 * i, DC, 2 * P, columns=None if i else columns)

            core.stream(block, 8, moves=[(saved_rows(x_saved), x)])

            @block.scalar
            def _(act):
                columns.scalar(act)
                for g in range(16):
                    if g % 2 == 0:
                        core.w.round_upto(act, core.tile0 + g // 2 + 2)
                    core.wait_group(act, g)
                    if g >= 2:
                        act.wait_ge(core.freed, core.groups_at_start + g - 1)
                    dst = sigmoids[:, g % 2, :] if g < 8 else K[:, g - 8, :]
                    act.activation(dst, core.bank[g % BANKS][:, :], ACT.Sigmoid).then_inc(sigmoid, 1)
                core.w.round_upto(act, core.ahead(8))

            @block.vector
            def _(dve):
                columns.vector(dve)
                for g in range(8):
                    dve.wait_ge(sigmoid, g + 1)
                    dve.tensor_tensor(Q[:, g, :], core.bank[g % BANKS][:, :], sigmoids[:, g % 2, :],
                                      ALU.mult).then_inc(core.freed, 1)
                for h in range(8):
                    dve.wait_ge(sigmoid, 8 + h + 1)
                    dve.tensor_scalar(K[:, h, :], K[:, h, :], lower[:, 8 + h:9 + h], lower[:, h:h + 1],
                                      ALU.mult, ALU.add).then_inc(core.freed, 1)
        keep = view(4096 * 3, SEQ)
        with ExitStack() as c:
            kept, logged, scanned, to_last, up, down, out_ = (core.sem(s) for s in (
                "kept", "logged", "scanned", "to_last", "exp_b", "exp_minus_b", "exp_to_last"))
            made_q, made_ki, made_k, turned, copied, one_less, decayed = (core.sem(s) for s in (
                "made_q", "made_ki", "made_k", "turned", "copied", "one_less", "decayed"))
            block = core.stage(c)
            b_ = KI

            @block.tensor
            def _(pe):
                core.products_by_rows(pe, 0, DC, HALVES)

            @block.sync
            def _(sp):
                core.w.load_upto(sp, core.ahead(4) + core.w.RAW)

            @block.gpsimd
            def _(pool):
                pool.memset(keep, 1.0).then_inc(kept, 1)
                pool.wait_ge(kept, 1)
                k2 = keep.rearrange("p (n c) -> p n c", c=HG_CHUNK)
                pool.affine_select(out=k2, in_=k2, compare_op=ALU.not_equal, fill=0.0, base=0,
                                   pattern=[[0, SEQ // HG_CHUNK], [1, HG_CHUNK]], channel_multiplier=0)\
                    .then_inc(kept, 1)
                core.w.split_upto(pool, core.ahead(4))

            @block.scalar
            def _(act):
                for h in range(HG_HEADS):
                    act.activation(b_[:, h, :], K[:, h, :], ACT.Ln).then_inc(logged, 1)
                core.w.round_upto(act, core.tile0 + 2)
                for h in range(HG_HEADS):
                    if h == 2:
                        core.w.round_upto(act, core.tile0 + 3)
                    act.wait_ge(to_last, h + 1)
                    if h >= 2:
                        act.wait_ge(decayed, h - 1)
                    act.activation(scratch[:, h % 2, :], b_[:, h, :], ACT.Exp).then_inc(up, 1)
                    act.activation(scratch[:, 2 + h % 2, :], b_[:, h, :], ACT.Exp, scale=-1.0)\
                       .then_inc(down, 1)
                    d = scratch[:, 4 + h % 2, :]
                    act.activation(d, d, ACT.Exp).then_inc(out_, 1)
                for g in range(2 * TB):
                    half, tb = divmod(g, TB)
                    if tb == 0:
                        core.w.round_upto(act, core.tile0 + 4 + half)
                    core.copy_group(act, g, V[:, tb, half * 512:(half + 1) * 512], 512)

            @block.vector
            def _(dve):
                dve.wait_ge(kept, 2)
                for h in range(HG_HEADS):
                    dve.wait_ge(logged, h + 1)
                    dve.tensor_tensor_scan(b_[:, h, :], keep, b_[:, h, :], 0.0, ALU.mult, ALU.add)\
                       .then_inc(scanned, 1)
                    dve.tensor_scalar(K[:, h, :], K[:, h, :], -1.0, 1.0, ALU.mult, ALU.add)\
                       .then_inc(one_less, 1)

                def last_minus(h):
                    if h >= 2:
                        dve.wait_ge(made_k, h - 1)
                    dve.wait_ge(scanned, h + 1)
                    b3 = b_[:, h, :].rearrange("p (n c) -> p n c", c=HG_CHUNK)
                    d3 = scratch[:, 4 + h % 2, :].rearrange("p (n c) -> p n c", c=HG_CHUNK)
                    last = b3[:, :, HG_CHUNK - 1:HG_CHUNK].to_broadcast([P, SEQ // HG_CHUNK, HG_CHUNK])
                    dve.tensor_tensor(d3, last, b3, ALU.subtract).then_inc(to_last, 1)

                last_minus(0)
                for h in range(HG_HEADS):
                    if h + 1 < HG_HEADS:
                        last_minus(h + 1)
                    dve.wait_ge(one_less, h + 1)
                    dve.wait_ge(up, h + 1)
                    dve.tensor_tensor(Q[:, h, :], Q[:, h, :], scratch[:, h % 2, :], ALU.mult)\
                       .then_inc(made_q, 1)
                    e3 = scratch[:, h % 2, :].rearrange("p (n c) -> p n c", c=HG_CHUNK)
                    dve.tensor_copy(decay[:, h, :], e3[:, :, HG_CHUNK - 1]).then_inc(made_q, 1)
                    dve.wait_ge(down, h + 1)
                    dve.tensor_tensor(KI[:, h, :], K[:, h, :], scratch[:, 2 + h % 2, :], ALU.mult)\
                       .then_inc(decayed, 1)
                    dve.wait_ge(out_, h + 1)
                    dve.wait_ge(decayed, h + 1)
                    dve.tensor_tensor(K[:, h, :], K[:, h, :], scratch[:, 4 + h % 2, :], ALU.mult)\
                       .then_inc(made_k, 1)

        intra = view(20480, 2, HG_HEADS * P)
        turn_heads(core, [(lambda tb, h=h: K[:, h, tb * P:(tb + 1) * P], TB,
                           KON[:, :, h * P:(h + 1) * P]) for h in range(HG_HEADS)],
                   clear=(intra, state))
        C = P // HG_CHUNK
        o = view(4096, TB, D)
        with ExitStack() as c:
            scores_in, masked, intra_done, kv_done = (core.sem(s) for s in (
                "scores_in", "masked", "intra_done", "kv_done"))
            updated, out_ready, out_read = (core.sem(s) for s in ("updated", "out_ready", "out_read"))
            block = core.stage(c)

            @block.tensor
            def _(pe):
                for tb in range(TB):
                    tok = slice(tb * P, (tb + 1) * P)
                    if tb >= 1:
                        pe.wait_ge(masked, 2 * tb)
                    for h in range(HG_HEADS):
                        ins = pe.matmul(core.bank[h // 4][:, h % 4 * P:(h % 4 + 1) * P],
                                        KI[:, h, tok], Q[:, h, tok], start=True, stop=True)
                        if h % 4 == 3:
                            ins.then_inc(scores_in, 1)
                    ob = core.bank[2 + tb % 2 * 2:4 + tb % 2 * 2]
                    if tb >= 2:
                        pe.wait_ge(out_read, 2 * (tb - 1))
                    for h in range(HG_HEADS):
                        pe.wait_ge(masked, 2 * tb + h // 4 + 1)
                        pe.matmul(ob[h // 4][:, h % 4 * P:(h % 4 + 1) * P],
                                  intra[:, tb % 2, h * P:(h + 1) * P], V[:, tb, h * P:(h + 1) * P],
                                  start=(h % 4 == 0), stop=False, skip_group_check=True)\
                          .then_inc(intra_done, 1)
                    for n in range(C):
                        step = tb * C + n
                        rows = slice(n * HG_CHUNK, (n + 1) * HG_CHUNK)
                        for g in range(2):
                            heads = range(4 * g, 4 * g + 4)
                            if step:
                                pe.wait_ge(updated, HG_HEADS * (step - 1) + 4 * g + 4)
                            for h in heads:
                                ins = pe.matmul(ob[g][rows, h % 4 * P:(h % 4 + 1) * P],
                                                Q[:, h, tb * P + n * HG_CHUNK:tb * P + (n + 1) * HG_CHUNK],
                                                state[:, h, :], start=False, stop=(h % 4 == 3),
                                                skip_group_check=True)
                            if n == C - 1:
                                ins.then_inc(out_ready, 1)
                            if step < TB * C - 1:
                                for h in heads:
                                    ins = pe.matmul(core.bank[6 + g][:, h % 4 * P:(h % 4 + 1) * P],
                                                    KON[rows, tb, h * P:(h + 1) * P],
                                                    V[rows, tb, h * P:(h + 1) * P], start=True, stop=True)
                                ins.then_inc(kv_done, 1)

            @block.vector
            def _(dve):
                m = mask32[:, :].bitcast(I32).unsqueeze(1).to_broadcast([P, 4, P])

                def mask(tb):
                    if tb >= 2:
                        dve.wait_ge(intra_done, HG_HEADS * (tb - 1))
                    for g in range(2):
                        dve.wait_ge(scores_in, 2 * tb + g + 1)
                        dst = intra[:, tb % 2, g * BANK:(g + 1) * BANK].rearrange("p (h s) -> p h s", h=4)
                        dve.copy_predicated(dst, m, core.bank[g][:, :].rearrange("p (h s) -> p h s", h=4))\
                           .then_inc(masked, 1)

                for tb in range(TB):
                    mask(tb)
                    for n in range(C):
                        step = tb * C + n
                        if step == TB * C - 1:
                            break
                        for h in range(HG_HEADS):
                            dve.wait_ge(kv_done, 2 * step + h // 4 + 1)
                            if step:
                                dve.wait_ge(updated, HG_HEADS * (step - 1) + h + 1)
                            dve.scalar_tensor_tensor(
                                state[:, h, :], state[:, h, :], decay[:, h, step:step + 1],
                                core.bank[6 + h // 4][:, h % 4 * P:(h % 4 + 1) * P],
                                ALU.mult, ALU.add).then_inc(updated, 1)

            @block.scalar
            def _(act):
                for tb in range(TB):
                    for g in range(2):
                        act.wait_ge(out_ready, 2 * tb + g + 1)
                        act.activation(o[:, tb, g * BANK:(g + 1) * BANK], core.bank[2 + tb % 2 * 2 + g][:, :],
                                       ACT.Copy).then_inc(out_read, 1)

        def gated_product(target, gate_buf, norm=None, moves=()):
            with ExitStack() as c:
                gated, squared, meaned, rooted, normed = (core.sem(s) for s in (
                    "gated", "squared", "mean", "rooted", "normed"))
                block = core.stage(c)
                n = TB * HG_HEADS
                mean, rms, rstd = small[:, 0:n], small[:, 32:32 + n], small[:, 64:64 + n]

                @block.tensor
                def _(pe):
                    core.products_by_rows(pe, 0, DC, HALVES)

                core.stream(block, 4, moves)

                @block.scalar
                def _(act):
                    if norm is not None:
                        for tb in range(TB):
                            act.activation(norm[1][:, tb, :], norm[0][:, tb, :], ACT.Square)\
                               .then_inc(squared, 1)
                        core.w.round_upto(act, core.tile0 + 2)
                        act.wait_ge(meaned, TB + 1)
                        act.activation(rms, mean, ACT.Sqrt).then_inc(rooted, 1)
                    for g in range(2 * TB):
                        if g % TB == 0:
                            core.w.round_upto(act, core.tile0 + 2 * (g // TB) + 3)
                        core.wait_group(act, g)
                        if g >= 2:
                            act.wait_ge(core.freed, core.groups_at_start + g - 1)
                        act.activation(gate_buf[:, g % 2, :], core.bank_of(g)[:, :], ACT.Silu)\
                           .then_inc(gated, 1)
                    core.w.round_upto(act, core.ahead(4))

                @block.vector
                def _(dve):
                    if norm is not None:
                        for tb in range(TB):
                            dve.wait_ge(squared, tb + 1)
                            dve.tensor_reduce(mean[:, tb * HG_HEADS:(tb + 1) * HG_HEADS],
                                              norm[1][:, tb, :].rearrange("p (h d) -> p h d", d=P),
                                              AX.X, ALU.add).then_inc(meaned, 1)
                        dve.wait_ge(meaned, TB)
                        dve.tensor_scalar(mean, mean, 1.0 / P, EPS, ALU.mult, ALU.add)\
                           .then_inc(meaned, 1)
                        dve.wait_ge(rooted, 1)
                        dve.reciprocal(rstd, rms).then_inc(normed, 1)
                        dve.wait_ge(normed, 1)
                        for tb in range(TB):
                            xt = norm[0][:, tb, :].rearrange("p (h d) -> p h d", d=P)
                            r = rstd[:, tb * HG_HEADS:(tb + 1) * HG_HEADS].unsqueeze(2)\
                                .to_broadcast([P, HG_HEADS, P])
                            dve.tensor_tensor(xt, xt, r, ALU.mult).then_inc(normed, 1)
                        dve.wait_ge(normed, 1 + TB)
                    for g in range(2 * TB):
                        dve.wait_ge(gated, g + 1)
                        tt = target(g % TB, g // TB)
                        gate = gate_buf[:, g % 2, :].rearrange("p (h d) -> p h d", d=P)
                        dve.tensor_tensor(tt, tt, gate, ALU.mult).then_inc(core.freed, 1)

        def rows_of(a):
            return lambda tb, half: a[:, tb, half * 512:(half + 1) * 512]\
                .rearrange("p (h d) -> p h d", d=P)

        borrowed = [(part[:, 0:LORA_CHUNKS, :].bitcast(F32), columns_saved[i])
                    for i, part in enumerate((core.xh, core.xl))]
        gated_product(rows_of(o), view(8192, 2, 512), norm=(o, view(0, TB, D)),
                      moves=[(saved, part) for part, saved in borrowed])
        core.recycle()

        qnT, knT, vN = view(0, 8, SEQ), view(4096, 8, SEQ), view(8192, TB, D)
        qpT, kpT = view(12288, 4, SEQ), view(14336, SEQ)
        q_rows, kv_rows = view(17664, TB, Q_LORA), view(14848, TB, KV_LORA)
        kr, kr_twice = view(15872, TB, PE_DIM), view(21760, TB, P)
        qpN = view(17664, TB, 8 * PE_DIM)
        t1, t2 = view(19712, 1024), view(20736, 1024)
        with ExitStack() as c:
            rotated, kr_in, y_moved = (core.sem(s) for s in ("rotated", "kr_in", "y_moved"))
            block = core.stage(c)

            LAST_GROUPS = 2 * TB + 8 + TB + 8 + 2 * TB
            halves = core.sem("rotated_halves")
            turns = Turns(core, [(lambda tb: kr_twice[:, tb, :], TB, kpT)] +
                          [(lambda tb, q=q: qpN[:, tb, q * P:(q + 1) * P], TB, qpT[:, q, :])
                           for q in range(4)], groups=LAST_GROUPS)
            q_part = LowRank(core, small, 0, q_rows, q_a_gain, 0, 0, 0)
            kv_part = LowRank(core, small, TB, kv_rows, kv_a_gain, 3, 4, 12)

            @block.tensor
            def _(pe):
                g = core.products_by_rows(pe, 0, DC, ((0, Q_LORA), (Q_LORA, KV_LORA + PE_DIM)))
                q_part.columns.tensor(pe)
                g = core.products_by_columns(pe, g, 3, 4 * NOPE, columns=q_part.columns)
                kv_part.columns.tensor(pe)
                pe.wait_ge(kv_part.columns.remainder, 2)
                g = core.products_by_columns(pe, g, 3, 4 * NOPE)
                g = core.products_by_rows(pe, g, 3, ((0, 8 * PE_DIM),))
                g = core.products_by_columns(pe, g, 2, 8 * NOPE, x0=3)
                core.products_by_rows(pe, g, 2, HALVES, x0=3)
                turns.tensor(pe, lambda pe, m: pe.wait_ge(halves, 6) if m == 0 else None)

            @block.sync
            def _(sp):
                sp.dma_start(saved_rows(y_saved), o).then_inc(y_moved, 16)
                core.w.load_upto(sp, core.ahead(10) + core.w.RAW)
                sp.wait_ge(y_moved, 16)

            @block.gpsimd
            def _(pool):
                core.w.split_upto(pool, core.ahead(10))

            @block.scalar
            def _(act):
                core.w.round_upto(act, core.tile0 + 3)
                for tb in range(TB):
                    q_part.square(act, tb)
                q_part.root(act)
                core.w.round_upto(act, core.tile0 + 5)
                for tb in range(TB):
                    kv_part.square(act, tb)
                    act.activation(kr[:, tb, :], core.bank_of(TB + tb)[:, KV_LORA:KV_LORA + PE_DIM],
                                   ACT.Copy).then_inc(kr_in, 1)
                kv_part.root(act)
                q_part.columns.scalar_round(act)
                act.wait_ge(core.freed, core.groups_at_start + 2 * TB)
                places = [(qnT[:, h, :], 0 if h < 4 else 1) for h in range(8)]
                places += [(qpN[:, tb, :], 2) for tb in range(TB)]
                places += [(knT[:, h, :], 3) for h in range(8)]
                places += [(vN[:, tb, 512 * half:512 * (half + 1)], 4 + half)
                           for half in range(2) for tb in range(TB)]
                for i, (dst, tile) in enumerate(places):
                    if i == 4:
                        kv_part.columns.scalar_round(act)
                    if i == 12:
                        act.wait_ge(y_moved, 16)
                    core.w.round_upto(act, core.tile0 + 4 + tile + 2)
                    core.copy_group(act, 2 * TB + i, dst, 512)
                turns.scalar(act)
                core.w.round_upto(act, core.ahead(10))

            @block.vector
            def _(dve):
                turn = Turn(dve, rotated)
                q_part.scale(dve)
                dve.wait_ge(kr_in, TB)
                kv_part.scale(dve)
                q_part.columns.vector_split(dve)
                kv_part.columns.vector_split(dve)
                done = Turn(dve, halves)
                rope(dve, turn, kr, 1, plain_tables(1), t1, t2, done=done)
                for half in range(2):
                    done(dve.tensor_copy(kr_twice[:, :, half * HEAD:(half + 1) * HEAD], kr))
                dve.wait_ge(core.freed, core.groups_at_start + 2 * TB + 12)
                rope(dve, turn, qpN, 8, plain_tables(1), t1, t2, done=done)
                turns.vector(dve)

        y_b = qnT
        x = view(14848, TB, D)
        units = []
        for b in range(TB):
            keys = (b + 1) * P
            q_tok = slice(b * P, (b + 1) * P)
            for h in range(MLA_HEADS):
                half = slice((h % 2) * HEAD, (h % 2 + 1) * HEAD)
                units.append(([(qnT[:, h, q_tok], knT[:, h, 0:keys]),
                               (qpT[half, h // 2, q_tok], kpT[half, 0:keys])], keys,
                              causal[:, BANK - keys:BANK],
                              lambda k, h=h: vN[:, k, h * P:(h + 1) * P], V_DIM,
                              weighted(y_b[:, h, q_tok])))
        attention(core, units, (NOPE + PE_DIM) ** -0.5, (view(18944, 3, BANK), view(20480, 2, BANK), small),
                  transfers=[(x, saved_rows(x_saved))] + borrowed)

        gates = arena[:, 4096:12288].rearrange("p (n t d) -> p n t d", n=2, t=TB)
        gate_bias = view(12288, 2 * D)
        y_a = view(18944, TB, D)
        gated_product(lambda tb, half: y_b[:, 4 * half:4 * half + 4, tb * P:(tb + 1) * P],
                      view(4096, 2, 512))
        with ExitStack() as c:
            biased, gated = core.sem("biased"), core.sem("gated")
            block = core.stage(c)

            @block.tensor
            def _(pe):
                core.products_by_rows(pe, 0, DC, [(0, 512)] * 4)

            bias_in, y_in = core.sem("bias_in"), core.sem("y_in")

            @block.sync
            def _(sp):
                sp.dma_start(gate_bias, over_partitions(t["b_gate_2"])).then_inc(bias_in, 16)
                core.w.load_upto(sp, core.tile0 + 5)
                sp.dma_start(y_a, saved_rows(y_saved)).then_inc(y_in, 16)
                core.w.load_upto(sp, core.ahead(8) + core.w.RAW)
                sp.wait_ge(y_in, 16)

            @block.gpsimd
            def _(pool):
                core.w.split_upto(pool, core.ahead(8))

            @block.vector
            def _(dve):
                dve.wait_ge(bias_in, 16)
                for g in range(4 * TB):
                    c_, tb = divmod(g, TB)
                    core.wait_group(dve, g)
                    dve.tensor_tensor(gates[:, c_ // 2, tb, c_ % 2 * 512:(c_ % 2 + 1) * 512],
                                      core.bank[g % BANKS][:, :], gate_bias[:, c_ * 512:(c_ + 1) * 512],
                                      ALU.add).then_inc(core.freed, 1)

            @block.scalar
            def _(act):
                for g in range(4 * TB):
                    c_, tb = divmod(g, TB)
                    if tb == 0:
                        core.w.round_upto(act, core.tile0 + 2 * c_ + 3)
                    act.wait_ge(core.freed, core.groups_at_start + g + 1)
                    part = gates[:, c_ // 2, tb, c_ % 2 * 512:(c_ % 2 + 1) * 512]
                    act.activation(part, part, ACT.Sigmoid).then_inc(gated, 1)
                core.w.round_upto(act, core.ahead(8))

        def gate_product(branch, source, **kw):
            with ExitStack() as c:
                step = core.sem("step")
                block = core.stage(c)
                columns = Columns(core, source, **kw)

                @block.tensor
                def _(pe):
                    columns.tensor(pe)
                    core.products_by_rows(pe, 0, DC, HALVES, columns=columns)

                core.stream(block, 4)

                @block.scalar
                def _(act):
                    columns.scalar(act)
                    core.w.round_upto(act, core.ahead(4))

                @block.vector
                def _(dve):
                    columns.vector(dve)
                    for g in range(2 * TB):
                        core.wait_group(dve, g)
                        part = (slice(None), branch, g % TB, slice(g // TB * 512, (g // TB + 1) * 512))
                        dve.tensor_tensor(gates[part], core.bank[g][:, :], gates[part], ALU.mult)\
                           .then_inc(core.freed, 1)
                        if branch:
                            first = (part[0], 0) + part[2:]
                            dve.wait_ge(core.freed, core.groups_at_start + g + 1)
                            dve.tensor_tensor(gates[first], gates[first], gates[part], ALU.add)\
                               .then_inc(step, 1)

        gate_product(0, y_a, gain=hg_gain.to_broadcast([P, HG_HEADS]))
        gate_product(1, y_b, by_head=True)
        add_product(core, ((gates[:, 0],), {}), x, norm=(view(0, TB, D), small),
                    final=(view(12288, D), t["final_norm_g_2"].partition_broadcast(P),
                           out.rearrange("l (t p) d -> p (l t) d", p=P), out_stored))
        assert core.w.n_taken == len(core.w.tiles)


INPUTS = ("x mem positions g_mix w_in g_qa g_ka g_qb g_kb lam_q1 lam_k1 lam_q2 lam_k2 w_out g_xattn "
          "g_mem w_xq w_xk w_xv w_xo g_xq g_xk g_ffn w_ffn_in conv_w conv_b w_ffn_out norm_g_2 w_in_2 "
          "b_gate_2 lb_logits_2 hg_norm_g_2 q_a_g_2 w_uq_2 kv_a_g_2 w_ukv_2 w_proj_a_2 w_proj_b_2 "
          "w_out_2 final_norm_g_2").split()


def kernel(**inputs):
    import numpy as _np
    import concourse.bacc as _bacc
    from concourse.bass_utils import run_bass_kernel_spmd as _run

    nc = _bacc.Bacc("TRN2", target_bir_lowering=False, num_devices=1)
    arrays, aps = {}, {}
    for name in INPUTS:
        a = _np.ascontiguousarray(inputs[name])
        arrays[f"in_{name}"] = a
        ap = nc.dram_tensor(f"in_{name}", a.shape, mybir.dt.from_np(a.dtype), kind="ExternalInput").ap()
        is_matrix = name.startswith("w_")
        aps[name] = ap[0] if is_matrix else ap
    out = nc.dram_tensor("out", (1, SEQ, D), F32, kind="ExternalOutput").ap()
    x_saved = nc.dram_tensor("x_saved", (SEQ, D), F32, kind="Internal").ap()
    y_saved = nc.dram_tensor("y_saved", (SEQ, D), F32, kind="Internal").ap()
    columns_saved = [nc.dram_tensor(name, (P, LORA_CHUNKS, SEQ), F32, kind="Internal").ap()
                     for name in ("rounded_saved", "remainder_saved")]
    two_blocks(nc, aps, out, x_saved, y_saved, columns_saved)
    r = _run(nc, [arrays], core_ids=[0])
    return r.results[0]["out"]
```
